# Optimizing a Trainium2 kernel written in Bass

```python
import jax
import jax.numpy as jnp
from jax import lax
import numpy as np

D_MODEL = 1024
BATCH = 1
SEQ = 256
DEPTH = 1
DEC_BATCH = 1
DEC_SEQ = 64
PAST_LEN = 512

CHUNK = 64
N_META = 16
H_R = 8
HEAD_R = 64
D_R = H_R * HEAD_R
LORA_W = 64
LORA_A = 64
LORA_G = 128
RWKV_IN = 3 * D_R + LORA_W + LORA_A + LORA_G
RWKV_SPLITS = (D_R, 2 * D_R, 3 * D_R, 3 * D_R + LORA_W, 3 * D_R + LORA_W + LORA_A)
LNX_EPS = 64e-5
H_F = 8
HEAD_F = 64
D_F = H_F * HEAD_F
FOX_IN = 3 * D_F + H_F
Q_BLOCK = 128
D_IN = RWKV_IN + FOX_IN
D_MIX = D_R + D_F
N_KEYS = 128
N_EXPERTS = N_KEYS * N_KEYS
PEER_HEADS = 8
PEER_TOPK = 16
D_KEY = 256
D_KEY_HALF = D_KEY // 2
PEER_BLOCK = 256
ALPHA = (2.0 * DEPTH) ** 0.25
BETA = (8.0 * DEPTH) ** -0.25
LN_EPS = 1e-5

kernel_name = 'rwkv7_fox_peer_streaming_step'

def _normal(key, shape, scale):
    return jax.random.normal(key, shape, jnp.float32) * scale

def _layernorm(x, g, b):
    xf = x.astype(jnp.float32)
    xc = xf - jnp.mean(xf, axis=-1, keepdims=True)
    var = jnp.mean(xc * xc, axis=-1, keepdims=True)
    return (xc * lax.rsqrt(var + LN_EPS) * g.astype(jnp.float32) + b.astype(jnp.float32)).astype(x.dtype)

def _wkv7_scan(r, w, k, v, a, b, s0):
    def step(S, inp):
        r_t, w_t, k_t, v_t, a_t, b_t = inp
        sa = jnp.einsum('bhvk,bhk->bhv', S, a_t)
        S = S * w_t[:, :, None, :] + sa[..., None] * b_t[:, :, None, :] + v_t[..., None] * k_t[:, :, None, :]
        return S, jnp.einsum('bhvk,bhk->bhv', S, r_t)
    xs = tuple(jnp.swapaxes(t, 0, 1) for t in (r, w, k, v, a, b))
    s_final, ys = lax.scan(step, s0.astype(jnp.float32), xs)
    return jnp.swapaxes(ys, 0, 1), s_final

def _rwkv7(pr, shift_prev, wkv_prev, rwkv_mix, rwkv_w0, rwkv_w2, rwkv_a0, rwkv_a2, rwkv_g2,
           rwkv_k_k, rwkv_k_a, rwkv_r_k, rwkv_lnx_g, rwkv_lnx_b):
    B, T, _ = pr.shape
    f32 = jnp.float32
    prf = pr.astype(f32)
    prev = jnp.concatenate([shift_prev.astype(f32), prf[:, :-1]], axis=1)
    xm = prf + (prev - prf) * rwkv_mix.astype(f32)
    r, k, v, xw, xa, xg = jnp.split(xm, RWKV_SPLITS, axis=-1)
    w = -jax.nn.softplus(-(rwkv_w0 + jnp.tanh(xw) @ rwkv_w2)) - 0.5
    a = jax.nn.sigmoid(rwkv_a0 + xa @ rwkv_a2)
    g = jax.nn.sigmoid(xg) @ rwkv_g2

    def heads(t):
        return t.reshape(B, T, H_R, HEAD_R)

    kk = heads(k * rwkv_k_k)
    kk = kk / jnp.maximum(jnp.linalg.norm(kk, axis=-1, keepdims=True), 1e-12)
    k = heads(k * (1.0 + (a - 1.0) * rwkv_k_a))
    r, v, a = heads(r), heads(v), heads(a)
    decay = jnp.exp(-jnp.exp(heads(w)))
    y, wkv_new = _wkv7_scan(r, decay, k, v, -kk, kk * a, wkv_prev)
    yc = y - jnp.mean(y, axis=-1, keepdims=True)
    y = yc * lax.rsqrt(jnp.mean(yc * yc, axis=-1, keepdims=True) + LNX_EPS)
    y = y.reshape(B, T, D_R) * rwkv_lnx_g + rwkv_lnx_b
    bonus = jnp.sum(r * k * rwkv_r_k, axis=-1, keepdims=True) * v
    y = (y + bonus.reshape(B, T, D_R)) * g
    return y.astype(pr.dtype), pr[:, -1:], wkv_new

def _fox_attend(q, k, v, logf, q_offset):
    T = q.shape[1]
    c = jnp.swapaxes(jnp.cumsum(logf, axis=1), 1, 2)
    scale = HEAD_F ** -0.5
    outs = []
    for start in range(0, T, Q_BLOCK):
        stop = min(start + Q_BLOCK, T)
        k_end = q_offset + stop
        s = jnp.einsum('bqhd,bkhd->bhqk', q[:, start:stop], k[:, :k_end]).astype(jnp.float32) * scale
        s = s + c[:, :, q_offset + start:k_end, None] - c[:, :, None, :k_end]
        q_pos = jnp.arange(q_offset + start, k_end)
        mask = jnp.arange(k_end)[None, :] <= q_pos[:, None]
        s = jnp.where(mask, s, -jnp.inf)
        p = jax.nn.softmax(s, axis=-1).astype(v.dtype)
        outs.append(jnp.einsum('bhqk,bkhd->bqhd', p, v[:, :k_end]))
    return jnp.concatenate(outs, axis=1)

def _fox(pf, k_past, v_past, logf_past, fox_b_f, fox_norm_g):
    B, T, _ = pf.shape
    q, k, v, f_logit = jnp.split(pf, (D_F, 2 * D_F, 3 * D_F), axis=-1)
    q = q.reshape(B, T, H_F, HEAD_F)
    k = k.reshape(B, T, H_F, HEAD_F)
    v = v.reshape(B, T, H_F, HEAD_F)
    logf = jax.nn.log_sigmoid((f_logit + fox_b_f).astype(jnp.float32))
    k_all = jnp.concatenate([k_past.astype(k.dtype), k], axis=1)
    v_all = jnp.concatenate([v_past.astype(v.dtype), v], axis=1)
    logf_all = jnp.concatenate([logf_past.astype(jnp.float32), logf], axis=1)
    o = _fox_attend(q, k_all, v_all, logf_all, k_past.shape[1]).astype(jnp.float32)
    o = o * lax.rsqrt(jnp.mean(o * o, axis=-1, keepdims=True) + 1e-6)
    o = o.reshape(B, T, D_F) * fox_norm_g
    return o.astype(pf.dtype), k, v, logf

def _peer(h, peer_w_q, peer_keys1, peer_keys2, peer_u, peer_v):
    B, T, D = h.shape
    f32 = jnp.float32
    n = B * T
    n_pad = (-n) % PEER_BLOCK
    xb = jnp.pad(h.reshape(n, D), ((0, n_pad), (0, 0))).reshape(-1, PEER_BLOCK, D)
    keys1 = peer_keys1.astype(f32)
    keys2 = peer_keys2.astype(f32)

    def block(xt):
        q = (xt @ peer_w_q).reshape(PEER_BLOCK, PEER_HEADS, 2, D_KEY_HALF).astype(f32)
        s1 = jnp.einsum('thd,nd->thn', q[:, :, 0], keys1)
        s2 = jnp.einsum('thd,nd->thn', q[:, :, 1], keys2)
        v1, i1 = lax.top_k(s1, PEER_TOPK)
        v2, i2 = lax.top_k(s2, PEER_TOPK)
        cand_s = (v1[..., :, None] + v2[..., None, :]).reshape(PEER_BLOCK, PEER_HEADS, PEER_TOPK * PEER_TOPK)
        cand_i = (i1[..., :, None] * N_KEYS + i2[..., None, :]).reshape(PEER_BLOCK, PEER_HEADS, PEER_TOPK * PEER_TOPK)
        best_s, pos = lax.top_k(cand_s, PEER_TOPK)
        idx = jnp.take_along_axis(cand_i, pos, axis=-1)
        gate = jax.nn.softmax(best_s, axis=-1)
        act = jax.nn.gelu(jnp.einsum('thkd,td->thk', peer_u[idx], xt).astype(f32), approximate=False)
        return jnp.einsum('thk,thkd->td', (gate * act).astype(peer_v.dtype), peer_v[idx])

    out = lax.map(block, xb).reshape(-1, D)[:n]
    return out.reshape(B, T, D).astype(h.dtype)

def _layer(h, shift_prev, wkv_prev, k_past, v_past, logf_past, *, w_in, rwkv_mix, rwkv_w0, rwkv_w2,
           rwkv_a0, rwkv_a2, rwkv_g2, rwkv_k_k, rwkv_k_a, rwkv_r_k, rwkv_lnx_g, rwkv_lnx_b, fox_b_f,
           fox_norm_g, w_out, ln1_g, ln1_b, peer_w_q, peer_keys1, peer_keys2, peer_u, peer_v, ln2_g, ln2_b):
    p = h @ w_in
    y_r, shift_new, wkv_new = _rwkv7(p[..., :RWKV_IN], shift_prev, wkv_prev, rwkv_mix, rwkv_w0, rwkv_w2,
                                     rwkv_a0, rwkv_a2, rwkv_g2, rwkv_k_k, rwkv_k_a, rwkv_r_k,
                                     rwkv_lnx_g, rwkv_lnx_b)
    y_f, k_new, v_new, logf_new = _fox(p[..., RWKV_IN:], k_past, v_past, logf_past, fox_b_f, fox_norm_g)
    mix = jnp.concatenate([y_r, y_f], axis=-1) @ w_out
    h = _layernorm(ALPHA * h + mix, ln1_g, ln1_b)
    h = _layernorm(ALPHA * h + _peer(h, peer_w_q, peer_keys1, peer_keys2, peer_u, peer_v), ln2_g, ln2_b)
    return h, (shift_new, wkv_new, k_new, v_new, logf_new)

def setup_inputs(seed: int = 0) -> dict:
    key = jax.random.key(seed)
    k = jax.random.split(key, 40)
    L = DEPTH
    col_scale = np.ones((D_IN,), np.float32)
    col_scale[2 * D_R:3 * D_R] = BETA
    col_scale[RWKV_IN + 2 * D_F:RWKV_IN + 3 * D_F] = BETA
    return {
        'x_prompt': _normal(k[0], (BATCH, SEQ, D_MODEL), 1.0),
        'x_sample': _normal(k[1], (DEC_BATCH, DEC_SEQ, D_MODEL), 1.0),
        'state_rwkv_shift': _normal(k[2], (L, DEC_BATCH, 1, RWKV_IN), 1.0),
        'state_rwkv_wkv': _normal(k[3], (L, DEC_BATCH, H_R, HEAD_R, HEAD_R), 0.3),
        'cache_fox_k': _normal(k[4], (L, DEC_BATCH, PAST_LEN, H_F, HEAD_F), 1.0),
        'cache_fox_v': _normal(k[5], (L, DEC_BATCH, PAST_LEN, H_F, HEAD_F), BETA),
        'cache_fox_logf': jax.nn.log_sigmoid(_normal(k[6], (L, DEC_BATCH, PAST_LEN, H_F), 0.5) + 2.0),
        'meta_tokens': _normal(k[7], (N_META, D_MODEL), 1.0),
        'ln_in_g': 1.0 + _normal(k[8], (D_MODEL,), 0.05),
        'ln_in_b': _normal(k[9], (D_MODEL,), 0.02),
        'w_in': _normal(k[10], (L, D_MODEL, D_IN), D_MODEL ** -0.5) * jnp.asarray(col_scale),
        'rwkv_mix': jax.random.uniform(k[11], (L, RWKV_IN), jnp.float32),
        'rwkv_w0': jax.random.uniform(k[12], (L, D_R), jnp.float32, -6.0, -1.0),
        'rwkv_w2': _normal(k[13], (L, LORA_W, D_R), 0.1 * LORA_W ** -0.5),
        'rwkv_a0': _normal(k[14], (L, D_R), 0.1),
        'rwkv_a2': _normal(k[15], (L, LORA_A, D_R), 0.3 * LORA_A ** -0.5),
        'rwkv_g2': _normal(k[16], (L, LORA_G, D_R), LORA_G ** -0.5),
        'rwkv_k_k': 0.85 + _normal(k[17], (L, D_R), 0.05),
        'rwkv_k_a': 1.0 + _normal(k[18], (L, D_R), 0.05),
        'rwkv_r_k': _normal(k[19], (L, H_R, HEAD_R), 0.1),
        'rwkv_lnx_g': 1.0 + _normal(k[20], (L, D_R), 0.05),
        'rwkv_lnx_b': _normal(k[21], (L, D_R), 0.02),
        'fox_b_f': 2.0 + _normal(k[22], (L, H_F), 0.5),
        'fox_norm_g': 1.0 + _normal(k[23], (L, D_F), 0.05),
        'w_out': _normal(k[24], (L, D_MIX, D_MODEL), BETA * D_MIX ** -0.5),
        'ln1_g': 1.0 + _normal(k[25], (L, D_MODEL), 0.05),
        'ln1_b': _normal(k[26], (L, D_MODEL), 0.02),
        'peer_w_q': _normal(k[27], (L, D_MODEL, PEER_HEADS * D_KEY), D_MODEL ** -0.5),
        'peer_keys1': _normal(k[28], (L, N_KEYS, D_KEY_HALF), D_KEY_HALF ** -0.5),
        'peer_keys2': _normal(k[29], (L, N_KEYS, D_KEY_HALF), D_KEY_HALF ** -0.5),
        'peer_u': _normal(k[30], (L, N_EXPERTS, D_MODEL), D_MODEL ** -0.5),
        'peer_v': _normal(k[31], (L, N_EXPERTS, D_MODEL), BETA),
        'ln2_g': 1.0 + _normal(k[32], (L, D_MODEL), 0.05),
        'ln2_b': _normal(k[33], (L, D_MODEL), 0.02),
    }

def reference(x_prompt, x_sample, state_rwkv_shift, state_rwkv_wkv, cache_fox_k, cache_fox_v, cache_fox_logf,
              meta_tokens, ln_in_g, ln_in_b, w_in, rwkv_mix, rwkv_w0, rwkv_w2, rwkv_a0, rwkv_a2, rwkv_g2,
              rwkv_k_k, rwkv_k_a, rwkv_r_k, rwkv_lnx_g, rwkv_lnx_b, fox_b_f, fox_norm_g, w_out, ln1_g, ln1_b,
              peer_w_q, peer_keys1, peer_keys2, peer_u, peer_v, ln2_g, ln2_b):
    B = x_prompt.shape[0]
    dt = x_prompt.dtype
    meta = jnp.broadcast_to(meta_tokens.astype(dt)[None], (B, N_META, D_MODEL))
    hp = _layernorm(jnp.concatenate([meta, x_prompt], axis=1), ln_in_g, ln_in_b)
    hs = _layernorm(x_sample, ln_in_g, ln_in_b)
    zero_shift = jnp.zeros((B, 1, RWKV_IN), dt)
    zero_wkv = jnp.zeros((B, H_R, HEAD_R, HEAD_R), jnp.float32)
    no_kv = jnp.zeros((B, 0, H_F, HEAD_F), dt)
    no_logf = jnp.zeros((B, 0, H_F), jnp.float32)
    p_states = []
    s_states = []
    for l in range(DEPTH):
        lp = dict(w_in=w_in[l], rwkv_mix=rwkv_mix[l], rwkv_w0=rwkv_w0[l], rwkv_w2=rwkv_w2[l],
                  rwkv_a0=rwkv_a0[l], rwkv_a2=rwkv_a2[l], rwkv_g2=rwkv_g2[l], rwkv_k_k=rwkv_k_k[l],
                  rwkv_k_a=rwkv_k_a[l], rwkv_r_k=rwkv_r_k[l], rwkv_lnx_g=rwkv_lnx_g[l],
                  rwkv_lnx_b=rwkv_lnx_b[l], fox_b_f=fox_b_f[l], fox_norm_g=fox_norm_g[l], w_out=w_out[l],
                  ln1_g=ln1_g[l], ln1_b=ln1_b[l], peer_w_q=peer_w_q[l], peer_keys1=peer_keys1[l],
                  peer_keys2=peer_keys2[l], peer_u=peer_u[l], peer_v=peer_v[l], ln2_g=ln2_g[l], ln2_b=ln2_b[l])
        hp, st_p = _layer(hp, zero_shift, zero_wkv, no_kv, no_kv, no_logf, **lp)
        hs, st_s = _layer(hs, state_rwkv_shift[l], state_rwkv_wkv[l], cache_fox_k[l], cache_fox_v[l],
                          cache_fox_logf[l], **lp)
        p_states.append(st_p)
        s_states.append(st_s)
    p_shift, p_wkv, p_k, p_v, p_logf = (jnp.stack(z) for z in zip(*p_states))
    s_shift, s_wkv, s_k, s_v, s_logf = (jnp.stack(z) for z in zip(*s_states))
    y_prompt = hp[:, N_META:]
    y_sample = hs
    return (y_prompt, y_sample, p_shift, p_wkv, p_k, p_v, p_logf, s_shift, s_wkv, s_k, s_v, s_logf)


_drawn_inputs = setup_inputs


def setup_inputs(seed=0):
    import zlib

    import numpy as np

    out = dict(_drawn_inputs(seed))
    spreads = {}
    factors = {'cache_fox_logf': 3.374, 'rwkv_w2': 6.92, 'rwkv_lnx_b': 3.553, 'ln2_b': 2.842}
    for name, (base, spread) in spreads.items():
        noise = np.random.default_rng([zlib.crc32(name.encode()), seed]).standard_normal(out[name].shape)
        drawn = base * np.exp(spread * noise) if base else spread * noise
        out[name] = jnp.asarray(drawn.astype(out[name].dtype))
    for name, factor in factors.items():
        out[name] = (out[name] * factor).astype(out[name].dtype)
    return out
```

```python
from contextlib import ExitStack

import numpy as np

import concourse.bass as bass
from concourse import mybir

ALU = mybir.AluOpType
ACT = mybir.ActivationFunctionType
AX_X = mybir.AxisListType.X
F32 = mybir.dt.float32
F32R = mybir.dt.float32r
U32 = mybir.dt.uint32

P = 128
D = 1024
KT = D // P
N_META, SEQ, DEC, PAST = 16, 256, 64, 512
TP = N_META + SEQ
T = TP + DEC
H, HD = 8, 64
NJ = H * HD // P
RW_TILES = 14
CH = 64
PADP = -(-TP // CH) * CH
TC = PADP + DEC
NG = TC // P
QB = 96
NQB = -(-TP // QB)
KEYS = PAST + DEC
KX = HD + H
NK = 128
PH, TOPK = 8, 16
ALPHA = 2.0 ** 0.25
LN_EPS = 1e-5
LNX_EPS = 64e-5
NEG = -1.0e30
NI = NK
RIT = 4
GIT = 6
LOW = -3.0e38
CDEC = -float(np.exp(-0.5))

COLS = {}
_n = 0
for _name, _w in (("ln_in_g", 8), ("ln_in_b", 8), ("ln1_g", 8), ("ln1_b", 8), ("ln2_g", 8), ("ln2_b", 8),
                  ("mix", 14), ("w0", 4), ("a0", 4), ("k_k", 4), ("k_a", 4), ("r_k", 4), ("lnx_g", 4),
                  ("lnx_b", 4), ("fnorm", 4), ("shift", 14), ("b_f", 1)):
    COLS[_name] = _n
    _n += _w
NCOL = _n

V_ITEMS, K_ITEMS, Q_ITEMS = 4, NJ, NJ
RW_ORDER = [12, 13, 4, 5, 6, 7, 0, 1, 2, 3, 8, 9, 10, 11]
I_K = V_ITEMS
I_Q = I_K + K_ITEMS
I_RW = I_Q + Q_ITEMS
I_WO = I_RW + RW_TILES
I_WQ = I_WO + KT
N_ITEMS = I_WQ + 2 * PH
RAWS, HIS = 3, 2

PROMPT_UNITS = [("p", h, b) for h in range(H) for b in range(NQB)]
UNITS = PROMPT_UNITS[:12] + [("s", 0, 0), ("s", 1, 0)] + PROMPT_UNITS[12:] + [("s", 2, 0), ("s", 3, 0)]
NU = len(UNITS)


def unit_shape(u):
    kind, a, b = u
    if kind == "s":
        return P, KEYS, [(0, 64)] + [(64 + P * i, P) for i in range(4)]
    rows = min(QB, TP - QB * b)
    tiles = [(QB * i, min(QB, TP - QB * i)) for i in range(b + 1)]
    return rows, sum(n for _, n in tiles), tiles


def build(nc, xT, cols, wbig, wf, w2a2, g2, keysT, ckT, cv, clf, s0T, uT, vE,
          yT, wkvo, ko, vpo, vso, lfo, sho):
    ctx = ExitStack()
    with ctx:
        BASE = 16512
        MAIN = P * T * 4
        TAIL = BASE + MAIN

        def at(name, shape, off, dt=F32):
            return nc.alloc_sbuf_tensor_at(name, list(shape), dt, offset=off)

        class Region:

            def __init__(self, start, end):
                self.pos, self.end = start, end

            def put(self, name, shape, dt=F32):
                n = int(np.prod(shape[1:])) * 4
                n = -(-n // 32) * 32
                t = at(name, shape, self.pos, dt)
                self.pos += n
                assert self.pos <= self.end, (name, self.pos - self.end)
                return t

        def sem(name):
            return ctx.enter_context(nc.semaphore(name))

        def region_end():
            return 229368

        tail = Region(TAIL, region_end())
        colv = tail.put("colv", [P, NCOL])
        H1h = tail.put("H1h", [P, KT, T], F32R)
        H1l = tail.put("H1l", [P, KT, T], F32R)
        ring_at = tail.pos
        hraw = [tail.put(f"hraw{i}", [P, 512]) for i in range(4)]
        hlo = [at(f"hlo{i}", [P, 512], ring_at + 2048 * i, F32R) for i in range(4)]
        hhi_at = tail.pos
        hhi = [tail.put(f"hhi{i}", [P, 512], F32R) for i in range(2)]
        hhiq = [at(f"hhiq{i}", [P, 256], hhi_at + 1024 * i, F32R) for i in range(4)]
        pairs_at = tail.pos
        pair1 = tail.put("pair1", [P, T])
        pair2 = tail.put("pair2", [P, T])
        pairg = tail.put("pairg", [P, T])
        iotak = tail.put("iotak", [P, NK])
        one_hots = Region(ring_at, pairs_at)
        ohA = one_hots.put("ohA", [P, 3, 4, NK])
        ohB = one_hots.put("ohB", [P, 3, 4, NK])
        wsplit = Region(pairs_at, region_end())
        Wh = [wsplit.put(f"Wh{i}", [P, T], F32R) for i in range(2)]
        Wl = [wsplit.put(f"Wl{i}", [P, T], F32R) for i in range(2)]

        W = at("W", [P, NI, T], BASE)
        routing = Region(BASE + 96 * T * 4, TAIL)
        scores = routing.put("scores", [P, 3 * 2 * PH * NK])
        top1 = routing.put("top1", [P, 16])
        top2 = routing.put("top2", [P, 16])
        ix1 = routing.put("ix1", [P, 16], U32)
        ix2 = routing.put("ix2", [P, 16], U32)
        ix1f = routing.put("ix1f", [P, 16])
        ix2f = routing.put("ix2f", [P, 16])
        knock1 = routing.put("knock1", [P, NK])
        knock2 = routing.put("knock2", [P, NK])
        cand = routing.put("cand", [P, 16, 16])
        candk = routing.put("candk", [P, 16, 16])
        pos = routing.put("pos", [P, 16], U32)
        posh = routing.put("posh", [P, 16], U32)
        posl = routing.put("posl", [P, 16], U32)
        poshf = routing.put("poshf", [P, 16])
        poslf = routing.put("poslf", [P, 16])
        hit1 = routing.put("hit1", [P, 16, 16])
        hit2 = routing.put("hit2", [P, 16, 16])
        iota16 = routing.put("iota16", [P, 16, 16])
        best = routing.put("best", [P, 3 * PH, 16])
        sel1 = routing.put("sel1", [P, 3 * PH, 16])
        sel2 = routing.put("sel2", [P, 3 * PH, 16])
        gsum = routing.put("gsum", [P, 3 * PH])
        identb = routing.put("identb", [P, P])
        unit_s = routing.put("unit_s", [P, 2 * NK])
        top = routing.put("top", [P, 16])
        last = Region(BASE, TAIL)
        ones2 = last.put("ones2", [P, P])
        XF = last.put("XF", [P, KT, T])
        SQF = last.put("SQF", [P, KT, T])
        SDF = last.put("SDF", [P, T])

        m = Region(BASE, TAIL)
        ident = m.put("ident", [P, P])
        ones = m.put("ones", [P, P])
        blk = m.put("blk", [P, P])
        causal = m.put("causal", [P, 2 * P])
        lev = m.put("lev", [P, 6, P])
        eye2 = m.put("eye2", [P, HD])
        amask = m.put("amask", [P, P])
        keep = m.put("keep", [P, TC])
        ones8 = m.put("ones8", [H, KEYS])
        w2s = m.put("w2s", [P, NJ * P])
        g2s = m.put("g2s", [P, NJ * P])
        wfs = m.put("wfs", [P, KT, H])
        kst = m.put("kst", [P, 2, NK])
        hT = m.put("hT", [P, KT, T])
        xm = m.put("xm", [P, RW_TILES, TC])
        shs = m.put("shs", [P, RW_TILES, 2])
        states = m.put("states", [P, 8, NJ, HD])
        oT = m.put("oT", [P, NJ, T])
        SD = m.put("SD", [P, T])
        DL = m.put("DL", [P, NJ, TC // CH])
        att_at = m.pos
        lf = m.put("lf", [H, 4, T])
        lfs = m.put("lfs", [H, 2, KEYS])
        qx = m.put("qx", [KX, H, T])
        kx = m.put("kx", [KX, H, T])
        ckx = m.put("ckx", [KX, H, PAST])
        vp = m.put("vp", [P, NQB, H * HD])
        vs = m.put("vs", [P, 5, H * HD])
        pr = m.put("pr", [P, 2, KEYS])
        pt = m.put("pt", [P, 2, 5 * P])
        st = m.put("st", [P, 2, 4])
        att_end = m.pos
        xin = at("xin", [P, KT, T], att_at + 3 * 8192)
        SQ0 = at("SQ0", [P, KT, T], att_at + 3 * 8192 + 10752)
        g = Region(att_at, att_end)
        NR = g.put("NR", [P, H, 2 * P])
        AK = g.put("AK", [P, H, 2 * P])
        Tn = g.put("Tn", [P, H, P])
        TT = g.put("TT", [P, H, P])
        Xs = g.put("Xs", [P, H, P])
        Nm = g.put("Nm", [P, 2, H // 2, P])
        AX = g.put("AX", [P, H, P])
        X12 = g.put("X12", [P, H, P])
        bN = g.put("bN", [P, H, HD])
        kN = g.put("kN", [P, H, HD])
        vN = g.put("vN", [P, H, HD])
        Y1 = g.put("Y1", [P, NJ, P])
        MT = g.put("MT", [P, 2, NJ, HD])
        AR = g.put("AR", [P, NJ, NG, 2 * P])
        o = Region(att_at, att_end)
        MX = o.put("MX", [P, KT, T])
        MXh = o.put("MXh", [P, KT, T], F32R)
        MXl = o.put("MXl", [P, KT, T], F32R)
        X1 = o.put("X1", [P, KT, T])
        SQ1 = o.put("SQ1", [P, KT, T])
        QT = at("QT", [P, 2 * PH, T], att_at)
        wring_at = m.pos
        raw = [m.put(f"wraw{i}", [P, D]) for i in range(RAWS)]
        wlo = [at(f"wlo{i}", [P, D], wring_at + 4096 * i, F32R) for i in range(RAWS)]
        whi = [m.put(f"whi{i}", [P, D], F32R) for i in range(HIS)]
        AA = m.put("AA", [P, NJ, TC])
        Zs = at("Zs", [P, 2, NJ, HD], m.pos)
        pb = m.put("pb", [P, 3, TC + 1])
        hTh = at("hTh", [P, KT, T], TAIL + 448, F32R)
        hTl = at("hTl", [P, KT, T], TAIL + 448 + KT * T * 4, F32R)
        r2 = Region(TAIL + 448, region_end() - 512)
        SG = r2.put("SG", [P, NJ, TC])
        LS = r2.put("LS", [P, NJ, TC])
        KK = r2.put("KK", [P, NJ, TC])
        BH = r2.put("BH", [P, NJ, TC])
        KH = r2.put("KH", [P, NJ, TC])
        E1 = r2.put("E1", [P, NJ, TC])
        PS = ctx.enter_context(nc.psum_tensor("PS", [P, 8, 512], F32))

        s_cols, s_x, s_small, s_cache, s_out = (sem(x) for x in ("s_cols", "s_x", "s_small", "s_cache", "s_out"))
        s_shift = sem("s_shift")
        s_raw = [sem(f"s_raw{i}") for i in range(RAWS)]
        s_whi, s_wlo, s_item = sem("s_whi"), sem("s_wlo"), sem("s_item")
        s_pool, s_dve, s_act = sem("s_pool"), sem("s_dve"), sem("s_act")
        s_const, s_onesg = sem("s_const"), sem("s_onesg")
        s_mean, s_xc, s_sq, s_var, s_sd, s_ln = (sem(x) for x in ("s_mean", "s_xc", "s_sq", "s_var", "s_sd", "s_ln"))
        s_hhi, s_hlo = sem("s_hhi"), sem("s_hlo")
        s_f, s_fz, s_fe, s_logf, s_negc = (sem(x) for x in ("s_f", "s_fz", "s_fe", "s_logf", "s_negc"))
        s_vev, s_pev, s_xm = sem("s_vev"), sem("s_pev"), sem("s_xm")
        s_sc, s_max, s_exp, s_norm, s_tr, s_tev, s_pv, s_oev = (
            sem(x) for x in ("s_sc", "s_max", "s_exp", "s_norm", "s_tr", "s_tev", "s_pv", "s_oev"))
        s_tanh, s_lora, s_loev, s_sgate, s_ggev = (
            sem(x) for x in ("s_tanh", "s_lora", "s_loev", "s_sgate", "s_ggev"))
        s_ls, s_d, s_lprev, s_dprev, s_kkraw, s_kksq, s_n2, s_n2m, s_kkrt = (
            sem(x) for x in ("s_ls", "s_d", "s_lprev", "s_dprev", "s_kkraw", "s_kksq", "s_n2", "s_n2m", "s_kkrt"))
        s_rk, s_bsum, s_prep = sem("s_rk"), sem("s_bsum"), sem("s_prep")
        s_nat, s_natev, s_A, s_Aev, s_tt, s_tn, s_tnev, s_nm, s_lx, s_xs, s_ly, s_up = (
            sem(x) for x in ("s_nat", "s_natev", "s_A", "s_Aev", "s_tt", "s_tn", "s_tnev", "s_nm", "s_lx", "s_xs",
                             "s_ly", "s_up"))
        s_akv, s_akvev, s_w1, s_w1ev, s_y1, s_y1ev, s_z, s_zev, s_ya, s_yaev, s_ms, s_stt, s_y, s_yev = (
            sem(x) for x in ("s_akv", "s_akvev", "s_w1", "s_w1ev", "s_y1", "s_y1ev", "s_z", "s_zev", "s_ya", "s_yaev",
                             "s_ms", "s_stt", "s_y", "s_yev"))
        s_gm, s_gc, s_gsq, s_gv, s_gsd = (sem(x) for x in ("s_gm", "s_gc", "s_gsq", "s_gv", "s_gsd"))
        s_osq, s_ov, s_osd = sem("s_osq"), sem("s_ov"), sem("s_osd")
        s_mx, s_mxh, s_mxl, s_wo = sem("s_mx"), sem("s_mxh"), sem("s_mxl"), sem("s_wo")
        s_h1h, s_h1l, s_qev, s_scp, s_scev = (sem(x) for x in ("s_h1h", "s_h1l", "s_qev", "s_scp", "s_scev"))
        s_rconst = sem("s_rconst")
        s_hraw = [sem(f"s_hraw{i}") for i in range(4)]
        s_hhi2, s_hlo2, s_up_mm, s_gelu = sem("s_hhi2"), sem("s_hlo2"), sem("s_up_mm"), sem("s_gelu")
        s_routed, s_gexp, s_gate, s_pt, s_pairs = (
            sem(x) for x in ("s_routed", "s_gexp", "s_gate", "s_pt", "s_pairs"))
        s_oha, s_ohr, s_ohb, s_grid, s_w = (sem(x) for x in ("s_oha", "s_ohr", "s_ohb", "s_grid", "s_w"))
        s_vraw = [sem(f"s_vraw{i}") for i in range(4)]
        s_vhi, s_vlo, s_wh, s_wl, s_down = (sem(x) for x in ("s_vhi", "s_vlo", "s_wh", "s_wl", "s_down"))
        s_hf, s_xf = sem("s_hf"), sem("s_xf")

        def col(name, k=0, n=1, rows=P):
            c = COLS[name] + k
            return colv[0:rows, c:c + n]

        def over(ap2, n):
            return ap2.unsqueeze(1).to_broadcast([ap2.shape[0], n, ap2.shape[1]])

        def along(ap2, n):
            return ap2.unsqueeze(2).to_broadcast([ap2.shape[0], ap2.shape[1], n])

        def flat(t3, a, n):
            return t3[:].rearrange("p x y -> p (x y)")[:, a:a + n]

        def head(h):
            return h // 2, HD * (h % 2)

        block = ctx.enter_context(nc.Block())

        @block.sync
        def _(sp):
            sp.dma_start(colv[:], cols).then_inc(s_cols, 16)
            sp.dma_start(xin[:], xT).then_inc(s_x, 16)
            sp.dma_start(wfs[:], wf).then_inc(s_small, 16)
            sp.dma_start(w2s[:], w2a2).then_inc(s_small, 16)
            sp.dma_start(g2s[:], g2).then_inc(s_small, 16)
            sp.dma_start(kst[:], keysT).then_inc(s_small, 16)
            sp.dma_start(states[:, 6, :, :], s0T).then_inc(s_small, 16)

            def load(i):
                if i >= RAWS:
                    sp.wait_ge(s_item, i - RAWS + 1)
                sp.dma_start(raw[i % RAWS][:], wbig[i]).then_inc(s_raw[i % RAWS], 16)

            for i in range(I_RW):
                load(i)
                if i == RAWS - 1:
                    sp.wait_ge(s_ln, 1)
                    sp.dma_start(ckx[0:HD, :, :], ckT).then_inc(s_cache, 16)
                    sp.dma_start(vs[0:HD, 0, :], cv[0:HD, :]).then_inc(s_cache, 16)
                    sp.dma_start(vs[:, 1:4, :], cv[HD:PAST - HD, :].rearrange("(i p) c -> p i c", p=P)).then_inc(s_cache, 16)
                    sp.dma_start(vs[0:HD, 4, :], cv[PAST - HD:PAST, :]).then_inc(s_cache, 16)
                    sp.dma_start(lfs[:, 0, 0:PAST], clf).then_inc(s_cache, 16)
            sp.wait_ge(s_vev, 4)
            for b in range(NQB):
                n = min(QB, TP - QB * b)
                sp.dma_start(vpo[QB * b:QB * b + n, :], vp[0:n, b, :]).then_inc(s_out, 16)
            sp.dma_start(vso, vs[HD:P, 4, :]).then_inc(s_out, 16)
            sp.wait_ge(s_pev, K_ITEMS)
            sp.dma_start(ko, kx[0:HD, :, :]).then_inc(s_out, 16)
            sp.wait_ge(s_logf, 1)
            sp.dma_start(lfo, lf[:, 2, :]).then_inc(s_out, 16)
            for i in range(I_RW, I_WO):
                load(i)
            sp.wait_ge(s_shift, RW_TILES)
            sp.dma_start(sho, shs[:]).then_inc(s_out, 16)
            for i in range(I_WO, N_ITEMS):
                load(i)
                if i == I_WO + RAWS - 1:
                    sp.wait_ge(s_stt, 6)
                    sp.dma_start(wkvo[:, 0], states[:, 5, :, :]).then_inc(s_out, 16)
                    sp.dma_start(wkvo[:, 1], states[:, 7, :, :]).then_inc(s_out, 16)

            sp.wait_ge(s_mx, 1)
            for q in range(4):
                sp.dma_start(hraw[q][:], uT[q]).then_inc(s_hraw[q], 16)
            with sp.Fori(1, 2 * NI // 4) as k:
                for q in range(4):
                    sp.wait_ge(s_up_mm, k * 8 + (2 * q - 6))
                    sp.dma_start(hraw[q][:], uT[bass.ds(k * 4 + q, 1)].rearrange("a p c -> (a p) c")).then_inc(s_hraw[q], 16)
            sp.wait_ge(s_grid, T // 4)
            for q in range(4):
                sp.dma_start(hraw[q][:], vE[q]).then_inc(s_vraw[q], 16)
            with sp.Fori(1, 2 * NI // 4) as k:
                for q in range(4):
                    sp.wait_ge(s_down, k * 4 + (q - 3))
                    sp.dma_start(hraw[q][:], vE[bass.ds(k * 4 + q, 1)].rearrange("a p c -> (a p) c")).then_inc(s_vraw[q], 16)
            sp.wait_ge(s_xf, 2)
            sp.dma_start(yT, XF[:]).then_inc(s_out, 16)
            sp.wait_ge(s_out, 16 * (NQB + 1 + 1 + 1 + 1 + 2 + 1))

        @block.gpsimd
        def _(pool):
            n = [0]

            def own(ins):
                n[0] += 1
                ins.then_inc(s_pool, 1)
                pool.wait_ge(s_pool, n[0])

            def select(t, pattern, op, base, cm, fill):
                own(nc.gpsimd.affine_select(out=t, in_=t, pattern=pattern, compare_op=op, fill=fill, base=base,
                                            channel_multiplier=cm))

            nc.gpsimd.memset(ones[:], 1.0 / D).then_inc(s_onesg, 1)
            own(nc.gpsimd.memset(ident[:], 0.0))
            select(ident[:], [[-1, P]], ALU.not_equal, 0, 1, 1.0)
            own(nc.gpsimd.memset(blk[:], 0.0))
            for e in range(2):
                own(nc.gpsimd.memset(blk[HD * e:HD * e + HD, HD * e:HD * e + HD], 1.0 / HD))
            own(nc.gpsimd.memset(causal[:], 1.0))
            for e, base in ((0, -1), (1, 0)):
                c = causal[:, P * e:P * e + P]
                select(c, [[1, P]], ALU.is_ge, base, -1, 0.0)
                own(nc.gpsimd.memset(c[0:CH, CH:P], 0.0))
            own(nc.gpsimd.memset(lev[:], 0.0))
            for l in range(6):
                b = 1 << l
                v = lev[:, l, :].rearrange("p (g x b) -> p g x b", x=2, b=b)[:, :, 1, :]
                own(nc.gpsimd.memset(v, 1.0))
                pat = [[2 * b, P // (2 * b)], [0, b]]
                select(v, [[-2 * b, P // (2 * b)], [0, b]], ALU.is_ge, 0, 1, 0.0)
                select(v, pat, ALU.is_ge, b - 1, -1, 0.0)
            own(nc.gpsimd.memset(eye2[:], 0.0))
            select(eye2[:], [[-1, HD]], ALU.not_equal, 0, 1, 1.0)
            select(eye2[:], [[-1, HD]], ALU.not_equal, -HD, 1, 1.0)
            own(nc.gpsimd.memset(amask[:], 0.0))
            select(amask[:], [[-1, P]], ALU.is_ge, 0, 1, NEG)
            own(nc.gpsimd.memset(keep[:], 1.0))
            own(nc.gpsimd.memset(keep[:, 0:TC:CH], 0.0))
            own(nc.gpsimd.memset(ones8[:], 1.0))
            own(nc.gpsimd.memset(qx[HD:KX, :, :], 0.0))
            select(qx[HD:KX, :, :], [[-1, H], [0, T]], ALU.not_equal, 0, 1, 1.0)
            own(nc.gpsimd.memset(pb[:, :, 0:1], 0.0))
            own(nc.gpsimd.memset(pb[:, :, TP + 1:PADP], 0.0))
            own(nc.gpsimd.memset(states[:, 0, :, :], 0.0))
            own(nc.gpsimd.iota(iotak[:], pattern=[[1, NK]], base=0, channel_multiplier=0,
                               allow_small_or_imprecise_dtypes=True))
            nc.gpsimd.sem_inc(s_const, 1)

            pool.wait_ge(s_logf, 2)
            pool.wait_ge(s_ln, 1)
            for dst, src, w in ((kx[HD:KX, :, 0:TP], lf[:, 3, 0:TP], TP),
                                (kx[HD:KX, :, TP:T], lfs[:, 1, PAST:KEYS], DEC),
                                (ckx[HD:KX, :, :], lfs[:, 1, 0:PAST], PAST)):
                nc.gpsimd.tensor_scalar(dst, over(src, H), -1.0, 0.0, ALU.mult, ALU.add).then_inc(s_negc, 1)

            n_nm = 0
            for gi in range(NG):
                for l in range(1, 6):
                    for hf in range(2):
                        if l == 1:
                            pool.wait_ge(s_Aev, 4 * gi + 2 * hf + 1)
                        if n_nm >= 2:
                            pool.wait_ge(s_lx, n_nm - 1)
                        nc.gpsimd.tensor_tensor(Nm[:, hf, :, :], NR[:, 4 * hf:4 * hf + 4, 0:P], over(lev[:, l, :], 4),
                                                ALU.mult).then_inc(s_nm, 1)
                        n_nm += 1

            pool.wait_ge(s_scp, 12)
            own(nc.gpsimd.memset(identb[:], 0.0))
            select(identb[:], [[-1, P]], ALU.not_equal, 0, 1, 1.0)
            own(nc.gpsimd.iota(iota16[:], pattern=[[0, 16], [1, 16]], base=0, channel_multiplier=0,
                               allow_small_or_imprecise_dtypes=True))
            nc.gpsimd.sem_inc(s_rconst, 1)

            def lo(c, q):
                pool.wait_ge(s_hhi2, c + 1)
                cols_ = slice(256 * (q % 2), 256 * (q % 2) + 256)
                nc.gpsimd.tensor_tensor(hlo[q // 2 % 4][:, cols_], hraw[q // 2 % 4][:, cols_], hhiq[q % 4][:].bitcast(F32),
                                        ALU.subtract).then_inc(s_hlo2, 1)

            for q in range(4 * RIT):
                lo(q, q)
            with pool.Fori(1, NI // RIT) as k:
                for q in range(4 * RIT):
                    lo(k * (4 * RIT) + q, q)

            pool.wait_ge(s_down, 2 * NI)
            nc.gpsimd.memset(ones2[:], 1.0 / D).then_inc(s_onesg, 1)

        @block.scalar
        def _(act):
            n = [0]

            def own(ins):
                n[0] += 1
                ins.then_inc(s_act, 1)
                act.wait_ge(s_act, n[0])

            def A(out, in_, f, **kw):
                return nc.scalar.activation(out, in_, f, **kw)

            def norm_stats(k, X, S, sd, eps):
                act.wait_ge(s_xc, k)
                A(S[:], X[:], ACT.Square).then_inc(s_sq, 1)
                act.wait_ge(s_var, k)
                A(sd[:], PS[:, 1, 0:T], ACT.Sqrt, bias=eps).then_inc(s_sd, 1)

            norm_stats(1, xin, SQ0, SD, LN_EPS)
            act.wait_ge(s_ln, 1)
            A(hTh[:], hT[:], ACT.Copy).then_inc(s_hhi, 1)

            def whi_of(i):
                act.wait_ge(s_raw[i % RAWS], 16 * (i // RAWS + 1))
                if i >= HIS:
                    act.wait_ge(s_item, i - HIS + 1)
                A(whi[i % HIS][:], raw[i % RAWS][:], ACT.Copy).then_inc(s_whi, 1)

            def evacuate(i):
                if i < V_ITEMS:
                    if i == V_ITEMS - 1:
                        act.wait_ge(s_item, V_ITEMS)
                        act.wait_ge(s_cache, 80)
                        for b in range(NQB):
                            A(vp[0:QB, b, :], PS[0:QB, 4 + b, :], ACT.Copy).then_inc(s_vev, 1)
                        A(vs[HD:P, 4, :], PS[HD:P, 7, :], ACT.Copy).then_inc(s_vev, 1)
                    return
                act.wait_ge(s_item, i + 1)
                b = PS[:, i % 2, :]
                if i < I_RW:
                    dst, j, scale = (kx, i - I_K, 1.0) if i < I_Q else (qx, i - I_Q, HD ** -0.5)
                    A(dst[0:HD, 2 * j, :], b[0:HD, 0:T], ACT.Copy, scale=scale)
                    A(dst[0:HD, 2 * j + 1, :], b[HD:P, 0:T], ACT.Copy, scale=scale).then_inc(s_pev, 1)
                    return
                r = i - I_RW
                t = RW_ORDER[r]
                if r >= 3:
                    act.wait_ge(s_xm, r - 2)
                s = pb[:, r % 3, :]
                A(s[:, 1:TP + 1], b[:, 0:TP], ACT.Copy)
                A(s[:, PADP:PADP + 1], col("shift", t), ACT.Copy)
                A(shs[:, t, :], b[:, TP - 1:T:DEC], ACT.Copy).then_inc(s_shift, 1)
                A(s[:, PADP + 1:TC + 1], b[:, TP:T], ACT.Copy).then_inc(s_pev, 1)

            def attention(s):
                if s < NU:
                    rows, keys, _ = unit_shape(UNITS[s])
                    act.wait_ge(s_max, s + 1)
                    if s >= 2:
                        act.wait_ge(s_tr, s - 1)
                    b = 2 if UNITS[s][0] == "s" else 2 + s % 2
                    A(pr[0:rows, s % 2, 0:keys], flat(PS, 512 * b, keys)[0:rows], ACT.Exp,
                      bias=st[0:rows, s % 2, 1:2], accum_out=st[0:rows, s % 2, 2:3]).then_inc(s_exp, 1)
                if 1 <= s <= NU:
                    u = s - 1
                    rows, _, tiles = unit_shape(UNITS[u])
                    act.wait_ge(s_tr, u + 1)
                    if u >= 2:
                        act.wait_ge(s_pv, u - 1)
                    b = 4 if UNITS[u][0] == "s" else 4 + u % 2
                    parts = [(0, 1, 64), (1, 5, P)] if UNITS[u][0] == "s" else [(i, i + 1, w) for i, (_, w) in enumerate(tiles)]
                    for a, z, w in parts:
                        ins = A(pt[0:w, u % 2, P * a:P * z].rearrange("p (x r) -> p x r", r=P)[:, :, 0:rows],
                                flat(PS, 512 * b + P * a, P * (z - a))[0:w].rearrange("p (x r) -> p x r", r=P)[:, :, 0:rows],
                                ACT.Copy)
                    ins.then_inc(s_tev, 1)
                if s >= 2:
                    u = s - 2
                    kind, a, qb = UNITS[u]
                    act.wait_ge(s_pv, u + 1)
                    if kind == "s":
                        A(oT[:, a, TP:T], PS[:, 6 + u % 2, 0:DEC], ACT.Copy).then_inc(s_oev, 1)
                    else:
                        rows = unit_shape(UNITS[u])[0]
                        j, o_ = head(a)
                        A(oT[o_:o_ + HD, j, QB * qb:QB * qb + rows], PS[o_:o_ + HD, 6 + u % 2, 0:rows],
                          ACT.Copy).then_inc(s_oev, 1)

            act.wait_ge(s_const, 1)
            whi_of(0)
            act.wait_ge(s_fz, 1)
            own(A(lf[:, 1, :], lf[:, 1, :], ACT.Exp, scale=-1.0))
            A(lf[:, 1, :], lf[:, 1, :], ACT.Ln, bias=1.0).then_inc(s_fe, 1)
            for i in range(I_WO):
                if i + 1 < I_WO:
                    whi_of(i + 1)
                evacuate(i)
                if i >= I_RW:
                    attention(2 * (i - I_RW))
                    attention(2 * (i - I_RW) + 1)
            for s in range(2 * RW_TILES, NU + 2):
                attention(s)

            act.wait_ge(s_xm, RW_TILES)
            A(xm[0:HD, 12, :], xm[0:HD, 12, :], ACT.Tanh).then_inc(s_tanh, 1)
            A(xm[:, 13, :], xm[:, 13, :], ACT.Sigmoid).then_inc(s_tanh, 1)
            for j in range(NJ):
                act.wait_ge(s_lora, 2 * j + 1)
                A(SG[:, j, :], PS[:, 0, 0:TC], ACT.Sigmoid, bias=col("w0", j)).then_inc(s_loev, 1)
                act.wait_ge(s_lora, 2 * j + 2)
                A(AA[:, j, :], PS[:, 1, 0:TC], ACT.Sigmoid, bias=col("a0", j)).then_inc(s_loev, 1)
            act.wait_ge(s_ls, 1)
            A(E1[:], LS[:], ACT.Exp, scale=CDEC).then_inc(s_d, 1)
            act.wait_ge(s_lprev, 1)
            own(A(SG[:], SG[:], ACT.Exp, scale=CDEC))
            A(LS[:], LS[:], ACT.Exp, scale=-CDEC).then_inc(s_dprev, 1)
            act.wait_ge(s_kkraw, 1)
            A(KH[:], BH[:], ACT.Square).then_inc(s_kksq, 1)
            act.wait_ge(s_n2m, 1)
            A(KK[:], KK[:], ACT.Sqrt).then_inc(s_kkrt, 1)
            act.wait_ge(s_bsum, 1)
            for j in range(NJ):
                act.wait_ge(s_sgate, j + 1)
                A(xm[:, j, :], PS[:, 6 + j % 2, 0:TC], ACT.Copy).then_inc(s_ggev, 1)

            act.wait_ge(s_oev, NU)
            act.wait_ge(s_out, 16 * (NQB + 4))
            for gi in range(NG):
                for k, dst in enumerate((vN, bN, kN, AX)):
                    act.wait_ge(s_nat, 4 * gi + k + 1)
                    if k == 0 and gi:
                        act.wait_ge(s_ya, gi)
                    src = PS[:, 6 + k % 2, :].rearrange("p (h c) -> p h c", c=HD)
                    A(dst[:, :, 0:HD], src, ACT.Copy).then_inc(s_natev, 1)
                act.wait_ge(s_akv, gi + 1)
                A(AX[:, :, HD:P], PS[:, 6, :].rearrange("p (h c) -> p h c", c=HD), ACT.Copy).then_inc(s_akvev, 1)
                for hf in range(2):
                    act.wait_ge(s_tn, 2 * gi + hf + 1)
                    A(Tn[:, 4 * hf:4 * hf + 4, :], PS[:, 4 + hf, :].rearrange("p (h c) -> p h c", c=P),
                      ACT.Copy).then_inc(s_tnev, 1)
                for l in range(1, 6):
                    for hf in range(2):
                        act.wait_ge(s_lx, 10 * gi + 2 * (l - 1) + hf + 1)
                        if l > 1 or gi:
                            act.wait_ge(s_ly, 10 * gi + 2 * (l - 1) + hf - 1)
                        A(Xs[:, 4 * hf:4 * hf + 4, :], PS[:, hf, :].rearrange("p (h c) -> p h c", c=P),
                          ACT.Copy).then_inc(s_xs, 1)
                for hf in range(2):
                    act.wait_ge(s_w1, 2 * gi + hf + 1)
                    A(X12[:, 4 * hf:4 * hf + 4, :], PS[:, hf, :].rearrange("p (h c) -> p h c", c=P),
                      ACT.Copy).then_inc(s_w1ev, 1)
                act.wait_ge(s_ya, gi + 1)
                A(SG[:, :, P * gi:P * gi + P], PS[:, 7, :].rearrange("p (j t) -> p j t", j=NJ), ACT.Copy).then_inc(s_yaev, 1)

            act.wait_ge(s_gc, 1)
            A(E1[:], SG[:], ACT.Square).then_inc(s_gsq, 1)
            act.wait_ge(s_gv, 1)
            A(KK[:].rearrange("p j t -> p (j t)"), flat(PS, 3 * 512, NJ * TC), ACT.Sqrt, bias=LNX_EPS).then_inc(s_gsd, 1)
            A(KH[:, :, 0:T], oT[:], ACT.Square).then_inc(s_osq, 1)
            act.wait_ge(s_ov, 1)
            A(BH[:, :, 0:T], PS[:, 4:8, 0:T], ACT.Sqrt, bias=1e-6).then_inc(s_osd, 1)
            act.wait_ge(s_mx, 1)
            A(MXh[:], MX[:], ACT.Copy).then_inc(s_mxh, 1)
            for i in range(I_WO, I_WQ):
                whi_of(i)
            norm_stats(2, X1, SQ1, SD, LN_EPS)
            act.wait_ge(s_ln, 2)
            A(H1h[:], X1[:], ACT.Copy).then_inc(s_h1h, 1)

            for i in range(I_WQ, N_ITEMS):
                whi_of(i)
                if i > I_WQ:
                    q = i - 1 - I_WQ
                    act.wait_ge(s_item, i)
                    A(QT[:, q, :], PS[:, (i - 1) % 2, 0:T], ACT.Copy).then_inc(s_qev, 1)
            act.wait_ge(s_item, N_ITEMS)
            A(QT[:, 2 * PH - 1, :], PS[:, (N_ITEMS - 1) % 2, 0:T], ACT.Copy).then_inc(s_qev, 1)
            for k in range(12):
                act.wait_ge(s_scp, k + 1)
                A(scores[:, 512 * k:512 * k + 512], PS[:, 2 + k % 2, :], ACT.Copy).then_inc(s_scev, 1)

            def quarter(c, q, load):
                if q % 2 == 0:
                    act.wait_ge(s_hraw[q // 2 % 4], load)
                if not isinstance(c, int) or c >= 4:
                    act.wait_ge(s_up_mm, c - 3)
                A(hhiq[q % 4][:], hraw[q // 2 % 4][:, 256 * (q % 2):256 * (q % 2) + 256], ACT.Copy).then_inc(s_hhi2, 1)

            def gelu(e, slot):
                act.wait_ge(s_up_mm, e * 4 + 4)
                A(W[:, bass.ds(e, 1), :].rearrange("p a t -> p (a t)"), PS[:, slot % 4, 0:T], ACT.Gelu).then_inc(s_gelu, 1)

            act.wait_ge(s_out, 16 * (NQB + 6))
            for e in range(RIT):
                for x in range(4):
                    quarter(4 * e + x, 4 * e + x, 16 * (e // 2 + 1))
                if e:
                    gelu(e - 1, e - 1)

            def up_rest(k):
                for e in range(RIT):
                    for x in range(4):
                        quarter(k * 16 + (4 * e + x), 4 * e + x, k * 32 + 16 * (e // 2 + 1))
                    gelu(k * 4 + (e - 1), e - 1)

            with act.Fori(1, 3 * PH) as k:
                up_rest(k)
            act.wait_ge(s_gexp, 1)
            A(best[:], best[:], ACT.Exp).then_inc(s_gate, 1)
            act.wait_ge(s_pairs, 6)
            with act.Fori(3 * PH, NI // RIT) as k:
                up_rest(k)
            gelu(NI - 1, NI - 1)

            def gates(g_, slot, t0):
                act.wait_ge(s_ohr, g_ + 1)
                for x in range(4):
                    ins = A(ohB[:, slot, x, :], ohB[:, slot, x, :], ACT.Copy, scale=pairg[:, bass.ds(t0 + x, 1)])
                ins.then_inc(s_ohb, 1)

            for q in range(GIT):
                gates(q, q % 3, 4 * q)
            with act.Fori(1, T // (4 * GIT)) as k:
                for q in range(GIT):
                    gates(k * GIT + q, q % 3, k * (4 * GIT) + 4 * q)

            def down(e, s, load):
                if not isinstance(e, int) or e >= 2:
                    act.wait_ge(s_down, e * 2 - 2)
                A(Wh[s][:], W[:, bass.ds(e, 1), :].rearrange("p a t -> p (a t)"), ACT.Copy).then_inc(s_wh, 1)
                for b in range(2):
                    act.wait_ge(s_vraw[2 * s + b], load)
                    if not isinstance(e, int) or 2 * e + b >= 2:
                        act.wait_ge(s_down, e * 2 + (b - 1))
                    A(hhi[b][:], hraw[2 * s + b][:], ACT.Copy).then_inc(s_vhi, 1)

            act.wait_ge(s_w, T // 4)
            for e in range(2):
                down(e, e, 16)
            with act.Fori(1, NI // 2) as k:
                for e in range(2):
                    down(k * 2 + e, e, k * 16 + 16)
            norm_stats(3, XF, SQF, SDF, LN_EPS)

        @block.tensor
        def _(pe):
            mm = nc.tensor.matmul

            def mean_over_d(X, bank, c1):
                for k in range(KT):
                    ins = mm(PS[:, bank, 0:T], c1[:], X[:, k, :], start=(k == 0), stop=(k == KT - 1))
                return ins

            def norm(k, X, S, c1):
                mean_over_d(X, 0, c1).then_inc(s_mean, 1)
                pe.wait_ge(s_sq, k)
                mean_over_d(S, 1, c1).then_inc(s_var, 1)

            def three(out, whi_, wlo_, xhi, xlo, start, stop):
                mm(out, whi_, xhi, start=start, stop=False)
                mm(out, whi_, xlo, start=False, stop=False)
                return mm(out, wlo_, xhi, start=False, stop=stop)

            pe.wait_ge(s_x, 16)
            pe.wait_ge(s_onesg, 1)
            norm(1, xin, SQ0, ones)

            pe.wait_ge(s_small, 80)
            pe.wait_ge(s_ln, 1)
            for k in range(KT):
                ins = mm(PS[0:H, 2, 0:T], wfs[:, k, :], hT[:, k, :], start=(k == 0), stop=(k == KT - 1))
            ins.then_inc(s_f, 1)

            def item(i, xh, xl):
                pe.wait_ge(s_wlo, i + 1)
                w, v = whi[i % HIS], wlo[i % RAWS]
                for k in range(KT):
                    ins = three(PS[:, i % 2, 0:T], w[:, P * k:P * k + P], v[:, P * k:P * k + P], xh[:, k, :], xl[:, k, :],
                                k == 0, k == KT - 1)
                ins.then_inc(s_item, 1)

            def scores_of(s):
                kind, a, qb = UNITS[s]
                rows, keys, tiles = unit_shape(UNITS[s])
                solo = s == 0 or "s" in (kind, UNITS[s - 1][0])
                if s:
                    pe.wait_ge(s_exp, s if solo else s - 1) if (solo or s >= 2) else None
                if kind == "p":
                    out = PS[0:rows, 2 + s % 2, :]
                    mm(out[:, 0:keys], qx[:, a, QB * qb:QB * qb + rows], kx[:, a, 0:keys], start=True, stop=False)
                    mm(out[:, QB * qb:keys], ident[0:rows, 0:rows], amask[0:rows, 0:rows], start=False,
                       stop=True).then_inc(s_sc, 1)
                    return
                for e in range(2):
                    h, o_ = 2 * a + e, HD * e
                    mm(PS[o_:o_ + HD, 2, :], qx[:, h, TP:T], ckx[:, h, :], start=True, stop=True)
                    mm(PS[o_:o_ + HD, 3, 0:DEC], qx[:, h, TP:T], kx[:, h, TP:T], start=True, stop=False)
                    ins = mm(PS[o_:o_ + HD, 3, 0:DEC], ident[0:HD, 0:HD], amask[0:HD, 0:HD], start=False, stop=True)
                ins.then_inc(s_sc, 1)

            def transposes_of(u):
                kind = UNITS[u][0]
                rows, _, tiles = unit_shape(UNITS[u])
                pe.wait_ge(s_norm, u + 1)
                if u:
                    solo = "s" in (kind, UNITS[u - 1][0])
                    if solo or u >= 2:
                        pe.wait_ge(s_tev, u if solo else u - 1)
                b = 4 if kind == "s" else 4 + u % 2
                for i, (k0, w) in enumerate(tiles):
                    ins = nc.tensor.transpose(flat(PS, 512 * b + P * i, rows)[0:w], pr[0:rows, u % 2, k0:k0 + w],
                                              ident[0:rows, 0:rows])
                ins.then_inc(s_tr, 1)

            def values_of(u):
                kind, a, qb = UNITS[u]
                rows, _, tiles = unit_shape(UNITS[u])
                pe.wait_ge(s_tev, u + 1)
                if u >= 2:
                    pe.wait_ge(s_oev, u - 1)
                for e in range(2 if kind == "s" else 1):
                    h = 2 * a + e if kind == "s" else a
                    o_ = head(h)[1]
                    q0, qn = (HD * e, DEC) if kind == "s" else (0, rows)
                    for i, (k0, w) in enumerate(tiles):
                        v = (vs if kind == "s" else vp)[0:w, i, HD * h:HD * h + HD]
                        ins = mm(PS[o_:o_ + HD, 6 + u % 2, 0:qn], v, pt[0:w, u % 2, P * i + q0:P * i + q0 + qn],
                                 start=(i == 0), stop=(i == len(tiles) - 1))
                ins.then_inc(s_pv, 1)

            def attention(s):
                if s < NU:
                    scores_of(s)
                if 1 <= s <= NU:
                    transposes_of(s - 1)
                if s >= 2:
                    values_of(s - 2)

            pe.wait_ge(s_hlo, 1)
            V0 = [0, QB, 2 * QB, T - P]
            for i in range(V_ITEMS):
                pe.wait_ge(s_wlo, i + 1)
                for kk in range(2):
                    k = 2 * i + kk
                    for b, t0 in enumerate(V0):
                        w, v = whi[i % HIS][:, 512 * kk:512 * kk + 512], wlo[i % RAWS][:, 512 * kk:512 * kk + 512]
                        ins = three(PS[:, 4 + b, :], hTh[:, k, t0:t0 + P], hTl[:, k, t0:t0 + P], w, v,
                                    k == 0, k == KT - 1)
                ins.then_inc(s_item, 1)
            for i in range(I_K, I_WO):
                if i - I_K >= 2:
                    pe.wait_ge(s_pev, i - I_K - 1)
                item(i, hTh, hTl)
                if i == I_RW:
                    pe.wait_ge(s_negc, 3)
                    pe.wait_ge(s_vev, 4)
                    pe.wait_ge(s_pev, K_ITEMS + Q_ITEMS)
                if i >= I_RW:
                    attention(2 * (i - I_RW))
                    attention(2 * (i - I_RW) + 1)
            for s in range(2 * RW_TILES, NU + 2):
                attention(s)

            pe.wait_ge(s_tanh, 1)
            pe.wait_ge(s_pev, I_WO - I_K)
            for j in range(NJ):
                if j:
                    pe.wait_ge(s_loev, 2 * j - 1)
                mm(PS[:, 0, 0:TC], w2s[0:HD, P * j:P * j + P], xm[0:HD, 12, :], start=True, stop=True).then_inc(s_lora, 1)
                if j:
                    pe.wait_ge(s_loev, 2 * j)
                mm(PS[:, 1, 0:TC], w2s[HD:P, P * j:P * j + P], xm[HD:P, 12, :], start=True, stop=True).then_inc(s_lora, 1)
            pe.wait_ge(s_kksq, 1)
            pe.wait_ge(s_loev, 8)
            for b in range(3):
                ins = mm(PS[:, b, :], blk[:], flat(KH, 512 * b, 512), start=True, stop=True)
            ins.then_inc(s_n2, 1)
            pe.wait_ge(s_rk, 1)
            for b in range(3):
                ins = mm(PS[:, 3 + b, :], blk[:], flat(KK, 512 * b, 512), start=True, stop=True)
            ins.then_inc(s_bsum, 1)
            pe.wait_ge(s_tanh, 2)
            pe.wait_ge(s_oev, NU)
            for j in range(NJ):
                if j >= 2:
                    pe.wait_ge(s_ggev, j - 1)
                mm(PS[:, 6 + j % 2, 0:TC], g2s[:, P * j:P * j + P], xm[:, 13, :], start=True, stop=True).then_inc(s_sgate, 1)

            pe.wait_ge(s_ggev, NJ)
            for gi in range(NG):
                tok = slice(P * gi, P * gi + P)
                for k, src in enumerate(("v", "b", "k", "a")):
                    if k == 0:
                        pe.wait_ge(s_prep, 1)
                        if gi:
                            pe.wait_ge(s_zev, gi)
                    if k >= 2:
                        pe.wait_ge(s_natev, 4 * gi + k - 1)
                    if k == 1 and gi:
                        pe.wait_ge(s_yaev, gi)
                    for j in range(NJ):
                        t = {"v": xm[:, 8 + j, tok], "b": BH[:, j, tok], "k": KH[:, j, tok], "a": AR[:, j, gi, 0:P]}[src]
                        ins = nc.tensor.transpose(PS[:, 6 + k % 2, P * j:P * j + P], t, ident[:])
                    ins.then_inc(s_nat, 1)
                for hf in range(2):
                    if hf:
                        pe.wait_ge(s_Aev, 4 * gi + 2)
                    elif gi:
                        pe.wait_ge(s_stt, 2 * gi)
                        pe.wait_ge(s_yev, 2 * gi)
                    for x, src in enumerate((BH, KH)):
                        for hh in range(4):
                            h = 4 * hf + hh
                            j, o_ = head(h)
                            ins = mm(PS[:, 2 * x + hh % 2, 256 * (hh // 2):256 * (hh // 2) + 256], src[o_:o_ + HD, j, tok],
                                     AR[o_:o_ + HD, j, gi, :], start=True, stop=True)
                        ins.then_inc(s_A, 1)
                pe.wait_ge(s_Aev, 4 * gi + 4)
                pe.wait_ge(s_natev, 4 * gi + 4)
                for h in range(H):
                    ins = mm(PS[:, 6, HD * h:HD * h + HD], AK[:, h, 0:P], vN[:, h, :], start=True, stop=True)
                ins.then_inc(s_akv, 1)
                for hf in range(2):
                    pe.wait_ge(s_tt, 2 * gi + hf + 1)
                    for hh in range(4):
                        ins = nc.tensor.transpose(PS[:, 4 + hf, P * hh:P * hh + P], TT[:, 4 * hf + hh, :], ident[:])
                    ins.then_inc(s_tn, 1)
                for l in range(1, 6):
                    for hf in range(2):
                        n = 10 * gi + 2 * (l - 1) + hf
                        pe.wait_ge(s_nm, n + 1)
                        if l == 1:
                            pe.wait_ge(s_tnev, 2 * gi + hf + 1)
                        else:
                            pe.wait_ge(s_up, n - 1)
                        for hh in range(4):
                            ins = mm(PS[:, hf, P * hh:P * hh + P], Nm[:, hf, hh, :], Tn[:, 4 * hf + hh, :], start=True, stop=True)
                        ins.then_inc(s_lx, 1)
                    for hf in range(2):
                        n = 10 * gi + 2 * (l - 1) + hf
                        pe.wait_ge(s_xs, n + 1)
                        for hh in range(4):
                            h = 4 * hf + hh
                            if l < 5:
                                mm(PS[:, 2 + hf, P * hh:P * hh + P], TT[:, h, :], Xs[:, h, :], start=True, stop=True)
                            ins = mm(PS[:, 4 + hf, P * hh:P * hh + P], Xs[:, h, :], TT[:, h, :], start=True, stop=True)
                        ins.then_inc(s_ly, 1)
                pe.wait_ge(s_akvev, gi + 1)
                for hf in range(2):
                    pe.wait_ge(s_up, 10 * gi + 9 + hf)
                    for hh in range(4):
                        h = 4 * hf + hh
                        ins = mm(PS[:, hf, P * hh:P * hh + P], TT[:, h, :], AX[:, h, :], start=True, stop=True)
                    ins.then_inc(s_w1, 1)
                pe.wait_ge(s_w1ev, 2 * gi + 2)
                for h in range(H):
                    j, o_ = head(h)
                    ins = mm(PS[o_:o_ + HD, 2, P * j:P * j + P], X12[:, h, 0:HD], NR[:, h, P:2 * P], start=True, stop=True)
                ins.then_inc(s_y1, 1)
                for c in range(2):
                    r = slice(CH * c, CH * c + CH)
                    for h in range(H):
                        j, o_ = head(h)
                        ins = mm(PS[o_:o_ + HD, 3 + c, HD * j:HD * j + HD], X12[r, h, 0:HD], bN[r, h, :], start=True, stop=True)
                ins.then_inc(s_y1, 1)
                for c in range(2):
                    r = slice(CH * c, CH * c + CH)
                    for h in range(H):
                        j, o_ = head(h)
                        out = PS[o_:o_ + HD, 5 + c, HD * j:HD * j + HD]
                        mm(out, bN[r, h, :], X12[r, h, HD:P], start=True, stop=False)
                        ins = mm(out, kN[r, h, :], vN[r, h, :], start=False, stop=True)
                ins.then_inc(s_z, 1)
                for h in range(H):
                    j, o_ = head(h)
                    out = PS[o_:o_ + HD, 7, P * j:P * j + P]
                    mm(out, X12[:, h, HD:P], NR[:, h, P:2 * P], start=True, stop=False)
                    ins = mm(out, vN[:, h, :], AK[:, h, P:2 * P], start=False, stop=True)
                ins.then_inc(s_ya, 1)
                pe.wait_ge(s_y1ev, 2 * gi + 2)
                for c in range(2):
                    cc = 2 * gi + c
                    s_in = cc if cc < 5 else 6
                    if c:
                        pe.wait_ge(s_stt, cc)
                    for h in range(H):
                        j, o_ = head(h)
                        ins = mm(PS[o_:o_ + HD, c, HD * j:HD * j + HD], MT[o_:o_ + HD, c, j, :], states[o_:o_ + HD, s_in, j, :],
                                 start=True, stop=True)
                    ins.then_inc(s_ms, 1)
                    for h in range(H):
                        j, o_ = head(h)
                        ins = mm(PS[o_:o_ + HD, 2 + c, CH * j:CH * j + CH], states[o_:o_ + HD, s_in, j, :],
                                 Y1[o_:o_ + HD, j, CH * c:CH * c + CH], start=True, stop=True)
                    ins.then_inc(s_y, 1)

            pe.wait_ge(s_yev, 6)
            pe.wait_ge(s_stt, 6)
            for b in range(3):
                ins = mm(PS[:, b, :], blk[:], flat(SG, 512 * b, 512), start=True, stop=True)
            ins.then_inc(s_gm, 1)
            pe.wait_ge(s_gsq, 1)
            for b in range(3):
                ins = mm(PS[:, 3 + b, :], blk[:], flat(E1, 512 * b, 512), start=True, stop=True)
            ins.then_inc(s_gv, 1)
            pe.wait_ge(s_osq, 1)
            pe.wait_ge(s_gsd, 1)
            for j in range(NJ):
                ins = mm(PS[:, 4 + j, 0:T], blk[:], KH[:, j, 0:T], start=True, stop=True)
            ins.then_inc(s_ov, 1)

            pe.wait_ge(s_mxl, 1)
            for i in range(I_WO, I_WQ):
                if i - I_WO >= 2:
                    pe.wait_ge(s_wo, i - I_WO - 1)
                item(i, MXh, MXl)
            pe.wait_ge(s_wo, KT)
            norm(2, X1, SQ1, ones)

            pe.wait_ge(s_h1l, 1)
            for i in range(I_WQ, N_ITEMS):
                if i - I_WQ >= 2:
                    pe.wait_ge(s_qev, i - I_WQ - 1)
                item(i, H1h, H1l)
            pe.wait_ge(s_qev, 2 * PH)
            for tt, t0 in enumerate((0, P, T - P)):
                for k4 in range(4):
                    k = 4 * tt + k4
                    if k >= 2:
                        pe.wait_ge(s_scev, k - 1)
                    for x in range(4):
                        q = 4 * k4 + x
                        ins = mm(PS[:, 2 + k % 2, P * x:P * x + P], QT[:, q, t0:t0 + P], kst[:, q % 2, :], start=True, stop=True)
                    ins.then_inc(s_scp, 1)

            def up(e, slot):
                for x in range(4):
                    pe.wait_ge(s_hlo2, e * 4 + (x + 1))
                    if x == 0 and not (isinstance(e, int) and e < 4):
                        pe.wait_ge(s_gelu, e - 3)
                    lo_ = hlo[(2 * slot + x // 2) % 4]
                    for kk in range(2):
                        k = 2 * x + kk
                        ins = three(PS[:, slot % 4, 0:T], hhiq[x][:, P * kk:P * kk + P], lo_[:, P * (k % 4):P * (k % 4) + P],
                                    H1h[:, k, :], H1l[:, k, :], k == 0, k == KT - 1)
                    ins.then_inc(s_up_mm, 1)

            pe.wait_ge(s_scev, 12)
            for e in range(RIT):
                up(e, e)
            with pe.Fori(1, 3 * PH) as k:
                for e in range(RIT):
                    up(k * 4 + e, e)
            pe.wait_ge(s_routed, 1)
            pe.wait_ge(s_rconst, 1)
            for x, src in enumerate((sel1, sel2, best)):
                if x == 2:
                    pe.wait_ge(s_routed, 2)
                for tt in range(3):
                    ins = nc.tensor.transpose(PS[:, 4 + x, P * tt:P * tt + P],
                                              src[:, PH * tt:PH * tt + PH, :].rearrange("p h k -> p (h k)"), identb[:])
                ins.then_inc(s_pt, 1)
            with pe.Fori(3 * PH, NI // RIT) as k:
                for e in range(RIT):
                    up(k * 4 + e, e)

            def grid(g_, q):
                pe.wait_ge(s_oha, g_ + 1)
                pe.wait_ge(s_ohb, g_ + 1)
                if not isinstance(g_, int):
                    pe.wait_ge(s_w, g_ - (GIT - 1))
                for x in range(4):
                    ins = mm(PS[:, 2 + q, P * x:P * x + P], ohA[:, q % 3, x, :], ohB[:, q % 3, x, :], start=True, stop=True)
                ins.then_inc(s_grid, 1)

            pe.wait_ge(s_gelu, NI)
            for q in range(GIT):
                grid(q, q)
            with pe.Fori(1, T // (4 * GIT)) as k:
                for q in range(GIT):
                    grid(k * GIT + q, q)

            def down(e, s, start, stop):
                pe.wait_ge(s_wl, e + 1)
                for b in range(2):
                    pe.wait_ge(s_vlo, e * 2 + (b + 1))
                    for kk in range(4):
                        ins = three(PS[:, 4 * b + kk, 0:T], hhi[b][:, P * kk:P * kk + P], hlo[2 * s + b][:, P * kk:P * kk + P],
                                    Wh[s][:], Wl[s][:], start, stop)
                    ins.then_inc(s_down, 1)

            pe.wait_ge(s_w, T // 4)
            for e in range(2):
                down(e, e, e == 0, False)
            with pe.Fori(1, NI // 2 - 1) as k:
                for e in range(2):
                    down(k * 2 + e, e, False, False)
            for e in range(NI - 2, NI):
                down(e, e % 2, False, e == NI - 1)
            pe.wait_ge(s_xf, 1)
            pe.wait_ge(s_onesg, 2)
            norm(3, XF, SQF, ones2)

        @block.vector
        def _(dve):
            v = nc.vector
            n = [0]

            def own(ins):
                n[0] += 1
                ins.then_inc(s_dve, 1)
                dve.wait_ge(s_dve, n[0])

            def tt(out, a, b, op):
                return v.tensor_tensor(out, a, b, op)

            def norm(k, X, out, sd, g_, b_, done):
                dve.wait_ge(s_mean, k)
                tt(X[:], X[:], over(PS[:, 0, 0:T], KT), ALU.subtract).then_inc(s_xc, 1)
                dve.wait_ge(s_sd, k)
                own(v.reciprocal(sd[:], sd[:]))
                dve.wait_ge(s_xc, k)
                own(tt(X[:], X[:], over(sd[:], KT), ALU.mult))
                for j in range(KT):
                    ins = v.tensor_scalar(out[:, j, :], X[:, j, :], col(g_, j), col(b_, j), ALU.mult, ALU.add)
                ins.then_inc(done, 1)
                return ins

            def wlo_of(i):
                dve.wait_ge(s_whi, i + 1)
                tt(wlo[i % RAWS][:], raw[i % RAWS][:], whi[i % HIS][:].bitcast(F32), ALU.subtract).then_inc(s_wlo, 1)

            dve.wait_ge(s_cols, 16)
            norm(1, xin, hT, SD, "ln_in_g", "ln_in_b", s_ln)
            dve.wait_ge(s_ln, 1)
            dve.wait_ge(s_hhi, 1)
            tt(hTl[:], hT[:], hTh[:].bitcast(F32), ALU.subtract).then_inc(s_hlo, 1)
            dve.wait_ge(s_f, 1)
            own(v.tensor_scalar(lf[:, 0, :], PS[0:H, 2, 0:T], col("b_f", rows=H), None, ALU.add))
            v.scalar_tensor_tensor(lf[:, 1, :], lf[:, 0, :], -1.0, lf[:, 0, :], ALU.mult, ALU.max).then_inc(s_fz, 1)
            dve.wait_ge(s_fe, 1)
            v.scalar_tensor_tensor(lf[:, 2, :], lf[:, 0, :], 0.0, lf[:, 1, :], ALU.min, ALU.subtract).then_inc(s_logf, 1)
            def attention(s):
                if 1 <= s <= NU:
                    u = s - 1
                    rows, keys, _ = unit_shape(UNITS[u])
                    dve.wait_ge(s_exp, u + 1)
                    own(v.reciprocal(st[0:rows, u % 2, 3:4], st[0:rows, u % 2, 2:3]))
                    v.tensor_scalar(pr[0:rows, u % 2, 0:keys], pr[0:rows, u % 2, 0:keys], st[0:rows, u % 2, 3:4], None,
                                    ALU.mult).then_inc(s_norm, 1)
                if s < NU:
                    rows, keys, _ = unit_shape(UNITS[s])
                    dve.wait_ge(s_sc, s + 1)
                    b = 2 if UNITS[s][0] == "s" else 2 + s % 2
                    own(v.reduce_max(st[0:rows, s % 2, 0:1], flat(PS, 512 * b, keys)[0:rows], AX_X))
                    v.tensor_scalar(st[0:rows, s % 2, 1:2], st[0:rows, s % 2, 0:1], -1.0, None, ALU.mult).then_inc(s_max, 1)

            for i in range(I_WO):
                if i == 0:
                    wlo_of(0)
                if i + 1 < I_WO:
                    wlo_of(i + 1)
                if i == V_ITEMS - 1:
                    dve.wait_ge(s_logf, 1)
                    dve.wait_ge(s_const, 1)
                    dve.wait_ge(s_cache, 80)
                    own(v.tensor_copy(lfs[:, 0, PAST:KEYS], lf[:, 2, TP:T]))
                    v.tensor_tensor_scan(lf[:, 3, 0:TP], ones8[:, 0:TP], lf[:, 2, 0:TP], 0.0, ALU.mult, ALU.add)
                    v.tensor_tensor_scan(lfs[:, 1, :], ones8[:], lfs[:, 0, :], 0.0, ALU.mult, ALU.add).then_inc(s_logf, 1)
                if i >= I_RW:
                    r = i - I_RW
                    t = RW_ORDER[r]
                    dve.wait_ge(s_pev, i - I_K + 1)
                    s = pb[:, r % 3, :]
                    own(tt(xm[:, t, :], s[:, 0:TC], s[:, 1:TC + 1], ALU.subtract))
                    v.scalar_tensor_tensor(xm[:, t, :], xm[:, t, :], col("mix", t), s[:, 1:TC + 1], ALU.mult,
                                           ALU.add).then_inc(s_xm, 1)
                    if i == I_WO - 1:
                        dve.wait_ge(s_xm, RW_TILES)
                    attention(2 * r)
                    attention(2 * r + 1)
            for s in range(2 * RW_TILES, NU + 2):
                attention(s)

            r_, k_, v_ = xm[:, 0:NJ, :], xm[:, NJ:2 * NJ, :], xm[:, 2 * NJ:3 * NJ, :]
            own(v.memset(xm[:, 0:3 * NJ, TP:PADP], 0.0))
            dve.wait_ge(s_loev, 8)
            own(v.memset(SG[:, :, TP:PADP], 0.0))
            for j in range(NJ):
                ins = v.tensor_tensor_scan(LS[:, j, :], keep[:], SG[:, j, :], 0.0, ALU.mult, ALU.add)
            ins.then_inc(s_ls, 1)
            dve.wait_ge(s_ls, 1)
            tt(SG[:], LS[:], SG[:], ALU.subtract).then_inc(s_lprev, 1)
            for j in range(NJ):
                ins = v.tensor_scalar(BH[:, j, :], k_[:, j, :], col("k_k", j), None, ALU.mult)
            ins.then_inc(s_kkraw, 1)
            dve.wait_ge(s_d, 1)
            dve.wait_ge(s_pv, NU)
            dve.wait_ge(s_oev, NU)
            v.tensor_copy(DL[:], E1[:, :, CH - 1:TC:CH])
            for gi in range(NG):
                ins = tt(AR[:, :, gi, P:2 * P], r_[:, :, P * gi:P * gi + P], E1[:, :, P * gi:P * gi + P], ALU.mult)
            own(ins)
            for j in range(NJ):
                own(v.tensor_scalar(E1[:, j, :], AA[:, j, :], 1.0, col("k_a", j), ALU.subtract, ALU.mult))
            dve.wait_ge(s_n2, 1)
            v.tensor_scalar(KK[:].rearrange("p j t -> p (j t)"), flat(PS, 0, NJ * TC), float(HD), 1e-24, ALU.mult,
                            ALU.max).then_inc(s_n2m, 1)
            own(v.scalar_tensor_tensor(k_, E1[:], 1.0, k_, ALU.add, ALU.mult))
            dve.wait_ge(s_dprev, 1)
            dve.wait_ge(s_kkrt, 1)
            own(v.reciprocal(KK[:], KK[:]))
            own(tt(KK[:], BH[:], KK[:], ALU.mult))
            for gi in range(NG):
                t = slice(P * gi, P * gi + P)
                v.scalar_tensor_tensor(AR[:, :, gi, 0:P], KK[:, :, t], -1.0, SG[:, :, t], ALU.mult, ALU.mult)
            own(tt(BH[:], KK[:], AA[:], ALU.mult))
            own(tt(BH[:], BH[:], LS[:], ALU.mult))
            own(tt(KH[:], k_, LS[:], ALU.mult))
            for j in range(NJ):
                ins = v.scalar_tensor_tensor(KK[:, j, :], r_[:, j, :], col("r_k", j), k_[:, j, :], ALU.mult, ALU.mult)
            ins.then_inc(s_rk, 1)
            dve.wait_ge(s_bsum, 1)
            v.scalar_tensor_tensor(AA[:].rearrange("p j t -> p (j t)"), flat(PS, 3 * 512, NJ * TC), float(HD),
                                   v_.rearrange("p j t -> p (j t)"), ALU.mult, ALU.mult).then_inc(s_prep, 1)
            dve.wait_ge(s_prep, 1)
            dve.wait_ge(s_out, 16 * (NQB + 4))

            for gi in range(NG):
                for hf in range(2):
                    for x, dst in enumerate((NR, AK)):
                        dve.wait_ge(s_A, 4 * gi + 2 * hf + x + 1)
                        if gi and hf == 0 and x == 0:
                            dve.wait_ge(s_ya, gi)
                        for b in range(2):
                            h0 = 4 * hf + b
                            ins = tt(dst[:, h0:h0 + 3:2, :], PS[:, 2 * x + b, :].rearrange("p (h c) -> p h c", c=2 * P),
                                     over(causal[:], 2), ALU.mult)
                        ins.then_inc(s_Aev, 1)
                    dve.wait_ge(s_Aev, 4 * gi + 2 * hf + 1)
                    hs = slice(4 * hf, 4 * hf + 4)
                    own(tt(TT[:, hs, :], NR[:, hs, 0:P], over(lev[:, 0, :], 4), ALU.mult))
                    tt(TT[:, hs, :], TT[:, hs, :], over(ident[:], 4), ALU.add).then_inc(s_tt, 1)
                for l in range(1, 6):
                    for hf in range(2):
                        hs = slice(4 * hf, 4 * hf + 4)
                        dve.wait_ge(s_ly, 10 * gi + 2 * (l - 1) + hf + 1)
                        if l == 1:
                            dve.wait_ge(s_tt, 2 * gi + hf + 1)
                            dve.wait_ge(s_tnev, 2 * gi + hf + 1)
                        if l < 5:
                            tt(Tn[:, hs, :], Tn[:, hs, :], PS[:, 2 + hf, :].rearrange("p (h c) -> p h c", c=P), ALU.add)
                        tt(TT[:, hs, :], TT[:, hs, :], PS[:, 4 + hf, :].rearrange("p (h c) -> p h c", c=P),
                           ALU.add).then_inc(s_up, 1)
                    if l < 5:
                        dve.wait_ge(s_up, 10 * gi + 2 * l)

                dve.wait_ge(s_y1, 2 * gi + 1)
                tt(Y1[:], PS[:, 2, :].rearrange("p (j t) -> p j t", j=NJ), AR[:, :, gi, P:2 * P], ALU.add).then_inc(s_y1ev, 1)
                dve.wait_ge(s_y1, 2 * gi + 2)
                for c in range(2):
                    ins = tt(MT[:, c, :, :], PS[:, 3 + c, 0:NJ * HD].rearrange("p (j k) -> p j k", k=HD), over(eye2[:], NJ),
                             ALU.add)
                ins.then_inc(s_y1ev, 1)
                dve.wait_ge(s_z, gi + 1)
                for c in range(2):
                    ins = tt(Zs[:, c, :, :], PS[:, 5 + c, 0:NJ * HD].rearrange("p (j v) -> p j v", j=NJ),
                             along(DL[:, :, 2 * gi + c], HD), ALU.mult)
                ins.then_inc(s_zev, 1)
                dve.wait_ge(s_zev, gi + 1)
                dve.wait_ge(s_yaev, gi + 1)
                for c in range(2):
                    cc = 2 * gi + c
                    s_to = cc + 1 if cc < 5 else 7
                    dve.wait_ge(s_ms, cc + 1)
                    own(tt(states[:, s_to, :, :], PS[:, c, 0:NJ * HD].rearrange("p (j v) -> p j v", j=NJ),
                           along(DL[:, :, cc], HD), ALU.mult))
                    tt(states[:, s_to, :, :], states[:, s_to, :, :], Zs[:, c, :, :], ALU.add).then_inc(s_stt, 1)
                    dve.wait_ge(s_y, cc + 1)
                    y = SG[:, :, CH * cc:CH * cc + CH]
                    tt(y, y, PS[:, 2 + c, 0:NJ * CH].rearrange("p (j t) -> p j t", j=NJ), ALU.add).then_inc(s_yev, 1)

            dve.wait_ge(s_gm, 1)
            dve.wait_ge(s_yev, 6)
            tt(SG[:].rearrange("p j t -> p (j t)"), SG[:].rearrange("p j t -> p (j t)"), flat(PS, 0, NJ * TC),
               ALU.subtract).then_inc(s_gc, 1)
            dve.wait_ge(s_gsd, 1)
            dve.wait_ge(s_gc, 1)
            own(v.reciprocal(KK[:], KK[:]))
            own(tt(SG[:], SG[:], KK[:], ALU.mult))
            for j in range(NJ):
                own(v.tensor_scalar(SG[:, j, :], SG[:, j, :], col("lnx_g", j), col("lnx_b", j), ALU.mult, ALU.add))
            own(tt(SG[:], SG[:], AA[:], ALU.add))
            tt(MX[:, 0:NJ, 0:TP], SG[:, :, 0:TP], xm[:, 0:NJ, 0:TP], ALU.mult)
            tt(MX[:, 0:NJ, TP:T], SG[:, :, PADP:TC], xm[:, 0:NJ, PADP:TC], ALU.mult)
            dve.wait_ge(s_osd, 1)
            own(v.reciprocal(BH[:, :, 0:T], BH[:, :, 0:T]))
            own(tt(oT[:], oT[:], BH[:, :, 0:T], ALU.mult))
            for j in range(NJ):
                ins = v.tensor_scalar(MX[:, NJ + j, :], oT[:, j, :], col("fnorm", j), None, ALU.mult)
            ins.then_inc(s_mx, 1)
            dve.wait_ge(s_mx, 1)
            dve.wait_ge(s_mxh, 1)
            tt(MXl[:], MX[:], MXh[:].bitcast(F32), ALU.subtract).then_inc(s_mxl, 1)

            wlo_of(I_WO)
            for i in range(I_WO, I_WQ):
                if i + 1 < I_WQ:
                    wlo_of(i + 1)
                dve.wait_ge(s_item, i + 1)
                v.scalar_tensor_tensor(X1[:, i - I_WO, :], hT[:, i - I_WO, :], ALPHA, PS[:, i % 2, 0:T], ALU.mult,
                                       ALU.add).then_inc(s_wo, 1)
            dve.wait_ge(s_wo, KT)
            norm(2, X1, X1, SD, "ln1_g", "ln1_b", s_ln)
            dve.wait_ge(s_ln, 2)
            dve.wait_ge(s_h1h, 1)
            tt(H1l[:], X1[:], H1h[:].bitcast(F32), ALU.subtract).then_inc(s_h1l, 1)
            for i in range(I_WQ, N_ITEMS):
                wlo_of(i)

            def route(k, part):
                if part == 0 or part == 1:
                    tk, ix, knock = ((top1, ix1, knock1), (top2, ix2, knock2))[part]
                    s = unit_s[:, part * NK:part * NK + NK]
                    if part == 0:
                        step(v.tensor_copy(unit_s[:], scores[:, bass.ds(k * (2 * NK), 2 * NK)]))
                    step(v.max(tk[:, 0:8], s))
                    step(v.max_index(ix[:, 0:8], tk[:, 0:8], s))
                    step(v.match_replace(knock[:], tk[:, 0:8], s, LOW))
                elif part == 2 or part == 3:
                    tk, ix, knock, ixf = ((top1, ix1, knock1, ix1f), (top2, ix2, knock2, ix2f))[part - 2]
                    step(v.max(tk[:, 8:16], knock[:]))
                    step(v.max_index(ix[:, 8:16], tk[:, 8:16], knock[:]))
                    step(v.tensor_copy(ixf[:], ix[:]))
                elif part == 4:
                    step(tt(cand[:], along(top1[:], 16), over(top2[:], 16), ALU.add))
                    c = cand[:].rearrange("p a b -> p (a b)")
                    step(v.max(top[:, 0:8], c))
                    step(v.max_index(pos[:, 0:8], top[:, 0:8], c))
                elif part == 5:
                    c, ck = (t[:].rearrange("p a b -> p (a b)") for t in (cand, candk))
                    step(v.match_replace(ck, top[:, 0:8], c, LOW))
                    step(v.max(top[:, 8:16], ck))
                    step(v.max_index(pos[:, 8:16], top[:, 8:16], ck))
                    step(v.tensor_copy(bestk(best, k), top[:]))
                elif part == 6:
                    step(v.tensor_scalar(posh[:], pos[:], 4, None, ALU.logical_shift_right))
                    step(v.tensor_scalar(posl[:], pos[:], 15, None, ALU.bitwise_and))
                    step(v.tensor_copy(poshf[:], posh[:]))
                    step(v.tensor_copy(poslf[:], posl[:]))
                    step(tt(hit1[:], iota16[:], along(poshf[:], 16), ALU.is_equal))
                    step(tt(hit2[:], iota16[:], along(poslf[:], 16), ALU.is_equal))
                else:
                    step(tt(hit1[:], hit1[:], over(ix1f[:], 16), ALU.mult))
                    step(tt(hit2[:], hit2[:], over(ix2f[:], 16), ALU.mult))
                    step(v.tensor_reduce(bestk(sel1, k), hit1[:], AX_X, ALU.add))
                    step(v.tensor_reduce(bestk(sel2, k), hit2[:], AX_X, ALU.add))

            def bestk(t, k):
                return t[:].rearrange("p u k -> p (u k)")[:, bass.ds(k * 16, 16)]

            def step(ins):
                dve.drain()

            dve.wait_ge(s_scev, 12)
            dve.wait_ge(s_rconst, 1)
            with dve.Fori(0, 3 * PH) as k:
                for part in range(8):
                    route(k, part)
            v.tensor_copy(gsum[:], best[:, :, 0]).then_inc(s_routed, 1)
            dve.wait_ge(s_routed, 1)
            tt(best[:], best[:], along(gsum[:], 16), ALU.subtract).then_inc(s_gexp, 1)
            dve.wait_ge(s_gate, 1)
            own(v.tensor_reduce(gsum[:], best[:], AX_X, ALU.add))
            own(v.reciprocal(gsum[:], gsum[:]))
            tt(best[:], best[:], along(gsum[:], 16), ALU.mult).then_inc(s_routed, 1)
            for x, dst in enumerate((pair1, pair2, pairg)):
                dve.wait_ge(s_pt, x + 1)
                v.tensor_copy(dst[:, 0:2 * P], PS[:, 4 + x, 0:2 * P]).then_inc(s_pairs, 1)
                v.tensor_copy(dst[:, 2 * P:T], PS[:, 4 + x, 2 * P + 3 * P - T:3 * P]).then_inc(s_pairs, 1)

            def one_hots(g_, slot, tok):
                if g_ is not None:
                    dve.wait_ge(s_grid, g_)
                tt(ohB[:, slot, :, :], over(iotak[:], 4), along(pair2[:, tok], NK), ALU.is_equal).then_inc(s_ohr, 1)
                tt(ohA[:, slot, :, :], over(iotak[:], 4), along(pair1[:, tok], NK), ALU.is_equal).then_inc(s_oha, 1)

            def weigh(g_, q, tok):
                dve.wait_ge(s_grid, g_ + 1)
                w = W[:, :, tok].rearrange("p e t -> p t e")
                tt(w, PS[:, 2 + q % GIT, :].rearrange("p (t e) -> p t e", e=NI), w, ALU.mult).then_inc(s_w, 1)

            dve.wait_ge(s_up_mm, 4 * NI)
            dve.wait_ge(s_pairs, 6)
            dve.wait_ge(s_gelu, NI)
            for q in range(GIT):
                one_hots(q - 2 if q >= 3 else None, q % 3, bass.ds(4 * q, 4))
                if q >= 2:
                    weigh(q - 2, q - 2, bass.ds(4 * q - 8, 4))
            with dve.Fori(1, T // (4 * GIT)) as k:
                for q in range(GIT):
                    one_hots(k * GIT + (q - 2), q % 3, bass.ds(k * (4 * GIT) + 4 * q, 4))
                    weigh(k * GIT + (q - 2), q - 2, bass.ds(k * (4 * GIT) + (4 * q - 8), 4))
            for q in (-2, -1):
                weigh(T // 4 + q, q, bass.ds(T + 4 * q, 4))

            def down(e, s):
                dve.wait_ge(s_wh, e + 1)
                tt(Wl[s][:], W[:, bass.ds(e, 1), :].rearrange("p a t -> p (a t)"), Wh[s][:].bitcast(F32),
                   ALU.subtract).then_inc(s_wl, 1)
                for b in range(2):
                    dve.wait_ge(s_vhi, e * 2 + (b + 1))
                    tt(hlo[2 * s + b][:], hraw[2 * s + b][:], hhi[b][:].bitcast(F32), ALU.subtract).then_inc(s_vlo, 1)

            dve.wait_ge(s_w, T // 4)
            for e in range(2):
                down(e, e)
            with dve.Fori(1, NI // 2) as k:
                for e in range(2):
                    down(k * 2 + e, e)

            dve.wait_ge(s_down, 2 * NI)
            own(tt(XF[:], H1h[:].bitcast(F32), H1l[:].bitcast(F32), ALU.add))
            v.scalar_tensor_tensor(XF[:], XF[:], ALPHA, PS[:, :, 0:T], ALU.mult, ALU.add).then_inc(s_xf, 1)
            dve.wait_ge(s_xf, 1)
            norm(3, XF, XF, SDF, "ln2_g", "ln2_b", s_xf)


def kernel(**inputs):
    from concourse import bacc as _bacc
    from concourse.bass_utils import run_bass_kernel_spmd as _run

    a = {n: np.asarray(x) for n, x in inputs.items()}
    DR = H * HD
    RW = RW_TILES * P

    def tile(w, c):
        return w[:, c:c + P].reshape(KT, P, P).transpose(1, 0, 2).reshape(P, D)

    x = np.concatenate([a["meta_tokens"], a["x_prompt"][0], a["x_sample"][0]])
    w_in, w_out, w_q = a["w_in"][0], a["w_out"][0], a["peer_w_q"][0]
    wv = w_in[:, RW + 2 * DR:RW + 3 * DR]
    items = [wv[2 * P * i:2 * P * i + 2 * P].reshape(2, P, DR).transpose(1, 0, 2).reshape(P, D) for i in range(V_ITEMS)]
    items += [tile(w_in, RW + DR + P * j) for j in range(NJ)]
    items += [tile(w_in, RW + P * j) for j in range(NJ)]
    items += [tile(w_in, P * t) for t in RW_ORDER]
    items += [tile(w_out, P * t) for t in range(KT)]
    items += [tile(w_q, P * t) for t in range(2 * PH)]
    vectors = {"ln_in_g": a["ln_in_g"], "ln_in_b": a["ln_in_b"], "ln1_g": a["ln1_g"], "ln1_b": a["ln1_b"],
               "ln2_g": a["ln2_g"], "ln2_b": a["ln2_b"], "mix": a["rwkv_mix"], "w0": a["rwkv_w0"], "a0": a["rwkv_a0"],
               "k_k": a["rwkv_k_k"], "k_a": a["rwkv_k_a"], "r_k": a["rwkv_r_k"], "lnx_g": a["rwkv_lnx_g"],
               "lnx_b": a["rwkv_lnx_b"], "fnorm": a["fox_norm_g"], "shift": a["state_rwkv_shift"],
               "b_f": np.pad(a["fox_b_f"].reshape(-1), (0, P - H))}
    cols = np.concatenate([vectors[n].reshape(-1, P).T for n in COLS], axis=1)
    ins = {
        "xT": x.reshape(T, KT, P).transpose(2, 1, 0),
        "cols": cols,
        "wbig": np.stack(items),
        "wf": w_in[:, RW + 3 * DR:].reshape(KT, P, H).transpose(1, 0, 2),
        "w2a2": np.concatenate([a["rwkv_w2"][0], a["rwkv_a2"][0]]),
        "g2": a["rwkv_g2"][0],
        "keysT": np.stack([a["peer_keys1"][0].T, a["peer_keys2"][0].T], axis=1),
        "ckT": a["cache_fox_k"][0, 0].transpose(2, 1, 0),
        "cv": a["cache_fox_v"][0, 0].reshape(PAST, DR),
        "clf": a["cache_fox_logf"][0, 0].T,
        "s0T": a["state_rwkv_wkv"][0, 0].reshape(NJ, 2, HD, HD).transpose(1, 3, 0, 2).reshape(P, NJ, HD),
        "uT": a["peer_u"][0].reshape(NK, NK, 2, 4, P).transpose(1, 2, 4, 3, 0).reshape(2 * NK, P, 512),
        "vE": a["peer_v"][0].reshape(NK, NK, 2, 512).transpose(1, 2, 0, 3).reshape(2 * NK, P, 512),
    }
    outs = {"yT": (P, KT, T), "wkvo": (P, 2, NJ, HD), "ko": (HD, H, T), "vpo": (TP, DR), "vso": (DEC, DR),
            "lfo": (H, T), "sho": (P, RW_TILES, 2)}
    nc = _bacc.Bacc("TRN2", target_bir_lowering=False, num_devices=1)
    arrays, args = {}, []
    for name, arr in ins.items():
        arrays[f"in_{name}"] = np.ascontiguousarray(arr)
        args.append(nc.dram_tensor(f"in_{name}", arr.shape, mybir.dt.from_np(arr.dtype), kind="ExternalInput").ap())
    for name, shape in outs.items():
        args.append(nc.dram_tensor(f"out_{name}", shape, F32, kind="ExternalOutput").ap())
    build(nc, *args)
    r = _run(nc, [arrays], core_ids=[0]).results[0]
    o = {n: np.asarray(r[f"out_{n}"]) for n in outs}

    y = o["yT"].transpose(2, 1, 0).reshape(T, D)
    sh = o["sho"].transpose(2, 1, 0).reshape(2, RW)
    wkv = o["wkvo"].reshape(2, HD, 2, NJ, HD).transpose(2, 3, 0, 4, 1).reshape(2, H, HD, HD)
    k = o["ko"].transpose(2, 1, 0)
    lf = o["lfo"].T
    one = (1, 1)
    return (y[N_META:TP].reshape(1, SEQ, D), y[TP:].reshape(1, DEC, D),
            sh[0].reshape(*one, 1, RW), wkv[0].reshape(*one, H, HD, HD), k[:TP].reshape(*one, TP, H, HD),
            o["vpo"].reshape(*one, TP, H, HD), lf[:TP].reshape(*one, TP, H),
            sh[1].reshape(*one, 1, RW), wkv[1].reshape(*one, H, HD, HD), k[TP:].reshape(*one, DEC, H, HD),
            o["vso"].reshape(*one, DEC, H, HD), lf[TP:].reshape(*one, DEC, H))
```

```python
from contextlib import ExitStack

import numpy as np

import concourse.bass as bass
from concourse import mybir

ALU = mybir.AluOpType
ACT = mybir.ActivationFunctionType
AX_X = mybir.AxisListType.X
F32 = mybir.dt.float32
F32R = mybir.dt.float32r
U32 = mybir.dt.uint32

P = 128
D = 1024
KT = D // P
N_META, SEQ, DEC, PAST = 16, 256, 64, 512
TP = N_META + SEQ
T = TP + DEC
H, HD = 8, 64
NJ = H * HD // P
RW_TILES = 14
CH = 64
PADP = -(-TP // CH) * CH
TC = PADP + DEC
NG = TC // P
QB = 96
NQB = -(-TP // QB)
KEYS = PAST + DEC
MEAN_BANK, VAR_BANK = 2, 3
NORM_ORDER = [list(range(KT)), list(range(KT)), [2, 3, 0, 1, 4, 5, 6, 7]]
KX = HD + H
NK = 128
XQ = 4
PH, TOPK = 8, 16
ALPHA = 2.0 ** 0.25
LN_EPS = 1e-5
LNX_EPS = 64e-5
NEG = -1.0e30
NI = NK
RIT = 4
GIT = 6
LOW = -3.0e38
CDEC = -float(np.exp(-0.5))

COLS = {}
_n = 0
for _name, _w in (("ln_in_g", 8), ("ln_in_b", 8), ("ln1_g", 8), ("ln1_b", 8), ("ln2_g", 8), ("ln2_b", 8),
                  ("mix", 14), ("w0", 4), ("a0", 4), ("k_k", 4), ("k_a", 4), ("r_k", 4), ("lnx_g", 4),
                  ("lnx_b", 4), ("fnorm", 4), ("shift", 14), ("b_f", 1)):
    COLS[_name] = _n
    _n += _w
NCOL = _n

V_ITEMS, K_ITEMS, Q_ITEMS = 4, NJ, NJ
RW_ORDER = [12, 13, 4, 5, 6, 7, 0, 1, 2, 3, 8, 9, 10, 11]
I_K = V_ITEMS
I_Q = I_K + K_ITEMS
I_RW = I_Q + Q_ITEMS
I_WO = I_RW + RW_TILES
I_WQ = I_WO + KT
N_ITEMS = I_WQ + 2 * PH
RAWS, HIS = 3, 2
POOL_ITEMS = range(I_RW, I_WO + 2)

PROMPT_UNITS = [("p", h, b) for h in range(H) for b in range(NQB)]
UNITS = PROMPT_UNITS[:12] + [("s", 0, 0), ("s", 1, 0)] + PROMPT_UNITS[12:] + [("s", 2, 0), ("s", 3, 0)]
NU = len(UNITS)

FILL = ["G0", "G1", "F0", "G2", "F1", "G3", "M0", "B0", "B1", "B2", "V0", "M1", "F2", "V1", "F3"]


def taken(f):
    act = FILL[f][0] in "GVF"
    return act, sum((x[0] in "GVF") == act for x in FILL[:f + 1])


def kind_of(f):
    return (FILL[f][0], int(FILL[f][1])) if 0 <= f < len(FILL) else ("", 0)


def hi_count(f):
    when = sorted((g + (1 if x[0] == "F" else 2), x[0] == "V", g) for g, x in enumerate(FILL) if x[0] in "VF")
    return [g for _, _, g in when].index(f) + 1


def chunk_tokens(g):
    if g < NG - 1:
        return [(P * g, P * g, P)]
    return [(P * g, P * g, TP - P * g), (PADP, TP, DEC)]


def unit_shape(u):
    kind, a, b = u
    if kind == "s":
        return P, KEYS, [(0, 64)] + [(64 + P * i, P) for i in range(4)]
    rows = min(QB, TP - QB * b)
    tiles = [(QB * i, min(QB, TP - QB * i)) for i in range(b + 1)]
    return rows, sum(n for _, n in tiles), tiles


def build(nc, xT, cols, wbig, wf, w2a2, g2, keysT, ckT, cv, clf, s0T, uT, vE,
          yT, wkvo, ko, vpo, vso, lfo, sho):
    ctx = ExitStack()
    with ctx:
        BASE, SBUF_END = 16512, 229368
        MAIN = P * T * 4
        TAIL = BASE + MAIN

        def at(name, shape, off, dt=F32):
            return nc.alloc_sbuf_tensor_at(name, list(shape), dt, offset=off)

        class Region:

            def __init__(self, start, end):
                self.pos, self.end = start, end

            def put(self, name, shape, dt=F32):
                n = int(np.prod(shape[1:])) * 4
                n = -(-n // 32) * 32
                t = at(name, shape, self.pos, dt)
                self.pos += n
                assert self.pos <= self.end, (name, self.pos - self.end)
                return t

        def sem(name):
            return ctx.enter_context(nc.semaphore(name))

        tail = Region(TAIL, SBUF_END)
        colv = tail.put("colv", [P, NCOL])
        H1h = tail.put("H1h", [P, KT, T], F32R)
        h1l_at = tail.pos
        H1l = tail.put("H1l", [P, KT, T], F32R)
        H1s = at("H1s", [P, KT, T], h1l_at)
        ring_at = tail.pos
        hraw = [tail.put(f"hraw{i}", [P, 512]) for i in range(4)]
        hlo = [at(f"hlo{i}", [P, 512], ring_at + 2048 * i, F32R) for i in range(4)]
        hhi_at = tail.pos
        hhi = [tail.put(f"hhi{i}", [P, 512], F32R) for i in range(2)]
        hhiq = [at(f"hhiq{i}", [P, 256], hhi_at + 1024 * i, F32R) for i in range(4)]
        pairs_at = tail.pos
        pair1 = tail.put("pair1", [P, T])
        pair2 = tail.put("pair2", [P, T])
        pairg = tail.put("pairg", [P, T])
        iotak = tail.put("iotak", [P, NK])
        one_hots = Region(ring_at, pairs_at)
        ohA = one_hots.put("ohA", [P, 3, 4, NK])
        ohB = one_hots.put("ohB", [P, 3, 4, NK])
        wsplit = Region(pairs_at, SBUF_END)
        Wh = [wsplit.put(f"Wh{i}", [P, T], F32R) for i in range(2)]
        Wl = [wsplit.put(f"Wl{i}", [P, T], F32R) for i in range(2)]

        W = at("W", [P, NI, T], BASE)
        routing = Region(BASE + 96 * T * 4, TAIL)
        scores = routing.put("scores", [P, 3 * 2 * PH * NK])
        top1 = routing.put("top1", [P, 16])
        top2 = routing.put("top2", [P, 16])
        ix1 = routing.put("ix1", [P, 16], U32)
        ix2 = routing.put("ix2", [P, 16], U32)
        ix1f = routing.put("ix1f", [P, 16])
        ix2f = routing.put("ix2f", [P, 16])
        knock1 = routing.put("knock1", [P, NK])
        knock2 = routing.put("knock2", [P, NK])
        cand = routing.put("cand", [P, 16, 16])
        candk = routing.put("candk", [P, 16, 16])
        pos = routing.put("pos", [P, 16], U32)
        posh = routing.put("posh", [P, 16], U32)
        posl = routing.put("posl", [P, 16], U32)
        poshf = routing.put("poshf", [P, 16])
        poslf = routing.put("poslf", [P, 16])
        hit1 = routing.put("hit1", [P, 16, 16])
        hit2 = routing.put("hit2", [P, 16, 16])
        iota16 = routing.put("iota16", [P, 16, 16])
        best = routing.put("best", [P, 3 * PH, 16])
        sel1 = routing.put("sel1", [P, 3 * PH, 16])
        sel2 = routing.put("sel2", [P, 3 * PH, 16])
        gsum = routing.put("gsum", [P, 3 * PH])
        identb = routing.put("identb", [P, P])
        unit_s = routing.put("unit_s", [P, 2 * NK])
        top = routing.put("top", [P, 16])
        last = Region(BASE, TAIL)
        ones2 = last.put("ones2", [P, P])
        XF = last.put("XF", [P, KT, T])
        SQF = last.put("SQF", [P, KT, T])
        SDF = last.put("SDF", [P, T])

        m = Region(BASE, TAIL)
        ident = m.put("ident", [P, P])
        ones = m.put("ones", [P, P])
        blk = m.put("blk", [P, P])
        causal = m.put("causal", [P, 2 * P])
        lev = m.put("lev", [P, 6, P])
        eye2 = m.put("eye2", [P, HD])
        amask = m.put("amask", [P, P])
        keep = m.put("keep", [P, TC])
        ones8_at = m.pos
        ones8 = m.put("ones8", [H, KEYS])
        w2s_at = m.pos
        w2s = m.put("w2s", [P, NJ * P])
        g2s = m.put("g2s", [P, NJ * P])
        wfl = at("wfl", [P, KT * H], m.pos, F32R)
        wfs = m.put("wfs", [P, KT * H])
        wfh = m.put("wfh", [P, KT * H], F32R)
        kst = m.put("kst", [P, 2, NK])
        hT = m.put("hT", [P, KT, T])
        xm = m.put("xm", [P, RW_TILES, TC])
        shs = m.put("shs", [P, RW_TILES, 2])
        states = m.put("states", [P, 8, NJ, HD])
        oT = m.put("oT", [P, NJ, T])
        SD = m.put("SD", [P, T])
        DL = m.put("DL", [P, NJ, TC // CH])
        att_at = m.pos
        lf = m.put("lf", [H, 4, T])
        lfs = m.put("lfs", [H, 2, KEYS])
        qx = m.put("qx", [KX, H, T])
        kx = m.put("kx", [KX, H, T])
        ckx = m.put("ckx", [KX, H, PAST])
        vp = m.put("vp", [P, NQB, H * HD])
        vs = m.put("vs", [P, 5, H * HD])
        pr = m.put("pr", [P, 2, KEYS])
        pt = m.put("pt", [P, 2, 5 * P])
        st = m.put("st", [P, 2, 4])
        att_end = m.pos
        xin = at("xin", [P, KT, T], att_at + 3 * 8192)
        SQ0 = at("SQ0", [P, KT, T], att_at + 3 * 8192 + 10752)
        g = Region(att_at, att_end)
        NR = g.put("NR", [P, H, 2 * P])
        AK = g.put("AK", [P, H, 2 * P])
        Tn = g.put("Tn", [P, H, P])
        TT = g.put("TT", [P, H, P])
        Xs = g.put("Xs", [P, H, P])
        Nm = g.put("Nm", [P, 2, H // 2, P])
        AX = g.put("AX", [P, H, P])
        X12 = g.put("X12", [P, H, P])
        bN = g.put("bN", [P, H, HD])
        kN = g.put("kN", [P, H, HD])
        vN = g.put("vN", [P, H, HD])
        Y1 = g.put("Y1", [P, NJ, P])
        MT = g.put("MT", [P, 2, NJ, HD])
        MXh = g.put("MXh", [P, KT, T], F32R)
        MXl = g.put("MXl", [P, KT, T], F32R)
        QT = at("QT", [P, 2 * PH, T], att_at)
        o = Region(att_at + 2 * PH * T * 4, att_end)
        X1 = o.put("X1", [P, KT, T])
        SQ1 = o.put("SQ1", [P, KT, T])
        assert o.pos <= g.pos - 2 * KT * T * 4
        wring_at = m.pos
        raw = [m.put(f"wraw{i}", [P, D]) for i in range(RAWS)]
        wlo = [at(f"wlo{i}", [P, D], wring_at + 4096 * i, F32R) for i in range(RAWS)]
        whi = [m.put(f"whi{i}", [P, D], F32R) for i in range(HIS)]
        AA = m.put("AA", [P, NJ, TC])
        Zs = at("Zs", [P, 2, NJ, HD], m.pos)
        pb = m.put("pb", [P, 3, TC + 1])
        BH = [m.put("BH0", [P, TC]), m.put("BH1", [P, TC]), at("BH2", [P, TC], w2s_at), at("BH3", [P, TC], ones8_at)]
        hTh = at("hTh", [P, KT, T], TAIL + 448, F32R)
        hTl = at("hTl", [P, KT, T], TAIL + 448 + KT * T * 4, F32R)
        sq = Region(TAIL + 448, TAIL + 448 + 2 * KT * T * 4)
        FSQ = sq.put("FSQ", [P, NJ, T])
        GSQ = sq.put("GSQ", [P, NJ, P])
        GSD = sq.put("GSD", [P, NJ, P])
        r2 = Region(sq.end, SBUF_END)
        AR = r2.put("AR", [P, 2, NJ, TC])
        LS = r2.put("LS", [P, NJ, TC])
        PS = ctx.enter_context(nc.psum_tensor("PS", [P, 8, 512], F32))

        s_cols, s_small, s_cache, s_out = (sem(x) for x in ("s_cols", "s_small", "s_cache", "s_out"))
        s_x = [sem(f"s_x{i}") for i in range(XQ)]
        s_shift, s_state = sem("s_shift"), sem("s_state")
        s_raw = [sem(f"s_raw{i}") for i in range(RAWS)]
        s_whi, s_wlo, s_wlo_pool, s_item = (sem(x) for x in ("s_whi", "s_wlo", "s_wlo_pool", "s_item"))
        s_pool, s_dve, s_act = sem("s_pool"), sem("s_dve"), sem("s_act")
        s_const, s_onesg = sem("s_const"), sem("s_onesg")
        s_mean, s_xc, s_sq, s_var, s_sd, s_ln = (sem(x) for x in ("s_mean", "s_xc", "s_sq", "s_var", "s_sd", "s_ln"))
        s_hhi, s_hlo = sem("s_hhi"), sem("s_hlo")
        s_f, s_fz, s_fe, s_logf, s_negc = (sem(x) for x in ("s_f", "s_fz", "s_fe", "s_logf", "s_negc"))
        s_vev, s_pev, s_xm = sem("s_vev"), sem("s_pev"), sem("s_xm")
        s_sc, s_max, s_exp, s_norm, s_tr, s_tev, s_pv, s_oev = (
            sem(x) for x in ("s_sc", "s_max", "s_exp", "s_norm", "s_tr", "s_tev", "s_pv", "s_oev"))
        s_tanh, s_lora, s_loev = (sem(x) for x in ("s_tanh", "s_lora", "s_loev"))
        s_ls, s_d, s_lprev, s_dprev, s_kksq, s_n2, s_n2m, s_rn, s_kkrt, s_prep = (
            sem(x) for x in ("s_ls", "s_d", "s_lprev", "s_dprev", "s_kksq", "s_n2", "s_n2m", "s_rn", "s_kkrt", "s_prep"))
        s_fill, s_fill_act, s_fill_dve = (sem(x) for x in ("s_fill", "s_fill_act", "s_fill_dve"))
        s_nat, s_natev, s_A, s_Aev, s_tt, s_tn, s_tnev, s_nm, s_lx, s_xs, s_ly, s_up = (
            sem(x) for x in ("s_nat", "s_natev", "s_A", "s_Aev", "s_tt", "s_tn", "s_tnev", "s_nm", "s_lx", "s_xs",
                             "s_ly", "s_up"))
        s_akv, s_akvev, s_w1, s_w1ev, s_y1, s_y1ev, s_z, s_zev, s_ya, s_yaev, s_ms, s_stt, s_y, s_yev = (
            sem(x) for x in ("s_akv", "s_akvev", "s_w1", "s_w1ev", "s_y1", "s_y1ev", "s_z", "s_zev", "s_ya", "s_yaev",
                             "s_ms", "s_stt", "s_y", "s_yev"))
        s_gc, s_gsq, s_gsd, s_gy = (sem(x) for x in ("s_gc", "s_gsq", "s_gsd", "s_gy"))
        s_osq, s_osd, s_fn = sem("s_osq"), sem("s_osd"), sem("s_fn")
        s_mxh, s_mxl, s_wo = sem("s_mxh"), sem("s_mxl"), sem("s_wo")
        s_h1h, s_h1l, s_qev, s_scp, s_scev = (sem(x) for x in ("s_h1h", "s_h1l", "s_qev", "s_scp", "s_scev"))
        s_rconst = sem("s_rconst")
        s_hraw = [sem(f"s_hraw{i}") for i in range(4)]
        s_hhi2, s_hlo2, s_up_mm, s_gelu = sem("s_hhi2"), sem("s_hlo2"), sem("s_up_mm"), sem("s_gelu")
        s_routed, s_gexp, s_gate, s_pt, s_pairs = (
            sem(x) for x in ("s_routed", "s_gexp", "s_gate", "s_pt", "s_pairs"))
        s_oha, s_ohr, s_ohb, s_grid, s_w = (sem(x) for x in ("s_oha", "s_ohr", "s_ohb", "s_grid", "s_w"))
        s_vraw = [sem(f"s_vraw{i}") for i in range(4)]
        s_vhi, s_vlo, s_wh, s_wl, s_down = (sem(x) for x in ("s_vhi", "s_vlo", "s_wh", "s_wl", "s_down"))
        s_h1s, s_xf, s_wfh, s_wfl, s_nr = (sem(x) for x in ("s_h1s", "s_xf", "s_wfh", "s_wfl", "s_nr"))

        def col(name, k=0, n=1, rows=P):
            c = COLS[name] + k
            return colv[0:rows, c:c + n]

        def over(ap2, n):
            return ap2.unsqueeze(1).to_broadcast([ap2.shape[0], n, ap2.shape[1]])

        def along(ap2, n):
            return ap2.unsqueeze(2).to_broadcast([ap2.shape[0], ap2.shape[1], n])

        def flat(t3, a, n):
            return t3[:].rearrange("p x y -> p (x y)")[:, a:a + n]

        def head(h):
            return h // 2, HD * (h % 2)

        block = ctx.enter_context(nc.Block())

        @block.sync
        def _(sp):
            sp.dma_start(colv[:], cols).then_inc(s_cols, 16)
            for q in range(XQ):
                ks = slice(KT // XQ * q, KT // XQ * (q + 1))
                sp.dma_start(xin[:, ks, :], xT[:, ks, :]).then_inc(s_x[q], 16)
            sp.dma_start(wfs[:], wf).then_inc(s_small, 16)
            sp.dma_start(w2s[:], w2a2).then_inc(s_small, 16)
            sp.dma_start(g2s[:], g2).then_inc(s_small, 16)
            sp.dma_start(kst[:], keysT).then_inc(s_small, 16)
            sp.dma_start(states[:, 6, :, :], s0T).then_inc(s_small, 16)

            def load(i):
                if i >= RAWS:
                    sp.wait_ge(s_item, i - RAWS + 1)
                sp.dma_start(raw[i % RAWS][:], wbig[i]).then_inc(s_raw[i % RAWS], 16)

            for i in range(I_RW):
                load(i)
                if i == RAWS - 1:
                    sp.wait_ge(s_ln, KT)
                    sp.dma_start(ckx[0:HD, :, :], ckT).then_inc(s_cache, 16)
                    sp.dma_start(vs[0:HD, 0, :], cv[0:HD, :]).then_inc(s_cache, 16)
                    sp.dma_start(vs[:, 1:4, :], cv[HD:PAST - HD, :].rearrange("(i p) c -> p i c", p=P)).then_inc(s_cache, 16)
                    sp.dma_start(vs[0:HD, 4, :], cv[PAST - HD:PAST, :]).then_inc(s_cache, 16)
                    sp.dma_start(lfs[:, 0, 0:PAST], clf).then_inc(s_cache, 16)
            sp.wait_ge(s_vev, 4)
            for b in range(NQB):
                n = min(QB, TP - QB * b)
                sp.dma_start(vpo[QB * b:QB * b + n, :], vp[0:n, b, :]).then_inc(s_out, 16)
            sp.dma_start(vso, vs[HD:P, 4, :]).then_inc(s_out, 16)
            sp.wait_ge(s_pev, K_ITEMS)
            sp.dma_start(ko, kx[0:HD, :, :]).then_inc(s_out, 16)
            sp.wait_ge(s_logf, 1)
            sp.dma_start(lfo, lf[:, 2, :]).then_inc(s_out, 16)
            for i in range(I_RW, I_WO):
                load(i)
            sp.wait_ge(s_shift, RW_TILES)
            sp.dma_start(sho, shs[:]).then_inc(s_out, 16)
            for i in range(I_WO, N_ITEMS):
                load(i)
                if i == I_WO + RAWS - 1:
                    sp.wait_ge(s_stt, 6)
                    sp.dma_start(wkvo[:, 0], states[:, 5, :, :]).then_inc(s_out, 16)
                    sp.dma_start(wkvo[:, 1], states[:, 7, :, :]).then_inc(s_out, 16)

            sp.wait_ge(s_gy, 3)
            sp.wait_ge(s_mxl, NJ + NG)
            for q in range(4):
                sp.dma_start(hraw[q][:], uT[q]).then_inc(s_hraw[q], 16)
            with sp.Fori(1, 2 * NI // 4) as k:
                for q in range(4):
                    sp.wait_ge(s_up_mm, k * 8 + (2 * q - 6))
                    sp.dma_start(hraw[q][:], uT[bass.ds(k * 4 + q, 1)].rearrange("a p c -> (a p) c")).then_inc(s_hraw[q], 16)
            sp.wait_ge(s_grid, T // 4)
            for q in range(4):
                sp.dma_start(hraw[q][:], vE[q]).then_inc(s_vraw[q], 16)
            with sp.Fori(1, 2 * NI // 4) as k:
                for q in range(4):
                    sp.wait_ge(s_down, k * 4 + (q - 3))
                    sp.dma_start(hraw[q][:], vE[bass.ds(k * 4 + q, 1)].rearrange("a p c -> (a p) c")).then_inc(s_vraw[q], 16)
            for q in range(4):
                sp.wait_ge(s_ln, 2 * KT + 2 * q + 2)
                sp.dma_start(yT[:, 2 * q:2 * q + 2, :], XF[:, 2 * q:2 * q + 2, :]).then_inc(s_out, 16)
            sp.wait_ge(s_out, 16 * (NQB + 1 + 1 + 1 + 1 + 2 + 4))

        @block.gpsimd
        def _(pool):
            n = [0]

            def own(ins):
                n[0] += 1
                ins.then_inc(s_pool, 1)
                pool.wait_ge(s_pool, n[0])

            def select(t, pattern, op, base, cm, fill):
                own(nc.gpsimd.affine_select(out=t, in_=t, pattern=pattern, compare_op=op, fill=fill, base=base,
                                            channel_multiplier=cm))

            nc.gpsimd.memset(ones[:], 1.0 / D).then_inc(s_onesg, 1)
            own(nc.gpsimd.memset(ident[:], 0.0))
            select(ident[:], [[-1, P]], ALU.not_equal, 0, 1, 1.0)
            own(nc.gpsimd.memset(blk[:], 0.0))
            for e in range(2):
                own(nc.gpsimd.memset(blk[HD * e:HD * e + HD, HD * e:HD * e + HD], 1.0 / HD))
            own(nc.gpsimd.memset(causal[:], 1.0))
            for e, base in ((0, -1), (1, 0)):
                c = causal[:, P * e:P * e + P]
                select(c, [[1, P]], ALU.is_ge, base, -1, 0.0)
                own(nc.gpsimd.memset(c[0:CH, CH:P], 0.0))
            own(nc.gpsimd.memset(lev[:], 0.0))
            for l in range(6):
                b = 1 << l
                v = lev[:, l, :].rearrange("p (g x b) -> p g x b", x=2, b=b)[:, :, 1, :]
                own(nc.gpsimd.memset(v, 1.0))
                pat = [[2 * b, P // (2 * b)], [0, b]]
                select(v, [[-2 * b, P // (2 * b)], [0, b]], ALU.is_ge, 0, 1, 0.0)
                select(v, pat, ALU.is_ge, b - 1, -1, 0.0)
            own(nc.gpsimd.memset(eye2[:], 0.0))
            select(eye2[:], [[-1, HD]], ALU.not_equal, 0, 1, 1.0)
            select(eye2[:], [[-1, HD]], ALU.not_equal, -HD, 1, 1.0)
            own(nc.gpsimd.memset(amask[:], 0.0))
            select(amask[:], [[-1, P]], ALU.is_ge, 0, 1, NEG)
            own(nc.gpsimd.memset(keep[:], 1.0))
            own(nc.gpsimd.memset(keep[:, 0:TC:CH], 0.0))
            own(nc.gpsimd.memset(ones8[:], 1.0))
            own(nc.gpsimd.memset(qx[HD:KX, :, :], 0.0))
            select(qx[HD:KX, :, :], [[-1, H], [0, T]], ALU.not_equal, 0, 1, 1.0)
            own(nc.gpsimd.memset(pb[:, :, 0:1], 0.0))
            own(nc.gpsimd.memset(pb[:, :, TP + 1:PADP], 0.0))
            own(nc.gpsimd.memset(states[:, 0, :, :], 0.0))
            nc.gpsimd.sem_inc(s_const, 1)

            pool.wait_ge(s_logf, 2)
            pool.wait_ge(s_ln, KT)
            for dst, src in ((kx[HD:KX, :, 0:TP], lf[:, 3, 0:TP]), (kx[HD:KX, :, TP:T], lfs[:, 1, PAST:KEYS]),
                             (ckx[HD:KX, :, :], lfs[:, 1, 0:PAST])):
                nc.gpsimd.tensor_scalar(dst, over(src, H), -1.0, 0.0, ALU.mult, ALU.add).then_inc(s_negc, 1)
            pool.wait_ge(s_negc, 3)

            def wlo_of(i):
                pool.wait_ge(s_whi, i + 1)
                nc.gpsimd.tensor_tensor(wlo[i % RAWS][:], raw[i % RAWS][:], whi[i % HIS][:].bitcast(F32),
                                        ALU.subtract).then_inc(s_wlo_pool, 1)

            wlo_of(I_RW)
            for r in range(RW_TILES):
                if r >= 3:
                    pool.wait_ge(s_xm, r - 2)
                    pool.wait_ge(s_shift, r - 2)
                nc.gpsimd.tensor_copy(pb[:, r % 3, PADP:PADP + 1], col("shift", RW_ORDER[r])).then_inc(s_state, 1)
                if r + 1 < RW_TILES:
                    wlo_of(I_RW + r + 1)
                pool.wait_ge(s_pev, I_RW + r - I_K + 1)
                nc.gpsimd.tensor_copy(shs[:, RW_ORDER[r], :], pb[:, r % 3, TP:TC + 1:TC - TP]).then_inc(s_shift, 1)

            n_nm = 0
            for gi in range(NG):
                for l in range(1, 6):
                    for hf in range(2):
                        if l == 1:
                            pool.wait_ge(s_Aev, 4 * gi + 2 * hf + 1)
                        if n_nm >= 2:
                            pool.wait_ge(s_lx, n_nm - 1)
                        nc.gpsimd.tensor_tensor(Nm[:, hf, :, :], NR[:, 4 * hf:4 * hf + 4, 0:P], over(lev[:, l, :], 4),
                                                ALU.mult).then_inc(s_nm, 1)
                        n_nm += 1
            wlo_of(I_WO)
            wlo_of(I_WO + 1)

            pool.wait_ge(s_scp, 12)
            own(nc.gpsimd.memset(identb[:], 0.0))
            select(identb[:], [[-1, P]], ALU.not_equal, 0, 1, 1.0)
            own(nc.gpsimd.iota(iotak[:], pattern=[[1, NK]], base=0, channel_multiplier=0,
                               allow_small_or_imprecise_dtypes=True))
            own(nc.gpsimd.iota(iota16[:], pattern=[[0, 16], [1, 16]], base=0, channel_multiplier=0,
                               allow_small_or_imprecise_dtypes=True))
            nc.gpsimd.sem_inc(s_rconst, 1)

            def lo(c, q):
                pool.wait_ge(s_hhi2, c + 1)
                cols_ = slice(256 * (q % 2), 256 * (q % 2) + 256)
                nc.gpsimd.tensor_tensor(hlo[q // 2 % 4][:, cols_], hraw[q // 2 % 4][:, cols_], hhiq[q % 4][:].bitcast(F32),
                                        ALU.subtract).then_inc(s_hlo2, 1)

            for q in range(4 * RIT):
                lo(q, q)
            with pool.Fori(1, NI // RIT) as k:
                for q in range(4 * RIT):
                    lo(k * (4 * RIT) + q, q)

            pool.wait_ge(s_up_mm, 4 * NI)
            nc.gpsimd.tensor_tensor(H1s[:], H1h[:].bitcast(F32), H1l[:].bitcast(F32), ALU.add).then_inc(s_h1s, 1)
            pool.wait_ge(s_down, 2 * NI)
            nc.gpsimd.memset(ones2[:], 1.0 / D).then_inc(s_onesg, 1)

        @block.scalar
        def _(act):
            n = [0]

            def own(ins):
                n[0] += 1
                ins.then_inc(s_act, 1)
                act.wait_ge(s_act, n[0])

            def A(out, in_, f, **kw):
                return nc.scalar.activation(out, in_, f, **kw)

            def norm_squares(n, X, S):
                for j, k in enumerate(NORM_ORDER[n]):
                    act.wait_ge(s_xc, KT * n + j + 1)
                    A(S[:, k, :], X[:, k, :], ACT.Square).then_inc(s_sq, 1)

            def norm_root(n, sd):
                act.wait_ge(s_var, n + 1)
                A(sd[:], PS[:, VAR_BANK, 0:T], ACT.Sqrt, bias=LN_EPS).then_inc(s_sd, 1)

            def whi_of(i):
                act.wait_ge(s_raw[i % RAWS], 16 * (i // RAWS + 1))
                if i >= HIS:
                    act.wait_ge(s_item, i - HIS + 1)
                A(whi[i % HIS][:], raw[i % RAWS][:], ACT.Copy).then_inc(s_whi, 1)

            def evacuate(i):
                if i < V_ITEMS:
                    if i == V_ITEMS - 1:
                        act.wait_ge(s_item, V_ITEMS)
                        act.wait_ge(s_cache, 80)
                        for b in range(NQB):
                            A(vp[0:QB, b, :], PS[0:QB, 4 + b, :], ACT.Copy).then_inc(s_vev, 1)
                        A(vs[HD:P, 4, :], PS[HD:P, 7, :], ACT.Copy).then_inc(s_vev, 1)
                    return
                act.wait_ge(s_item, i + 1)
                b = PS[:, i % 2, :]
                if i < I_RW:
                    dst, j, scale = (kx, i - I_K, 1.0) if i < I_Q else (qx, i - I_Q, HD ** -0.5)
                    A(dst[0:HD, 2 * j, :], b[0:HD, 0:T], ACT.Copy, scale=scale)
                    A(dst[0:HD, 2 * j + 1, :], b[HD:P, 0:T], ACT.Copy, scale=scale).then_inc(s_pev, 1)
                    return
                r = i - I_RW
                t = RW_ORDER[r]
                if r >= 3:
                    act.wait_ge(s_xm, r - 2)
                    act.wait_ge(s_shift, r - 2)
                s = pb[:, r % 3, :]
                A(s[:, 1:TP + 1], b[:, 0:TP], ACT.Copy)
                A(s[:, PADP + 1:TC + 1], b[:, TP:T], ACT.Copy).then_inc(s_pev, 1)

            def attention(s):
                if s < NU:
                    rows, keys, _ = unit_shape(UNITS[s])
                    act.wait_ge(s_max, s + 1)
                    if s >= 2:
                        act.wait_ge(s_tr, s - 1)
                    b = 2 if UNITS[s][0] == "s" else 2 + s % 2
                    A(pr[0:rows, s % 2, 0:keys], flat(PS, 512 * b, keys)[0:rows], ACT.Exp,
                      bias=st[0:rows, s % 2, 1:2], accum_out=st[0:rows, s % 2, 2:3]).then_inc(s_exp, 1)
                if 1 <= s <= NU:
                    u = s - 1
                    rows, _, tiles = unit_shape(UNITS[u])
                    act.wait_ge(s_tr, u + 1)
                    if u >= 2:
                        act.wait_ge(s_pv, u - 1)
                    b = 4 if UNITS[u][0] == "s" else 4 + u % 2
                    full = sum(w == QB for _, w in tiles)
                    parts = [(0, 1, 64), (1, 5, P)] if UNITS[u][0] == "s" else [(0, full, QB)] * (full > 0)
                    if UNITS[u][0] == "p" and full < len(tiles):
                        parts.append((full, full + 1, tiles[-1][1]))
                    for a, z, w in parts:
                        ins = A(pt[0:w, u % 2, P * a:P * z].rearrange("p (x r) -> p x r", r=P)[:, :, 0:rows],
                                flat(PS, 512 * b + P * a, P * (z - a))[0:w].rearrange("p (x r) -> p x r", r=P)[:, :, 0:rows],
                                ACT.Copy)
                    ins.then_inc(s_tev, 1)
                if s >= 2:
                    u = s - 2
                    kind, a, qb = UNITS[u]
                    act.wait_ge(s_pv, u + 1)
                    if kind == "s":
                        A(oT[:, a, TP:T], PS[:, 6 + u % 2, 0:DEC], ACT.Copy).then_inc(s_oev, 1)
                    else:
                        rows = unit_shape(UNITS[u])[0]
                        j, o_ = head(a)
                        A(oT[o_:o_ + HD, j, QB * qb:QB * qb + rows], PS[o_:o_ + HD, 6 + u % 2, 0:rows],
                          ACT.Copy).then_inc(s_oev, 1)

            norm_squares(0, xin, SQ0)
            whi_of(0)
            norm_root(0, SD)
            act.wait_ge(s_small, 80)
            A(wfh[:], wfs[:], ACT.Copy).then_inc(s_wfh, 1)
            for j in range(KT):
                act.wait_ge(s_ln, j + 1)
                A(hTh[:, j, :], hT[:, j, :], ACT.Copy).then_inc(s_hhi, 1)
                if j == 0:
                    whi_of(1)

            act.wait_ge(s_const, 1)
            act.wait_ge(s_fz, 1)
            own(A(lf[:, 1, :], lf[:, 1, :], ACT.Exp, scale=-1.0))
            A(lf[:, 1, :], lf[:, 1, :], ACT.Ln, bias=1.0).then_inc(s_fe, 1)
            def channels(r):
                if r == 1:
                    act.wait_ge(s_xm, 1)
                    A(xm[0:HD, 12, :], xm[0:HD, 12, :], ACT.Tanh).then_inc(s_tanh, 1)
                if r == 2:
                    act.wait_ge(s_xm, 2)
                    A(xm[:, 13, :], xm[:, 13, :], ACT.Sigmoid).then_inc(s_tanh, 1)
                    for j in range(NJ):
                        act.wait_ge(s_lora, 2 * j + 1)
                        A(AR[:, 0, j, :], PS[:, 6, 0:TC], ACT.Sigmoid, bias=col("w0", j)).then_inc(s_loev, 1)
                        act.wait_ge(s_lora, 2 * j + 2)
                        A(AA[:, j, :], PS[:, 7, 0:TC], ACT.Sigmoid, bias=col("a0", j)).then_inc(s_loev, 1)
                if 3 <= r < 3 + NJ:
                    j = r - 3
                    act.wait_ge(s_xm, 2 + j + 1)
                    if j == 3:
                        act.wait_ge(s_logf, 2)
                    A(BH[j][:], xm[:, NJ + j, :], ACT.Square, scale=col("k_k", j)).then_inc(s_kksq, 1)
                if r == 4:
                    act.wait_ge(s_ls, 1)
                    A(AR[:, 1, :, :], LS[:], ACT.Exp, scale=CDEC).then_inc(s_d, 1)
                if r == 5:
                    act.wait_ge(s_lprev, 1)
                    A(AR[:, 0, :, :], AR[:, 0, :, :], ACT.Exp, scale=CDEC).then_inc(s_dprev, 1)
                if r == 6:
                    A(LS[:], LS[:], ACT.Exp, scale=-CDEC).then_inc(s_dprev, 1)
                if r == 8:
                    act.wait_ge(s_rn, NJ)
                    for j in range(NJ):
                        A(BH[j][:], BH[j][:], ACT.Sqrt).then_inc(s_kkrt, 1)

            for i in range(I_WO):
                if 1 <= i < I_WO - 1:
                    whi_of(i + 1)
                if i >= I_RW:
                    attention(2 * (i - I_RW))
                evacuate(i)
                if i >= I_RW:
                    attention(2 * (i - I_RW) + 1)
                    channels(i - I_RW)
            for s in range(2 * RW_TILES, NU + 2):
                attention(s)

            def fill(f):
                kind, x = kind_of(f - 1)
                if kind == "M":
                    act.wait_ge(s_fill_dve, taken(f - 1)[1])
                    A(GSQ[:], AR[:, 0, :, P * x:P * x + P], ACT.Square).then_inc(s_gsq, 1)
                if kind == "F":
                    act.wait_ge(s_fn, x + 1)
                    A(MXh[:, x, :], oT[:, x, :], ACT.Copy).then_inc(s_mxh, 1)
                kind, x = kind_of(f - 2)
                if kind == "V":
                    act.wait_ge(s_gy, x + 1)
                    A(MXh[:, NJ:KT, P * x:P * x + P], AR[:, 0, :, P * x:P * x + P], ACT.Copy).then_inc(s_mxh, 1)
                kind, x = kind_of(f)
                if kind and kind in "GVF":
                    act.wait_ge(s_fill, f + 1)
                    b = PS[:, 6 + f % 2, :]
                if kind == "G":
                    A(xm[:, NJ + x, :], b[:, 0:TC], ACT.Copy).then_inc(s_fill_act, 1)
                if kind == "V":
                    A(GSD[:].rearrange("p j t -> p (j t)"), b, ACT.Sqrt, bias=LNX_EPS).then_inc(s_fill_act, 1)
                if kind == "F":
                    A(FSQ[:, x, :], b[:, 0:T], ACT.Sqrt, bias=1e-6).then_inc(s_fill_act, 1)

            act.wait_ge(s_oev, NU)
            act.wait_ge(s_out, 16 * (NQB + 4))
            for gi in range(NG):
                for k, dst in enumerate((vN, bN, kN, AX)):
                    act.wait_ge(s_nat, 4 * gi + k + 1)
                    if k == 0 and gi:
                        act.wait_ge(s_ya, gi)
                    src = PS[:, 6 + k % 2, :].rearrange("p (h c) -> p h c", c=HD)
                    A(dst[:, :, 0:HD], src, ACT.Copy).then_inc(s_natev, 1)
                act.wait_ge(s_akv, gi + 1)
                A(AX[:, :, HD:P], PS[:, 6, :].rearrange("p (h c) -> p h c", c=HD), ACT.Copy).then_inc(s_akvev, 1)
                if gi == 0:
                    A(FSQ[:], oT[:], ACT.Square).then_inc(s_osq, 1)
                for hf in range(2):
                    act.wait_ge(s_tn, 2 * gi + hf + 1)
                    A(Tn[:, 4 * hf:4 * hf + 4, :], PS[:, 4 + hf, :].rearrange("p (h c) -> p h c", c=P),
                      ACT.Copy).then_inc(s_tnev, 1)
                for l in range(1, 6):
                    for hf in range(2):
                        act.wait_ge(s_lx, 10 * gi + 2 * (l - 1) + hf + 1)
                        if l > 1 or gi:
                            act.wait_ge(s_ly, 10 * gi + 2 * (l - 1) + hf - 1)
                        A(Xs[:, 4 * hf:4 * hf + 4, :], PS[:, hf, :].rearrange("p (h c) -> p h c", c=P),
                          ACT.Copy).then_inc(s_xs, 1)
                    fill(5 * gi + l - 1)
                for hf in range(2):
                    act.wait_ge(s_w1, 2 * gi + hf + 1)
                    A(X12[:, 4 * hf:4 * hf + 4, :], PS[:, hf, :].rearrange("p (h c) -> p h c", c=P),
                      ACT.Copy).then_inc(s_w1ev, 1)
                act.wait_ge(s_ya, gi + 1)
                A(AR[:, 0, :, P * gi:P * gi + P], PS[:, 7, :].rearrange("p (j t) -> p j t", j=NJ), ACT.Copy).then_inc(s_yaev, 1)

            fill(len(FILL))
            whi_of(I_WO)
            whi_of(I_WO + 1)
            act.wait_ge(s_gc, 1)
            A(GSQ[:], AR[:, 0, :, P * (NG - 1):TC], ACT.Square).then_inc(s_gsq, 1)
            act.wait_ge(s_fill, len(FILL) + 2)
            A(GSD[:].rearrange("p j t -> p (j t)"), PS[:, 7, :], ACT.Sqrt, bias=LNX_EPS).then_inc(s_fill_act, 1)
            act.wait_ge(s_gy, NG)
            for a, z, w in chunk_tokens(NG - 1):
                ins = A(MXh[:, NJ:KT, z:z + w], AR[:, 0, :, a:a + w], ACT.Copy)
            ins.then_inc(s_mxh, 1)
            for i in range(I_WO + 2, I_WQ):
                whi_of(i)
            norm_squares(1, X1, SQ1)
            whi_of(I_WQ)
            norm_root(1, SD)
            for j in range(KT):
                act.wait_ge(s_ln, KT + j + 1)
                A(H1h[:, j, :], X1[:, j, :], ACT.Copy).then_inc(s_h1h, 1)

            for i in range(I_WQ, N_ITEMS):
                if i > I_WQ:
                    whi_of(i)
                    q = i - 1 - I_WQ
                    act.wait_ge(s_item, i)
                    A(QT[:, q, :], PS[:, (i - 1) % 2, 0:T], ACT.Copy).then_inc(s_qev, 1)
            act.wait_ge(s_item, N_ITEMS)
            A(QT[:, 2 * PH - 1, :], PS[:, (N_ITEMS - 1) % 2, 0:T], ACT.Copy).then_inc(s_qev, 1)
            for k in range(12):
                act.wait_ge(s_scp, k + 1)
                A(scores[:, 512 * k:512 * k + 512], PS[:, 2 + k % 2, :], ACT.Copy).then_inc(s_scev, 1)

            def quarter(c, q, load):
                if q % 2 == 0:
                    act.wait_ge(s_hraw[q // 2 % 4], load)
                if not isinstance(c, int) or c >= 4:
                    act.wait_ge(s_up_mm, c - 3)
                A(hhiq[q % 4][:], hraw[q // 2 % 4][:, 256 * (q % 2):256 * (q % 2) + 256], ACT.Copy).then_inc(s_hhi2, 1)

            def gelu(e, slot):
                act.wait_ge(s_up_mm, e * 4 + 4)
                A(W[:, bass.ds(e, 1), :].rearrange("p a t -> p (a t)"), PS[:, slot % 4, 0:T], ACT.Gelu).then_inc(s_gelu, 1)

            act.wait_ge(s_out, 16 * (NQB + 6))
            for e in range(RIT):
                for x in range(4):
                    quarter(4 * e + x, 4 * e + x, 16 * (e // 2 + 1))
                if e:
                    gelu(e - 1, e - 1)

            def up_rest(k):
                for e in range(RIT):
                    for x in range(4):
                        quarter(k * 16 + (4 * e + x), 4 * e + x, k * 32 + 16 * (e // 2 + 1))
                    gelu(k * 4 + (e - 1), e - 1)

            with act.Fori(1, 3 * PH) as k:
                up_rest(k)
            act.wait_ge(s_gexp, 1)
            A(best[:], best[:], ACT.Exp).then_inc(s_gate, 1)
            act.wait_ge(s_pairs, 6)
            with act.Fori(3 * PH, NI // RIT) as k:
                up_rest(k)
            gelu(NI - 1, NI - 1)

            def gates(g_, slot, t0):
                act.wait_ge(s_ohr, g_ + 1)
                for x in range(4):
                    ins = A(ohB[:, slot, x, :], ohB[:, slot, x, :], ACT.Copy, scale=pairg[:, bass.ds(t0 + x, 1)])
                ins.then_inc(s_ohb, 1)

            for q in range(GIT):
                gates(q, q % 3, 4 * q)
            with act.Fori(1, T // (4 * GIT)) as k:
                for q in range(GIT):
                    gates(k * GIT + q, q % 3, k * (4 * GIT) + 4 * q)

            def down(e, s, load):
                if not isinstance(e, int) or e >= 2:
                    act.wait_ge(s_down, e * 2 - 2)
                A(Wh[s][:], W[:, bass.ds(e, 1), :].rearrange("p a t -> p (a t)"), ACT.Copy).then_inc(s_wh, 1)
                for b in range(2):
                    act.wait_ge(s_vraw[2 * s + b], load)
                    if not isinstance(e, int) or 2 * e + b >= 2:
                        act.wait_ge(s_down, e * 2 + (b - 1))
                    A(hhi[b][:], hraw[2 * s + b][:], ACT.Copy).then_inc(s_vhi, 1)

            act.wait_ge(s_w, T // 4)
            for e in range(2):
                down(e, e, 16)
            with act.Fori(1, NI // 2) as k:
                for e in range(2):
                    down(k * 2 + e, e, k * 16 + 16)
            norm_squares(2, XF, SQF)
            norm_root(2, SDF)

        @block.tensor
        def _(pe):
            mm = nc.tensor.matmul

            def mean_part(n, j, X, c1):
                ins = mm(PS[:, MEAN_BANK, 0:T], c1[:], X[:, NORM_ORDER[n][j], :], start=(j == 0), stop=(j == KT - 1))
                if j == KT - 1:
                    ins.then_inc(s_mean, 1)

            def variance(n, S, c1):
                for j, k in enumerate(NORM_ORDER[n]):
                    pe.wait_ge(s_sq, KT * n + j + 1)
                    ins = mm(PS[:, VAR_BANK, 0:T], c1[:], S[:, k, :], start=(j == 0), stop=(j == KT - 1))
                ins.then_inc(s_var, 1)

            def three(out, whi_, wlo_, xhi, xlo, start, stop):
                mm(out, whi_, xhi, start=start, stop=False)
                mm(out, whi_, xlo, start=False, stop=False)
                return mm(out, wlo_, xhi, start=False, stop=stop)

            pe.wait_ge(s_onesg, 1)
            for j in range(KT):
                pe.wait_ge(s_x[j // (KT // XQ)], 16)
                mean_part(0, j, xin, ones)
            variance(0, SQ0, ones)

            def forget_logits():
                pe.wait_ge(s_wfl, 1)
                pe.wait_ge(s_hlo, KT)
                for k in range(KT):
                    w = slice(H * k, H * k + H)
                    ins = three(PS[0:H, 2, 0:T], wfh[:, w], wfl[:, w], hTh[:, k, :], hTl[:, k, :], k == 0, k == KT - 1)
                ins.then_inc(s_f, 1)

            def split(i):
                pool_did = min(max(i + 1 - POOL_ITEMS.start, 0), len(POOL_ITEMS))
                if i in POOL_ITEMS:
                    pe.wait_ge(s_wlo_pool, pool_did)
                else:
                    pe.wait_ge(s_wlo, i + 1 - pool_did)

            def item(i, xh, xl, ready=None, between=None, ks=range(KT)):
                if ks[0] == 0:
                    split(i)
                w, v = whi[i % HIS], wlo[i % RAWS]
                for k in ks:
                    if ready is not None:
                        pe.wait_ge(ready, k + 1)
                    if k == KT // 2 and between is not None:
                        between()
                    ins = three(PS[:, i % 2, 0:T], w[:, P * k:P * k + P], v[:, P * k:P * k + P], xh[:, k, :], xl[:, k, :],
                                k == 0, k == KT - 1)
                if ks[-1] == KT - 1:
                    ins.then_inc(s_item, 1)

            def scores_of(s):
                kind, a, qb = UNITS[s]
                rows, keys, tiles = unit_shape(UNITS[s])
                solo = s == 0 or "s" in (kind, UNITS[s - 1][0])
                if s:
                    pe.wait_ge(s_exp, s if solo else s - 1) if (solo or s >= 2) else None
                if kind == "p":
                    out = PS[0:rows, 2 + s % 2, :]
                    mm(out[:, 0:keys], qx[:, a, QB * qb:QB * qb + rows], kx[:, a, 0:keys], start=True, stop=False)
                    mm(out[:, QB * qb:keys], ident[0:rows, 0:rows], amask[0:rows, 0:rows], start=False,
                       stop=True).then_inc(s_sc, 1)
                    return
                for e in range(2):
                    h, o_ = 2 * a + e, HD * e
                    mm(PS[o_:o_ + HD, 2, :], qx[:, h, TP:T], ckx[:, h, :], start=True, stop=True)
                    mm(PS[o_:o_ + HD, 3, 0:DEC], qx[:, h, TP:T], kx[:, h, TP:T], start=True, stop=False)
                    ins = mm(PS[o_:o_ + HD, 3, 0:DEC], ident[0:HD, 0:HD], amask[0:HD, 0:HD], start=False, stop=True)
                ins.then_inc(s_sc, 1)

            def transposes_of(u):
                kind = UNITS[u][0]
                rows, _, tiles = unit_shape(UNITS[u])
                pe.wait_ge(s_norm, u + 1)
                if u:
                    solo = "s" in (kind, UNITS[u - 1][0])
                    if solo or u >= 2:
                        pe.wait_ge(s_tev, u if solo else u - 1)
                b = 4 if kind == "s" else 4 + u % 2
                for i, (k0, w) in enumerate(tiles):
                    ins = nc.tensor.transpose(flat(PS, 512 * b + P * i, rows)[0:w], pr[0:rows, u % 2, k0:k0 + w],
                                              ident[0:rows, 0:rows])
                ins.then_inc(s_tr, 1)

            def values_of(u):
                kind, a, qb = UNITS[u]
                rows, _, tiles = unit_shape(UNITS[u])
                pe.wait_ge(s_tev, u + 1)
                if u >= 2:
                    pe.wait_ge(s_oev, u - 1)
                if u == 4:
                    pe.wait_ge(s_loev, 8)
                if u >= 9 and u % 2 and (u - 9) // 2 < NJ:
                    pe.wait_ge(s_n2m, (u - 9) // 2 + 1)
                for e in range(2 if kind == "s" else 1):
                    h = 2 * a + e if kind == "s" else a
                    o_ = head(h)[1]
                    q0, qn = (HD * e, DEC) if kind == "s" else (0, rows)
                    for i, (k0, w) in enumerate(tiles):
                        v = (vs if kind == "s" else vp)[0:w, i, HD * h:HD * h + HD]
                        ins = mm(PS[o_:o_ + HD, 6 + u % 2, 0:qn], v, pt[0:w, u % 2, P * i + q0:P * i + q0 + qn],
                                 start=(i == 0), stop=(i == len(tiles) - 1))
                ins.then_inc(s_pv, 1)

            def attention(s):
                if s < NU:
                    scores_of(s)
                if 1 <= s <= NU:
                    transposes_of(s - 1)
                if s >= 2:
                    values_of(s - 2)

            V0 = [0, QB, 2 * QB, T - P]
            for i in range(V_ITEMS):
                split(i)
                for kk in range(2):
                    k = 2 * i + kk
                    pe.wait_ge(s_hlo, k + 1)
                    for b, t0 in enumerate(V0):
                        w, v = whi[i % HIS][:, 512 * kk:512 * kk + 512], wlo[i % RAWS][:, 512 * kk:512 * kk + 512]
                        ins = three(PS[:, 4 + b, :], hTh[:, k, t0:t0 + P], hTl[:, k, t0:t0 + P], w, v,
                                    k == 0, k == KT - 1)
                ins.then_inc(s_item, 1)
                if i == 0:
                    forget_logits()

            def channels(r):
                if r == 2:
                    pe.wait_ge(s_tanh, 1)
                    pe.wait_ge(s_oev, 2 * r)
                    for j in range(NJ):
                        if j:
                            pe.wait_ge(s_loev, 2 * j - 1)
                        mm(PS[:, 6, 0:TC], w2s[0:HD, P * j:P * j + P], xm[0:HD, 12, :], start=True,
                           stop=True).then_inc(s_lora, 1)
                        if j:
                            pe.wait_ge(s_loev, 2 * j)
                        mm(PS[:, 7, 0:TC], w2s[HD:P, P * j:P * j + P], xm[HD:P, 12, :], start=True,
                           stop=True).then_inc(s_lora, 1)
                if 4 <= r < 4 + NJ:
                    j = r - 4
                    pe.wait_ge(s_kksq, j + 1)
                    pe.wait_ge(s_oev, 2 * r)
                    mm(PS[:, 7, 0:TC], blk[:], BH[j][:], start=True, stop=True).then_inc(s_n2, 1)

            for i in range(I_K, I_WO):
                if i - I_K >= 2:
                    pe.wait_ge(s_pev, i - I_K - 1)
                r = i - I_RW
                if r < 0:
                    item(i, hTh, hTl)
                    continue
                if r == 0:
                    item(i, hTh, hTl)
                    pe.wait_ge(s_negc, 3)
                    pe.wait_ge(s_vev, 4)
                    pe.wait_ge(s_pev, K_ITEMS + Q_ITEMS)
                    attention(0)
                else:
                    item(i, hTh, hTl, between=lambda: attention(2 * r))
                attention(2 * r + 1)
                channels(r)
            for s in range(2 * RW_TILES, NU + 2):
                attention(s)

            def fill(f):
                if f >= 2:
                    by_act, n = taken(f - 2)
                    pe.wait_ge(s_fill_act if by_act else s_fill_dve, n)
                kind, x = kind_of(f)
                b = PS[:, 6 + f % 2, :]
                if kind == "G":
                    pe.wait_ge(s_tanh, 2)
                    ins = mm(b[:, 0:TC], g2s[:, P * x:P * x + P], xm[:, 13, :], start=True, stop=True)
                if kind == "B":
                    ins = mm(b, blk[:], xm[:, 0:NJ, :].rearrange("p j t -> p (j t)")[:, 512 * x:512 * x + 512], start=True,
                             stop=True)
                if kind == "M":
                    pe.wait_ge(s_yev, 2 * x + 2)
                    ins = mm(b.rearrange("p (j t) -> p j t", j=NJ), blk[:], AR[:, 0, :, P * x:P * x + P], start=True, stop=True)
                if kind == "V":
                    pe.wait_ge(s_gsq, x + 1)
                    ins = mm(b, blk[:], GSQ[:].rearrange("p j t -> p (j t)"), start=True, stop=True)
                if kind == "F":
                    pe.wait_ge(s_osq, 1)
                    ins = mm(b[:, 0:T], blk[:], FSQ[:, x, :], start=True, stop=True)
                ins.then_inc(s_fill, 1)

            pe.wait_ge(s_oev, NU)
            for gi in range(NG):
                tok = slice(P * gi, P * gi + P)
                for k, src in enumerate(("v", "b", "k", "a")):
                    if k == 0:
                        pe.wait_ge(s_prep, 1)
                        if gi:
                            pe.wait_ge(s_zev, gi)
                    if k >= 2:
                        pe.wait_ge(s_natev, 4 * gi + k - 1)
                    if k == 1 and gi:
                        pe.wait_ge(s_yaev, gi)
                    for j in range(NJ):
                        t = {"v": xm[:, 8 + j, tok], "b": BH[j][:, tok], "k": LS[:, j, tok], "a": AR[:, 0, j, tok]}[src]
                        ins = nc.tensor.transpose(PS[:, 6 + k % 2, P * j:P * j + P], t, ident[:])
                    ins.then_inc(s_nat, 1)
                for hf in range(2):
                    if hf:
                        pe.wait_ge(s_Aev, 4 * gi + 2)
                    elif gi:
                        pe.wait_ge(s_stt, 2 * gi)
                        pe.wait_ge(s_yev, 2 * gi)
                    for x in range(2):
                        for hh in range(4):
                            h = 4 * hf + hh
                            j, o_ = head(h)
                            src = LS[o_:o_ + HD, j, tok] if x else BH[j][o_:o_ + HD, tok]
                            out = PS[:, 2 * x + hh % 2, 256 * (hh // 2):256 * (hh // 2) + 256]
                            ins = mm(out.rearrange("p (x t) -> p x t", x=2), src, AR[o_:o_ + HD, :, j, tok],
                                     start=True, stop=True)
                        ins.then_inc(s_A, 1)
                pe.wait_ge(s_Aev, 4 * gi + 4)
                pe.wait_ge(s_natev, 4 * gi + 4)
                for h in range(H):
                    ins = mm(PS[:, 6, HD * h:HD * h + HD], AK[:, h, 0:P], vN[:, h, :], start=True, stop=True)
                ins.then_inc(s_akv, 1)
                for hf in range(2):
                    pe.wait_ge(s_tt, 2 * gi + hf + 1)
                    for hh in range(4):
                        ins = nc.tensor.transpose(PS[:, 4 + hf, P * hh:P * hh + P], TT[:, 4 * hf + hh, :], ident[:])
                    ins.then_inc(s_tn, 1)
                for l in range(1, 6):
                    for hf in range(2):
                        n = 10 * gi + 2 * (l - 1) + hf
                        pe.wait_ge(s_nm, n + 1)
                        if l == 1:
                            pe.wait_ge(s_tnev, 2 * gi + hf + 1)
                        else:
                            pe.wait_ge(s_up, n - 1)
                        for hh in range(4):
                            ins = mm(PS[:, hf, P * hh:P * hh + P], Nm[:, hf, hh, :], Tn[:, 4 * hf + hh, :], start=True, stop=True)
                        ins.then_inc(s_lx, 1)
                    for hf in range(2):
                        n = 10 * gi + 2 * (l - 1) + hf
                        pe.wait_ge(s_xs, n + 1)
                        for hh in range(4):
                            h = 4 * hf + hh
                            if l < 5:
                                mm(PS[:, 2 + hf, P * hh:P * hh + P], TT[:, h, :], Xs[:, h, :], start=True, stop=True)
                            ins = mm(PS[:, 4 + hf, P * hh:P * hh + P], Xs[:, h, :], TT[:, h, :], start=True, stop=True)
                        ins.then_inc(s_ly, 1)
                    if l == 1:
                        pe.wait_ge(s_akvev, gi + 1)
                    fill(5 * gi + l - 1)
                for hf in range(2):
                    pe.wait_ge(s_up, 10 * gi + 9 + hf)
                    for hh in range(4):
                        h = 4 * hf + hh
                        ins = mm(PS[:, hf, P * hh:P * hh + P], TT[:, h, :], AX[:, h, :], start=True, stop=True)
                    ins.then_inc(s_w1, 1)
                pe.wait_ge(s_w1ev, 2 * gi + 2)
                for h in range(H):
                    j, o_ = head(h)
                    ins = mm(PS[o_:o_ + HD, 2, P * j:P * j + P], X12[:, h, 0:HD], NR[:, h, P:2 * P], start=True, stop=True)
                ins.then_inc(s_y1, 1)
                for c in range(2):
                    r = slice(CH * c, CH * c + CH)
                    for h in range(H):
                        j, o_ = head(h)
                        ins = mm(PS[o_:o_ + HD, 3 + c, HD * j:HD * j + HD], X12[r, h, 0:HD], bN[r, h, :], start=True, stop=True)
                ins.then_inc(s_y1, 1)
                for f in (5 * gi + 3, 5 * gi + 4):
                    by_act, n = taken(f)
                    pe.wait_ge(s_fill_act if by_act else s_fill_dve, n)
                for c in range(2):
                    r = slice(CH * c, CH * c + CH)
                    for h in range(H):
                        j, o_ = head(h)
                        out = PS[o_:o_ + HD, 5 + c, HD * j:HD * j + HD]
                        mm(out, bN[r, h, :], X12[r, h, HD:P], start=True, stop=False)
                        ins = mm(out, kN[r, h, :], vN[r, h, :], start=False, stop=True)
                ins.then_inc(s_z, 1)
                for h in range(H):
                    j, o_ = head(h)
                    out = PS[o_:o_ + HD, 7, P * j:P * j + P]
                    mm(out, X12[:, h, HD:P], NR[:, h, P:2 * P], start=True, stop=False)
                    ins = mm(out, vN[:, h, :], AK[:, h, P:2 * P], start=False, stop=True)
                ins.then_inc(s_ya, 1)
                pe.wait_ge(s_y1ev, 2 * gi + 2)
                for c in range(2):
                    cc = 2 * gi + c
                    s_in = cc if cc < 5 else 6
                    if c:
                        pe.wait_ge(s_stt, cc)
                    for h in range(H):
                        j, o_ = head(h)
                        ins = mm(PS[o_:o_ + HD, c, HD * j:HD * j + HD], MT[o_:o_ + HD, c, j, :], states[o_:o_ + HD, s_in, j, :],
                                 start=True, stop=True)
                    ins.then_inc(s_ms, 1)
                    for h in range(H):
                        j, o_ = head(h)
                        ins = mm(PS[o_:o_ + HD, 2 + c, CH * j:CH * j + CH], states[o_:o_ + HD, s_in, j, :],
                                 Y1[o_:o_ + HD, j, CH * c:CH * c + CH], start=True, stop=True)
                    ins.then_inc(s_y, 1)

            FOX, RWKV = range(0, NJ), range(NJ, KT)
            pe.wait_ge(s_stt, 2 * NG)
            pe.wait_ge(s_yev, 2 * NG)
            mm(PS[:, 6, :].rearrange("p (j t) -> p j t", j=NJ), blk[:], AR[:, 0, :, P * (NG - 1):TC], start=True,
               stop=True).then_inc(s_fill, 1)
            pe.wait_ge(s_mxl, NJ + NG - 1)
            item(I_WO, MXh, MXl, ks=FOX)
            pe.wait_ge(s_gsq, NG)
            mm(PS[:, 7, :], blk[:], GSQ[:].rearrange("p j t -> p (j t)"), start=True, stop=True).then_inc(s_fill, 1)
            item(I_WO + 1, MXh, MXl, ks=FOX)

            pe.wait_ge(s_mxl, NJ + NG)
            for i in range(I_WO, I_WQ):
                if i - I_WO >= 2:
                    pe.wait_ge(s_wo, i - I_WO - 1)
                    item(i, MXh, MXl)
                else:
                    item(i, MXh, MXl, ks=RWKV)
                if i > I_WO:
                    pe.wait_ge(s_wo, i - I_WO)
                    mean_part(1, i - I_WO - 1, X1, ones)
            pe.wait_ge(s_wo, KT)
            mean_part(1, KT - 1, X1, ones)
            variance(1, SQ1, ones)

            for i in range(I_WQ, N_ITEMS):
                if i - I_WQ >= 2:
                    pe.wait_ge(s_qev, i - I_WQ - 1)
                item(i, H1h, H1l, ready=s_h1l if i == I_WQ else None)
            pe.wait_ge(s_qev, 2 * PH)
            for tt, t0 in enumerate((0, P, T - P)):
                for k4 in range(4):
                    k = 4 * tt + k4
                    if k >= 2:
                        pe.wait_ge(s_scev, k - 1)
                    for x in range(4):
                        q = 4 * k4 + x
                        ins = mm(PS[:, 2 + k % 2, P * x:P * x + P], QT[:, q, t0:t0 + P], kst[:, q % 2, :], start=True, stop=True)
                    ins.then_inc(s_scp, 1)

            def up(e, slot):
                for x in range(4):
                    pe.wait_ge(s_hlo2, e * 4 + (x + 1))
                    if x == 0 and not (isinstance(e, int) and e < 4):
                        pe.wait_ge(s_gelu, e - 3)
                    lo_ = hlo[(2 * slot + x // 2) % 4]
                    for kk in range(2):
                        k = 2 * x + kk
                        ins = three(PS[:, slot % 4, 0:T], hhiq[x][:, P * kk:P * kk + P], lo_[:, P * (k % 4):P * (k % 4) + P],
                                    H1h[:, k, :], H1l[:, k, :], k == 0, k == KT - 1)
                    ins.then_inc(s_up_mm, 1)

            pe.wait_ge(s_scev, 12)
            for e in range(RIT):
                up(e, e)
            with pe.Fori(1, 3 * PH) as k:
                for e in range(RIT):
                    up(k * 4 + e, e)
            pe.wait_ge(s_routed, 1)
            pe.wait_ge(s_rconst, 1)
            for x, src in enumerate((sel1, sel2, best)):
                if x == 2:
                    pe.wait_ge(s_routed, 2)
                for tt in range(3):
                    ins = nc.tensor.transpose(PS[:, 4 + x, P * tt:P * tt + P],
                                              src[:, PH * tt:PH * tt + PH, :].rearrange("p h k -> p (h k)"), identb[:])
                ins.then_inc(s_pt, 1)
            with pe.Fori(3 * PH, NI // RIT) as k:
                for e in range(RIT):
                    up(k * 4 + e, e)

            def grid(g_, q):
                pe.wait_ge(s_oha, g_ + 1)
                pe.wait_ge(s_ohb, g_ + 1)
                if not isinstance(g_, int):
                    pe.wait_ge(s_w, g_ - (GIT - 1))
                for x in range(4):
                    ins = mm(PS[:, 2 + q, P * x:P * x + P], ohA[:, q % 3, x, :], ohB[:, q % 3, x, :], start=True, stop=True)
                ins.then_inc(s_grid, 1)

            pe.wait_ge(s_gelu, NI)
            for q in range(GIT):
                grid(q, q)
            with pe.Fori(1, T // (4 * GIT)) as k:
                for q in range(GIT):
                    grid(k * GIT + q, q)

            def down(e, s, start, stop):
                pe.wait_ge(s_wl, e + 1)
                for b in range(2):
                    pe.wait_ge(s_vlo, e * 2 + (b + 1))
                    for kk in range(4):
                        ins = three(PS[:, 4 * b + kk, 0:T], hhi[b][:, P * kk:P * kk + P], hlo[2 * s + b][:, P * kk:P * kk + P],
                                    Wh[s][:], Wl[s][:], start, stop)
                    ins.then_inc(s_down, 1)

            pe.wait_ge(s_w, T // 4)
            for e in range(2):
                down(e, e, e == 0, False)
            with pe.Fori(1, NI // 2 - 1) as k:
                for e in range(2):
                    down(k * 2 + e, e, False, False)
            for e in range(NI - 2, NI):
                down(e, e % 2, False, e == NI - 1)
            pe.wait_ge(s_onesg, 2)
            pe.wait_ge(s_xf, 2)
            for j in range(KT):
                pe.wait_ge(s_xf, j + 1)
                mean_part(2, j, XF, ones2)
            variance(2, SQF, ones2)

        @block.vector
        def _(dve):
            v = nc.vector
            n = [0]

            def own(ins):
                n[0] += 1
                ins.then_inc(s_dve, 1)
                dve.wait_ge(s_dve, n[0])

            def tt(out, a, b, op):
                return v.tensor_tensor(out, a, b, op)

            def norm_center(n, X):
                dve.wait_ge(s_mean, n + 1)
                for k in NORM_ORDER[n]:
                    tt(X[:, k, :], X[:, k, :], PS[:, MEAN_BANK, 0:T], ALU.subtract).then_inc(s_xc, 1)

            def norm_apply(n, X, out, sd, g_, b_, lo=None):
                dve.wait_ge(s_sd, n + 1)
                own(v.reciprocal(sd[:], sd[:]))
                dve.wait_ge(s_xc, KT * n + KT)
                for j in range(KT + 3 if lo else KT + 1):
                    if j < KT:
                        tt(X[:, j, :], X[:, j, :], sd[:], ALU.mult).then_inc(s_nr, 1)
                    if 1 <= j <= KT:
                        dve.wait_ge(s_nr, KT * n + j)
                        v.tensor_scalar(out[:, j - 1, :], X[:, j - 1, :], col(g_, j - 1), col(b_, j - 1), ALU.mult,
                                        ALU.add).then_inc(s_ln, 1)
                    if lo and j >= 3:
                        dst, hi, hi_done, done = lo
                        dve.wait_ge(s_ln, KT * n + j - 2)
                        dve.wait_ge(hi_done, j - 2)
                        tt(dst[:, j - 3, :], out[:, j - 3, :], hi[:, j - 3, :].bitcast(F32), ALU.subtract).then_inc(done, 1)

            def wlo_of(i):
                dve.wait_ge(s_whi, i + 1)
                tt(wlo[i % RAWS][:], raw[i % RAWS][:], whi[i % HIS][:].bitcast(F32), ALU.subtract).then_inc(s_wlo, 1)

            dve.wait_ge(s_cols, 16)
            norm_center(0, xin)
            wlo_of(0)
            norm_apply(0, xin, hT, SD, "ln_in_g", "ln_in_b", (hTl, hTh, s_hhi, s_hlo))
            dve.wait_ge(s_wfh, 1)
            tt(wfl[:], wfs[:], wfh[:].bitcast(F32), ALU.subtract).then_inc(s_wfl, 1)
            wlo_of(1)
            dve.wait_ge(s_f, 1)
            own(v.tensor_scalar(lf[:, 0, :], PS[0:H, 2, 0:T], col("b_f", rows=H), None, ALU.add))
            v.scalar_tensor_tensor(lf[:, 1, :], lf[:, 0, :], -1.0, lf[:, 0, :], ALU.mult, ALU.max).then_inc(s_fz, 1)
            dve.wait_ge(s_fe, 1)
            v.scalar_tensor_tensor(lf[:, 2, :], lf[:, 0, :], 0.0, lf[:, 1, :], ALU.min, ALU.subtract).then_inc(s_logf, 1)

            def maxima(u):
                rows, keys, _ = unit_shape(UNITS[u])
                dve.wait_ge(s_sc, u + 1)
                b = 2 if UNITS[u][0] == "s" else 2 + u % 2
                own(v.reduce_max(st[0:rows, u % 2, 0:1], flat(PS, 512 * b, keys)[0:rows], AX_X))
                v.tensor_scalar(st[0:rows, u % 2, 1:2], st[0:rows, u % 2, 0:1], -1.0, None, ALU.mult).then_inc(s_max, 1)

            def probabilities(u):
                rows, keys, _ = unit_shape(UNITS[u])
                dve.wait_ge(s_exp, u + 1)
                own(v.reciprocal(st[0:rows, u % 2, 3:4], st[0:rows, u % 2, 2:3]))
                v.tensor_scalar(pr[0:rows, u % 2, 0:keys], pr[0:rows, u % 2, 0:keys], st[0:rows, u % 2, 3:4], None,
                                ALU.mult).then_inc(s_norm, 1)

            r_, k_, v_ = (xm[:, NJ * x:NJ * x + NJ, :] for x in range(3))

            def channels(r):
                if r == 3:
                    dve.wait_ge(s_loev, 8)
                    own(v.memset(AR[:, 0, :, TP:PADP], 0.0))
                    for j in range(NJ):
                        ins = v.tensor_tensor_scan(LS[:, j, :], keep[:], AR[:, 0, j, :], 0.0, ALU.mult, ALU.add)
                    ins.then_inc(s_ls, 1)
                    dve.wait_ge(s_ls, 1)
                    tt(AR[:, 0, :, :], LS[:], AR[:, 0, :, :], ALU.subtract).then_inc(s_lprev, 1)
                if 4 <= r < 4 + NJ:
                    j = r - 4
                    dve.wait_ge(s_n2, j + 1)
                    v.tensor_scalar(BH[j][:], PS[:, 7, 0:TC], float(HD), 1e-24, ALU.mult,
                                    ALU.max).then_inc(s_n2m, 1)
                    dve.wait_ge(s_n2m, j + 1)
                    v.reciprocal(BH[j][:], BH[j][:]).then_inc(s_rn, 1)
                if r == 8:
                    for j in range(NJ):
                        ins = v.tensor_scalar(v_[:, j, :], AA[:, j, :], 1.0, col("k_a", j), ALU.subtract, ALU.mult)
                    own(ins)
                if r == 9:
                    dve.wait_ge(s_kkrt, NJ)
                    for j in range(NJ):
                        ins = v.scalar_tensor_tensor(BH[j][:], k_[:, j, :], col("k_k", j), BH[j][:], ALU.mult, ALU.mult)
                    own(ins)
                    own(v.scalar_tensor_tensor(k_, v_, 1.0, k_, ALU.add, ALU.mult))
                if r == 10:
                    dve.wait_ge(s_dprev, 2)
                    for j in range(NJ):
                        ins = v.scalar_tensor_tensor(AR[:, 0, j, :], BH[j][:], -1.0, AR[:, 0, j, :], ALU.mult, ALU.mult)
                    own(ins)
                    dve.wait_ge(s_d, 1)
                    own(v.tensor_copy(DL[:], AR[:, 1, :, CH - 1:TC:CH]))
                    own(tt(AR[:, 1, :, :], AR[:, 1, :, :], r_, ALU.mult))
                if r == 11:
                    for j in range(NJ):
                        ins = tt(BH[j][:], BH[j][:], AA[:, j, :], ALU.mult)
                    own(ins)
                if r == 12:
                    for j in range(NJ):
                        ins = tt(BH[j][:], BH[j][:], LS[:, j, :], ALU.mult)
                    own(ins)
                if r == 13:
                    for j in range(NJ):
                        v.scalar_tensor_tensor(r_[:, j, :], r_[:, j, :], col("r_k", j), k_[:, j, :], ALU.mult, ALU.mult)
                    tt(LS[:], k_, LS[:], ALU.mult).then_inc(s_prep, 1)

            for i in range(I_WO):
                if 1 <= i < I_RW - 1:
                    wlo_of(i + 1)
                if i == V_ITEMS - 1:
                    dve.wait_ge(s_logf, 1)
                    dve.wait_ge(s_const, 1)
                    dve.wait_ge(s_cache, 80)
                    own(v.tensor_copy(lfs[:, 0, PAST:KEYS], lf[:, 2, TP:T]))
                    v.tensor_tensor_scan(lf[:, 3, 0:TP], ones8[:, 0:TP], lf[:, 2, 0:TP], 0.0, ALU.mult, ALU.add)
                    v.tensor_tensor_scan(lfs[:, 1, :], ones8[:], lfs[:, 0, :], 0.0, ALU.mult, ALU.add).then_inc(s_logf, 1)
                if i >= I_RW:
                    r = i - I_RW
                    t = RW_ORDER[r]
                    maxima(2 * r)
                    probabilities(2 * r)
                    maxima(2 * r + 1)
                    dve.wait_ge(s_pev, i - I_K + 1)
                    dve.wait_ge(s_state, r + 1)
                    s = pb[:, r % 3, :]
                    own(tt(xm[:, t, :], s[:, 0:TC], s[:, 1:TC + 1], ALU.subtract))
                    own(v.scalar_tensor_tensor(xm[:, t, :], xm[:, t, :], col("mix", t), s[:, 1:TC + 1], ALU.mult, ALU.add))
                    v.memset(xm[:, t, TP:PADP], 0.0).then_inc(s_xm, 1)
                    probabilities(2 * r + 1)
                    dve.wait_ge(s_xm, r + 1)
                    channels(r)
            dve.wait_ge(s_prep, 1)
            dve.wait_ge(s_pv, NU)
            dve.wait_ge(s_oev, NU)
            dve.wait_ge(s_out, 16 * (NQB + 4))

            def head_norm(x, finish):
                for a, _, w in chunk_tokens(x):
                    t = slice(a, a + w)
                    y = AR[:, 0, :, t]
                    if not finish:
                        ins = v.reciprocal(GSD[:, :, a - P * x:a - P * x + w], GSD[:, :, a - P * x:a - P * x + w])
                        continue
                    own(tt(y, y, GSD[:, :, a - P * x:a - P * x + w], ALU.mult))
                    for j in range(NJ):
                        ins = v.tensor_scalar(AR[:, 0, j, t], AR[:, 0, j, t], col("lnx_g", j), col("lnx_b", j), ALU.mult,
                                              ALU.add)
                    own(ins)
                    own(tt(y, y, AA[:, :, t], ALU.add))
                    ins = tt(y, y, xm[:, NJ:2 * NJ, t], ALU.mult)
                return ins

            def trailing(x):
                for a, z, w in chunk_tokens(x):
                    ins = tt(MXl[:, NJ:KT, z:z + w], AR[:, 0, :, a:a + w], MXh[:, NJ:KT, z:z + w].bitcast(F32), ALU.subtract)
                ins.then_inc(s_mxl, 1)

            def fill(f):
                kind, x = kind_of(f)
                if kind:
                    dve.wait_ge(s_fill, f + 1)
                b = PS[:, 6 + f % 2, :]
                if kind == "B":
                    c = slice(512 * x, 512 * x + 512)
                    v.scalar_tensor_tensor(AA[:].rearrange("p j t -> p (j t)")[:, c], b, float(HD),
                                           v_.rearrange("p j t -> p (j t)")[:, c], ALU.mult, ALU.mult).then_inc(s_fill_dve, 1)
                if kind == "M":
                    y = AR[:, 0, :, P * x:P * x + P]
                    tt(y, y, b.rearrange("p (j t) -> p j t", j=NJ), ALU.subtract).then_inc(s_fill_dve, 1)
                if kind == "V":
                    dve.wait_ge(s_fill_act, taken(f)[1])
                    own(head_norm(x, False))
                if kind == "F":
                    dve.wait_ge(s_fill_act, taken(f)[1])
                    own(v.reciprocal(FSQ[:, x, :], FSQ[:, x, :]))
                    own(tt(oT[:, x, :], oT[:, x, :], FSQ[:, x, :], ALU.mult))
                    v.tensor_scalar(oT[:, x, :], oT[:, x, :], col("fnorm", x), None, ALU.mult).then_inc(s_fn, 1)
                kind, x = kind_of(f - 1)
                if kind == "V":
                    dve.wait_ge(s_fill_dve, taken(FILL.index("B2"))[1])
                    head_norm(x, True).then_inc(s_gy, 1)
                if kind == "F":
                    dve.wait_ge(s_fn, x + 1)
                    dve.wait_ge(s_mxh, hi_count(f - 1))
                    tt(MXl[:, x, :], oT[:, x, :], MXh[:, x, :].bitcast(F32), ALU.subtract).then_inc(s_mxl, 1)
                kind, x = kind_of(f - 2)
                if kind == "V":
                    dve.wait_ge(s_gy, x + 1)
                    dve.wait_ge(s_mxh, hi_count(f - 2))
                    trailing(x)

            for gi in range(NG):
                for hf in range(2):
                    for x, dst in enumerate((NR, AK)):
                        dve.wait_ge(s_A, 4 * gi + 2 * hf + x + 1)
                        if gi and hf == 0 and x == 0:
                            dve.wait_ge(s_ya, gi)
                        for b in range(2):
                            h0 = 4 * hf + b
                            ins = tt(dst[:, h0:h0 + 3:2, :], PS[:, 2 * x + b, :].rearrange("p (h c) -> p h c", c=2 * P),
                                     over(causal[:], 2), ALU.mult)
                        ins.then_inc(s_Aev, 1)
                    dve.wait_ge(s_Aev, 4 * gi + 2 * hf + 1)
                    hs = slice(4 * hf, 4 * hf + 4)
                    own(tt(TT[:, hs, :], NR[:, hs, 0:P], over(lev[:, 0, :], 4), ALU.mult))
                    tt(TT[:, hs, :], TT[:, hs, :], over(ident[:], 4), ALU.add).then_inc(s_tt, 1)
                for l in range(1, 6):
                    for hf in range(2):
                        hs = slice(4 * hf, 4 * hf + 4)
                        dve.wait_ge(s_ly, 10 * gi + 2 * (l - 1) + hf + 1)
                        if l == 1:
                            dve.wait_ge(s_tt, 2 * gi + hf + 1)
                            dve.wait_ge(s_tnev, 2 * gi + hf + 1)
                        if l < 5:
                            tt(Tn[:, hs, :], Tn[:, hs, :], PS[:, 2 + hf, :].rearrange("p (h c) -> p h c", c=P), ALU.add)
                        tt(TT[:, hs, :], TT[:, hs, :], PS[:, 4 + hf, :].rearrange("p (h c) -> p h c", c=P),
                           ALU.add).then_inc(s_up, 1)
                    if l < 5:
                        dve.wait_ge(s_up, 10 * gi + 2 * l)
                    fill(5 * gi + l - 1)

                dve.wait_ge(s_y1, 2 * gi + 1)
                tt(Y1[:], PS[:, 2, :].rearrange("p (j t) -> p j t", j=NJ), AR[:, 1, :, P * gi:P * gi + P],
                   ALU.add).then_inc(s_y1ev, 1)
                dve.wait_ge(s_y1, 2 * gi + 2)
                for c in range(2):
                    ins = tt(MT[:, c, :, :], PS[:, 3 + c, 0:NJ * HD].rearrange("p (j k) -> p j k", k=HD), over(eye2[:], NJ),
                             ALU.add)
                ins.then_inc(s_y1ev, 1)
                dve.wait_ge(s_z, gi + 1)
                for c in range(2):
                    ins = tt(Zs[:, c, :, :], PS[:, 5 + c, 0:NJ * HD].rearrange("p (j v) -> p j v", j=NJ),
                             along(DL[:, :, 2 * gi + c], HD), ALU.mult)
                ins.then_inc(s_zev, 1)
                dve.wait_ge(s_zev, gi + 1)
                dve.wait_ge(s_yaev, gi + 1)
                for c in range(2):
                    cc = 2 * gi + c
                    s_to = cc + 1 if cc < 5 else 7
                    dve.wait_ge(s_ms, cc + 1)
                    own(tt(states[:, s_to, :, :], PS[:, c, 0:NJ * HD].rearrange("p (j v) -> p j v", j=NJ),
                           along(DL[:, :, cc], HD), ALU.mult))
                    tt(states[:, s_to, :, :], states[:, s_to, :, :], Zs[:, c, :, :], ALU.add).then_inc(s_stt, 1)
                    dve.wait_ge(s_y, cc + 1)
                    y = AR[:, 0, :, CH * cc:CH * cc + CH]
                    tt(y, y, PS[:, 2 + c, 0:NJ * CH].rearrange("p (j t) -> p j t", j=NJ), ALU.add).then_inc(s_yev, 1)

            dve.wait_ge(s_yev, 2 * NG)
            fill(len(FILL))
            dve.wait_ge(s_fill, len(FILL) + 1)
            y = AR[:, 0, :, P * (NG - 1):TC]
            tt(y, y, PS[:, 6, :].rearrange("p (j t) -> p j t", j=NJ), ALU.subtract).then_inc(s_gc, 1)
            dve.wait_ge(s_gc, 1)
            dve.wait_ge(s_fill_act, taken(len(FILL) - 1)[1] + 1)
            own(head_norm(NG - 1, False))
            head_norm(NG - 1, True).then_inc(s_gy, 1)
            dve.wait_ge(s_gy, NG)
            dve.wait_ge(s_mxh, NJ + NG)
            trailing(NG - 1)

            for i in range(I_WO, I_WQ):
                if I_WO + 2 <= i + 1 < I_WQ:
                    wlo_of(i + 1)
                dve.wait_ge(s_item, i + 1)
                v.scalar_tensor_tensor(X1[:, i - I_WO, :], hT[:, i - I_WO, :], ALPHA, PS[:, i % 2, 0:T], ALU.mult,
                                       ALU.add).then_inc(s_wo, 1)
            dve.wait_ge(s_wo, KT)
            norm_center(1, X1)
            wlo_of(I_WQ)
            norm_apply(1, X1, X1, SD, "ln1_g", "ln1_b", (H1l, H1h, s_h1h, s_h1l))
            for i in range(I_WQ + 1, N_ITEMS):
                wlo_of(i)

            def route(k, part):
                if part == 0 or part == 1:
                    tk, ix, knock = ((top1, ix1, knock1), (top2, ix2, knock2))[part]
                    s = unit_s[:, part * NK:part * NK + NK]
                    if part == 0:
                        step(v.tensor_copy(unit_s[:], scores[:, bass.ds(k * (2 * NK), 2 * NK)]))
                    step(v.max(tk[:, 0:8], s))
                    step(v.max_index(ix[:, 0:8], tk[:, 0:8], s))
                    step(v.match_replace(knock[:], tk[:, 0:8], s, LOW))
                elif part == 2 or part == 3:
                    tk, ix, knock, ixf = ((top1, ix1, knock1, ix1f), (top2, ix2, knock2, ix2f))[part - 2]
                    step(v.max(tk[:, 8:16], knock[:]))
                    step(v.max_index(ix[:, 8:16], tk[:, 8:16], knock[:]))
                    step(v.tensor_copy(ixf[:], ix[:]))
                elif part == 4:
                    step(tt(cand[:], along(top1[:], 16), over(top2[:], 16), ALU.add))
                    c = cand[:].rearrange("p a b -> p (a b)")
                    step(v.max(top[:, 0:8], c))
                    step(v.max_index(pos[:, 0:8], top[:, 0:8], c))
                elif part == 5:
                    c, ck = (t[:].rearrange("p a b -> p (a b)") for t in (cand, candk))
                    step(v.match_replace(ck, top[:, 0:8], c, LOW))
                    step(v.max(top[:, 8:16], ck))
                    step(v.max_index(pos[:, 8:16], top[:, 8:16], ck))
                    step(v.tensor_copy(bestk(best, k), top[:]))
                elif part == 6:
                    step(v.tensor_scalar(posh[:], pos[:], 4, None, ALU.logical_shift_right))
                    step(v.tensor_scalar(posl[:], pos[:], 15, None, ALU.bitwise_and))
                    step(v.tensor_copy(poshf[:], posh[:]))
                    step(v.tensor_copy(poslf[:], posl[:]))
                    step(tt(hit1[:], iota16[:], along(poshf[:], 16), ALU.is_equal))
                    step(tt(hit2[:], iota16[:], along(poslf[:], 16), ALU.is_equal))
                else:
                    step(tt(hit1[:], hit1[:], over(ix1f[:], 16), ALU.mult))
                    step(tt(hit2[:], hit2[:], over(ix2f[:], 16), ALU.mult))
                    step(v.tensor_reduce(bestk(sel1, k), hit1[:], AX_X, ALU.add))
                    step(v.tensor_reduce(bestk(sel2, k), hit2[:], AX_X, ALU.add))

            def bestk(t, k):
                return t[:].rearrange("p u k -> p (u k)")[:, bass.ds(k * 16, 16)]

            def step(ins):
                dve.drain()

            dve.wait_ge(s_scev, 12)
            dve.wait_ge(s_rconst, 1)
            with dve.Fori(0, 3 * PH) as k:
                for part in range(8):
                    route(k, part)
            v.tensor_copy(gsum[:], best[:, :, 0]).then_inc(s_routed, 1)
            dve.wait_ge(s_routed, 1)
            tt(best[:], best[:], along(gsum[:], 16), ALU.subtract).then_inc(s_gexp, 1)
            dve.wait_ge(s_gate, 1)
            own(v.tensor_reduce(gsum[:], best[:], AX_X, ALU.add))
            own(v.reciprocal(gsum[:], gsum[:]))
            tt(best[:], best[:], along(gsum[:], 16), ALU.mult).then_inc(s_routed, 1)
            for x, dst in enumerate((pair1, pair2, pairg)):
                dve.wait_ge(s_pt, x + 1)
                v.tensor_copy(dst[:, 0:2 * P], PS[:, 4 + x, 0:2 * P]).then_inc(s_pairs, 1)
                v.tensor_copy(dst[:, 2 * P:T], PS[:, 4 + x, 2 * P + 3 * P - T:3 * P]).then_inc(s_pairs, 1)

            def one_hots(g_, slot, tok):
                if g_ is not None:
                    dve.wait_ge(s_grid, g_)
                tt(ohB[:, slot, :, :], over(iotak[:], 4), along(pair2[:, tok], NK), ALU.is_equal).then_inc(s_ohr, 1)
                tt(ohA[:, slot, :, :], over(iotak[:], 4), along(pair1[:, tok], NK), ALU.is_equal).then_inc(s_oha, 1)

            def weigh(g_, q, tok):
                dve.wait_ge(s_grid, g_ + 1)
                w = W[:, :, tok].rearrange("p e t -> p t e")
                tt(w, PS[:, 2 + q % GIT, :].rearrange("p (t e) -> p t e", e=NI), w, ALU.mult).then_inc(s_w, 1)

            dve.wait_ge(s_up_mm, 4 * NI)
            dve.wait_ge(s_pairs, 6)
            dve.wait_ge(s_gelu, NI)
            for q in range(GIT):
                one_hots(q - 2 if q >= 3 else None, q % 3, bass.ds(4 * q, 4))
                if q >= 2:
                    weigh(q - 2, q - 2, bass.ds(4 * q - 8, 4))
            with dve.Fori(1, T // (4 * GIT)) as k:
                for q in range(GIT):
                    one_hots(k * GIT + (q - 2), q % 3, bass.ds(k * (4 * GIT) + 4 * q, 4))
                    weigh(k * GIT + (q - 2), q - 2, bass.ds(k * (4 * GIT) + (4 * q - 8), 4))
            for q in (-2, -1):
                weigh(T // 4 + q, q, bass.ds(T + 4 * q, 4))

            def down(e, s):
                dve.wait_ge(s_wh, e + 1)
                tt(Wl[s][:], W[:, bass.ds(e, 1), :].rearrange("p a t -> p (a t)"), Wh[s][:].bitcast(F32),
                   ALU.subtract).then_inc(s_wl, 1)
                for b in range(2):
                    dve.wait_ge(s_vhi, e * 2 + (b + 1))
                    tt(hlo[2 * s + b][:], hraw[2 * s + b][:], hhi[b][:].bitcast(F32), ALU.subtract).then_inc(s_vlo, 1)

            dve.wait_ge(s_w, T // 4)
            for e in range(2):
                down(e, e)
            with dve.Fori(1, NI // 2) as k:
                for e in range(2):
                    down(k * 2 + e, e)

            dve.wait_ge(s_down, 2 * NI)
            dve.wait_ge(s_h1s, 1)
            for k in NORM_ORDER[2]:
                v.scalar_tensor_tensor(XF[:, k, :], H1s[:, k, :], ALPHA, PS[:, k, 0:T], ALU.mult, ALU.add).then_inc(s_xf, 1)
            dve.wait_ge(s_xf, KT)
            norm_center(2, XF)
            norm_apply(2, XF, XF, SDF, "ln2_g", "ln2_b")


def kernel(**inputs):
    from concourse import bacc as _bacc
    from concourse.bass_utils import run_bass_kernel_spmd as _run

    a = {n: np.asarray(x) for n, x in inputs.items()}
    DR = H * HD
    RW = RW_TILES * P

    def tile(w, c):
        return w[:, c:c + P].reshape(KT, P, P).transpose(1, 0, 2).reshape(P, D)

    x = np.concatenate([a["meta_tokens"], a["x_prompt"][0], a["x_sample"][0]])
    w_in, w_out, w_q = a["w_in"][0], a["w_out"][0], a["peer_w_q"][0]
    wv = w_in[:, RW + 2 * DR:RW + 3 * DR]
    items = [wv[2 * P * i:2 * P * i + 2 * P].reshape(2, P, DR).transpose(1, 0, 2).reshape(P, D) for i in range(V_ITEMS)]
    items += [tile(w_in, RW + DR + P * j) for j in range(NJ)]
    items += [tile(w_in, RW + P * j) for j in range(NJ)]
    items += [tile(w_in, P * t) for t in RW_ORDER]
    w_out = np.concatenate([w_out[DR:], w_out[:DR]])
    items += [tile(w_out, P * t) for t in range(KT)]
    items += [tile(w_q, P * t) for t in range(2 * PH)]
    vectors = {"ln_in_g": a["ln_in_g"], "ln_in_b": a["ln_in_b"], "ln1_g": a["ln1_g"], "ln1_b": a["ln1_b"],
               "ln2_g": a["ln2_g"], "ln2_b": a["ln2_b"], "mix": a["rwkv_mix"], "w0": a["rwkv_w0"], "a0": a["rwkv_a0"],
               "k_k": a["rwkv_k_k"], "k_a": a["rwkv_k_a"], "r_k": a["rwkv_r_k"], "lnx_g": a["rwkv_lnx_g"],
               "lnx_b": a["rwkv_lnx_b"], "fnorm": a["fox_norm_g"], "shift": a["state_rwkv_shift"],
               "b_f": np.pad(a["fox_b_f"].reshape(-1), (0, P - H))}
    cols = np.concatenate([vectors[n].reshape(-1, P).T for n in COLS], axis=1)
    ins = {
        "xT": x.reshape(T, KT, P).transpose(2, 1, 0),
        "cols": cols,
        "wbig": np.stack(items),
        "wf": w_in[:, RW + 3 * DR:].reshape(KT, P, H).transpose(1, 0, 2).reshape(P, KT * H),
        "w2a2": np.concatenate([a["rwkv_w2"][0], a["rwkv_a2"][0]]),
        "g2": a["rwkv_g2"][0],
        "keysT": np.stack([a["peer_keys1"][0].T, a["peer_keys2"][0].T], axis=1),
        "ckT": a["cache_fox_k"][0, 0].transpose(2, 1, 0),
        "cv": a["cache_fox_v"][0, 0].reshape(PAST, DR),
        "clf": a["cache_fox_logf"][0, 0].T,
        "s0T": a["state_rwkv_wkv"][0, 0].reshape(NJ, 2, HD, HD).transpose(1, 3, 0, 2).reshape(P, NJ, HD),
        "uT": a["peer_u"][0].reshape(NK, NK, 2, 4, P).transpose(1, 2, 4, 3, 0).reshape(2 * NK, P, 512),
        "vE": a["peer_v"][0].reshape(NK, NK, 2, 512).transpose(1, 2, 0, 3).reshape(2 * NK, P, 512),
    }
    outs = {"yT": (P, KT, T), "wkvo": (P, 2, NJ, HD), "ko": (HD, H, T), "vpo": (TP, DR), "vso": (DEC, DR),
            "lfo": (H, T), "sho": (P, RW_TILES, 2)}
    nc = _bacc.Bacc("TRN2", target_bir_lowering=False, num_devices=1)
    arrays, args = {}, []
    for name, arr in ins.items():
        arrays[f"in_{name}"] = np.ascontiguousarray(arr)
        args.append(nc.dram_tensor(f"in_{name}", arr.shape, mybir.dt.from_np(arr.dtype), kind="ExternalInput").ap())
    for name, shape in outs.items():
        args.append(nc.dram_tensor(f"out_{name}", shape, F32, kind="ExternalOutput").ap())
    build(nc, *args)
    r = _run(nc, [arrays], core_ids=[0]).results[0]
    o = {n: np.asarray(r[f"out_{n}"]) for n in outs}

    y = o["yT"].transpose(2, 1, 0).reshape(T, D)
    sh = o["sho"].transpose(2, 1, 0).reshape(2, RW)
    wkv = o["wkvo"].reshape(2, HD, 2, NJ, HD).transpose(2, 3, 0, 4, 1).reshape(2, H, HD, HD)
    k = o["ko"].transpose(2, 1, 0)
    lf = o["lfo"].T
    one = (1, 1)
    return (y[N_META:TP].reshape(1, SEQ, D), y[TP:].reshape(1, DEC, D),
            sh[0].reshape(*one, 1, RW), wkv[0].reshape(*one, H, HD, HD), k[:TP].reshape(*one, TP, H, HD),
            o["vpo"].reshape(*one, TP, H, HD), lf[:TP].reshape(*one, TP, H),
            sh[1].reshape(*one, 1, RW), wkv[1].reshape(*one, H, HD, HD), k[TP:].reshape(*one, DEC, H, HD),
            o["vso"].reshape(*one, DEC, H, HD), lf[TP:].reshape(*one, DEC, H))
```

```python
from contextlib import ExitStack

import numpy as np

import concourse.bass as bass
from concourse import mybir

ALU = mybir.AluOpType
ACT = mybir.ActivationFunctionType
AX_X = mybir.AxisListType.X
F32 = mybir.dt.float32
F32R = mybir.dt.float32r
U32 = mybir.dt.uint32

P = 128
D = 1024
KT = D // P
N_META, SEQ, DEC, PAST = 16, 256, 64, 512
TP = N_META + SEQ
T = TP + DEC
H, HD = 8, 64
NJ = H * HD // P
RW_TILES = 14
CH = 64
PADP = -(-TP // CH) * CH
TC = PADP + DEC
NG = TC // P
QB = 104
NQB = -(-TP // QB)
KEYS = PAST + DEC
MEAN_BANK, VAR_BANK = 2, 3
A_BANKS = ((0, 2), (4, 0))
NORM_ORDER = [list(range(KT)), list(range(KT)), [2, 3, 0, 1, 4, 5, 6, 7]]
KX = HD + H
NK = 128
XQ = 4
PH = 8
ALPHA = 2.0 ** 0.25
LN_EPS = 1e-5
LNX_EPS = 64e-5
NEG = -1.0e30
NI = NK
RIT = 4
ROUTED = 23
GIT = 12
NGR = T // 4
OH_SLOTS, GRID_BANKS = 4, 6
LOW = -3.0e38
CDEC = -float(np.exp(-0.5))

COLS = {}
_n = 0
for _name, _w in (("ln_in_g", 8), ("ln_in_b", 8), ("ln1_g", 8), ("ln1_b", 8), ("ln2_g", 8), ("ln2_b", 8),
                  ("mix", 14), ("w0", 4), ("a0", 4), ("k_k", 4), ("k_a", 4), ("r_k", 4), ("lnx_g", 4),
                  ("lnx_b", 4), ("fnorm", 4), ("shift", 14), ("b_f", 1)):
    COLS[_name] = _n
    _n += _w
NCOL = _n

V_ITEMS, K_ITEMS, Q_ITEMS = 4, NJ, NJ
RW_ORDER = [12, 13, 4, 5, 6, 7, 0, 1, 2, 3, 8, 9, 10, 11]
I_K = V_ITEMS
I_Q = I_K + K_ITEMS
I_RW = I_Q + Q_ITEMS
I_WO = I_RW + RW_TILES
I_WQ = I_WO + KT
N_ITEMS = I_WQ + 2 * PH
RAWS, HIS = 3, 2
POOL_ITEMS = range(I_RW + 1, I_WO + 2)

PROMPT_UNITS = [("p", h, b) for h in range(H) for b in range(NQB)]
UNITS = (PROMPT_UNITS[:12] + [("s", 0, 0), ("s", 1, 0)] + PROMPT_UNITS[12:18] + [("s", 2, 0), ("s", 3, 0)]
         + PROMPT_UNITS[18:])
NU = len(UNITS)

FILL = ["G0", "G1", "F0", "G2", "F1", "G3", "M0", "B0", "B1", "B2", "V0", "M1", "F2", "V1", "F3"]


def taken(f):
    act = FILL[f][0] in "GVF"
    return act, sum((x[0] in "GVF") == act for x in FILL[:f + 1])


def kind_of(f):
    return (FILL[f][0], int(FILL[f][1])) if 0 <= f < len(FILL) else ("", 0)


def hi_count(f):
    when = sorted((g + (1 if x[0] == "F" else 2), x[0] == "V", g) for g, x in enumerate(FILL) if x[0] in "VF")
    return [g for _, _, g in when].index(f) + 1


def chunk_tokens(g):
    if g < NG - 1:
        return [(P * g, P * g, P)]
    return [(P * g, P * g, TP - P * g), (PADP, TP, DEC)]


def by_dve(g):
    return g % 3 == 2


def before(g):
    return g // 3 if by_dve(g) else 2 * (g // 3) + g % 3


def per(g):
    return GIT // 3 * (1 if by_dve(g) else 2)


def unit_shape(u):
    kind, a, b = u
    if kind == "s":
        return P, KEYS, [(0, 64)] + [(64 + P * i, P) for i in range(4)]
    rows = min(QB, TP - QB * b)
    tiles = [(QB * i, min(QB, TP - QB * i)) for i in range(b + 1)]
    return rows, sum(n for _, n in tiles), tiles


def build(nc, xT, cols, wbig, wf, w2a2, g2, keysT, ckT, cv, clf, s0T, uT, vE,
          yT, wkvo, ko, vpo, vso, lfo, sho):
    ctx = ExitStack()
    with ctx:
        BASE, SBUF_END = 16512, 229368
        MAIN = P * T * 4
        TAIL = BASE + MAIN

        def at(name, shape, off, dt=F32):
            return nc.alloc_sbuf_tensor_at(name, list(shape), dt, offset=off)

        class Region:

            def __init__(self, start, end):
                self.pos, self.end = start, end

            def put(self, name, shape, dt=F32):
                n = int(np.prod(shape[1:])) * 4
                n = -(-n // 32) * 32
                t = at(name, shape, self.pos, dt)
                self.pos += n
                assert self.pos <= self.end, (name, self.pos - self.end)
                return t

        def sem(name):
            return ctx.enter_context(nc.semaphore(name))

        tail = Region(TAIL, SBUF_END)
        colv = tail.put("colv", [P, NCOL])
        h1h_at = tail.pos
        H1h = tail.put("H1h", [P, KT, T], F32R)
        h1l_at = tail.pos
        H1l = tail.put("H1l", [P, KT, T], F32R)
        H1s = at("H1s", [P, KT, T], h1l_at)
        ring_at = tail.pos
        hraw = [tail.put(f"hraw{i}", [P, 512]) for i in range(4)]
        hlo = [at(f"hlo{i}", [P, 512], ring_at + 2048 * i, F32R) for i in range(4)]
        hhi_at = tail.pos
        hhi = [tail.put(f"hhi{i}", [P, 512], F32R) for i in range(2)]
        hhiq = [at(f"hhiq{i}", [P, 256], hhi_at + 1024 * i, F32R) for i in range(4)]
        pairs_at = tail.pos
        pair12 = tail.put("pair12", [P, 2, T])
        pair1, pair2 = pair12[:, 0, :], pair12[:, 1, :]
        pairg = tail.put("pairg", [P, T])
        iotak = tail.put("iotak", [P, NK])
        gridv = at("gridv", [P, 2, 4 * NK], h1h_at)
        hhv = hhi + [at(f"hhv{i}", [P, 512], h1h_at + 2048 * i, F32R) for i in range(2)]
        one_hots = Region(ring_at, pairs_at)
        oh = [one_hots.put(f"oh{i}", [P, 2, 4, NK]) for i in range(OH_SLOTS - 1)]
        oh.append(at("oh_last", [P, 2, 4, NK], h1h_at + KT // 2 * T * 4))
        wsplit = Region(pairs_at, SBUF_END)
        Wh = [wsplit.put(f"Wh{i}", [P, T], F32R) for i in range(2)]
        Wl = [wsplit.put(f"Wl{i}", [P, T], F32R) for i in range(2)]

        W = at("W", [P, NI, T], BASE)
        routing = Region(BASE + 3 * PH * RIT * T * 4, TAIL)
        scores = routing.put("scores", [P, 3 * 2 * PH * NK])
        top1 = routing.put("top1", [P, 16])
        top2 = routing.put("top2", [P, 16])
        ix1 = routing.put("ix1", [P, 16], U32)
        ix2 = routing.put("ix2", [P, 16], U32)
        ix1f = routing.put("ix1f", [P, 16])
        ix2f = routing.put("ix2f", [P, 16])
        knock1 = routing.put("knock1", [P, NK])
        knock2 = routing.put("knock2", [P, NK])
        cand = routing.put("cand", [P, 16, 16])
        candk = routing.put("candk", [P, 16, 16])
        pos = routing.put("pos", [P, 16], U32)
        posh = routing.put("posh", [P, 16], U32)
        posl = routing.put("posl", [P, 16], U32)
        poshf = routing.put("poshf", [P, 16])
        poslf = routing.put("poslf", [P, 16])
        hit1 = routing.put("hit1", [P, 16, 16])
        hit2 = routing.put("hit2", [P, 16, 16])
        iota16 = routing.put("iota16", [P, 16, 16])
        best = routing.put("best", [P, 3 * PH, 16])
        sel1 = routing.put("sel1", [P, 3 * PH, 16])
        sel2 = routing.put("sel2", [P, 3 * PH, 16])
        gsum = routing.put("gsum", [P, 3 * PH])
        identb = routing.put("identb", [P, P])
        unit_s = routing.put("unit_s", [P, 2 * NK])
        top = routing.put("top", [P, 16])
        last = Region(BASE, TAIL)
        ones2 = last.put("ones2", [P, P])
        XF = last.put("XF", [P, KT, T])
        SQF = last.put("SQF", [P, KT, T])
        SDF = last.put("SDF", [P, T])

        m = Region(BASE, TAIL)
        ident = m.put("ident", [P, P])
        ones = m.put("ones", [P, P])
        blk = m.put("blk", [P, P])
        causal = m.put("causal", [P, 2 * P])
        lev = m.put("lev", [P, 6, P])
        eye2 = m.put("eye2", [P, HD])
        amask = m.put("amask", [P, P])
        keep = m.put("keep", [P, TC])
        ones8_at = m.pos
        ones8 = m.put("ones8", [H, KEYS])
        w2s_at = m.pos
        w2s = m.put("w2s", [P, NJ * P])
        g2s = m.put("g2s", [P, NJ * P])
        wfl = at("wfl", [P, KT * H], m.pos, F32R)
        wfs = m.put("wfs", [P, KT * H])
        wfh = m.put("wfh", [P, KT * H], F32R)
        kst = m.put("kst", [P, 2, NK])
        hT = m.put("hT", [P, KT, T])
        xm = m.put("xm", [P, RW_TILES, TC])
        shs = m.put("shs", [P, RW_TILES, 2])
        states = m.put("states", [P, 8, NJ, HD])
        oT = m.put("oT", [P, NJ, T])
        SD = m.put("SD", [P, T])
        DL = m.put("DL", [P, NJ, TC // CH])
        att_at = m.pos
        lf = m.put("lf", [H, 4, T])
        lfs = m.put("lfs", [H, 2, KEYS])
        qx = m.put("qx", [KX, H, T])
        kx = m.put("kx", [KX, H, T])
        ckx = m.put("ckx", [KX, H, PAST])
        vp = m.put("vp", [P, NQB, H * HD])
        vs = m.put("vs", [P, 5, H * HD])
        pr = m.put("pr", [P, 2, KEYS])
        pt = m.put("pt", [P, 2, 5 * P])
        st = m.put("st", [P, 2, 4])
        att_end = m.pos
        xin = at("xin", [P, KT, T], att_at + 24576)
        SQ0 = at("SQ0", [P, KT, T], att_at + 24576 + KT * T * 4)
        g = Region(att_at, att_end)
        NR = g.put("NR", [P, H, 2 * P])
        AK = g.put("AK", [P, H, 2 * P])
        Tn = g.put("Tn", [P, H, P])
        TT = g.put("TT", [P, H, P])
        Xs = g.put("Xs", [P, H, P])
        Nm = g.put("Nm", [P, 2, H // 2, P])
        AX = g.put("AX", [P, H, P])
        X12 = g.put("X12", [P, H, P])
        bN = g.put("bN", [P, H, HD])
        kN = g.put("kN", [P, H, HD])
        vN = g.put("vN", [P, H, HD])
        Y1 = g.put("Y1", [P, NJ, P])
        MT = g.put("MT", [P, 2, NJ, HD])
        MXh = g.put("MXh", [P, KT, T], F32R)
        MXl = g.put("MXl", [P, KT, T], F32R)
        QT = at("QT", [P, 2 * PH, T], att_at)
        o = Region(att_at + 2 * PH * T * 4, att_end)
        X1 = o.put("X1", [P, KT, T])
        SQ1 = o.put("SQ1", [P, KT, T])
        assert o.pos <= g.pos - 2 * KT * T * 4
        wring_at = m.pos
        raw = [m.put(f"wraw{i}", [P, D]) for i in range(RAWS)]
        wlo = [at(f"wlo{i}", [P, D], wring_at + 4096 * i, F32R) for i in range(RAWS)]
        whi = [m.put(f"whi{i}", [P, D], F32R) for i in range(HIS)]
        AA = m.put("AA", [P, NJ, TC])
        Zs = at("Zs", [P, 2, NJ, HD], m.pos)
        pb = m.put("pb", [P, 3, TC + 1])
        BH = [m.put("BH0", [P, TC]), m.put("BH1", [P, TC]), at("BH2", [P, TC], w2s_at), at("BH3", [P, TC], ones8_at)]
        hTh = at("hTh", [P, KT, T], h1h_at, F32R)
        hTl = at("hTl", [P, KT, T], h1h_at + KT * T * 4, F32R)
        sq = Region(h1h_at, h1h_at + 2 * KT * T * 4)
        FSQ = sq.put("FSQ", [P, NJ, T])
        GSQ = sq.put("GSQ", [P, NJ, P])
        GSD = sq.put("GSD", [P, NJ, P])
        r2 = Region(sq.end, SBUF_END)
        AR = r2.put("AR", [P, 2, NJ, TC])
        LS = r2.put("LS", [P, NJ, TC])
        PS = ctx.enter_context(nc.psum_tensor("PS", [P, 8, 512], F32))

        s_cols, s_small, s_clf, s_cache, s_out = (sem(x) for x in ("s_cols", "s_small", "s_clf", "s_cache", "s_out"))
        s_x = [sem(f"s_x{i}") for i in range(XQ)]
        s_shift, s_state = sem("s_shift"), sem("s_state")
        s_raw = [sem(f"s_raw{i}") for i in range(RAWS)]
        s_whi, s_wlo, s_wlo_pool, s_item = (sem(x) for x in ("s_whi", "s_wlo", "s_wlo_pool", "s_item"))
        s_pool, s_dve, s_act = sem("s_pool"), sem("s_dve"), sem("s_act")
        s_const, s_onesg = sem("s_const"), sem("s_onesg")
        s_mean, s_xc, s_sq, s_var, s_sd, s_ln = (sem(x) for x in ("s_mean", "s_xc", "s_sq", "s_var", "s_sd", "s_ln"))
        s_hhi, s_hlo = sem("s_hhi"), sem("s_hlo")
        s_f, s_fz, s_fe, s_logf, s_negc = (sem(x) for x in ("s_f", "s_fz", "s_fe", "s_logf", "s_negc"))
        s_vev, s_pev, s_xm = sem("s_vev"), sem("s_pev"), sem("s_xm")
        s_sc, s_max, s_exp, s_norm, s_tr, s_tev, s_pv, s_oev = (
            sem(x) for x in ("s_sc", "s_max", "s_exp", "s_norm", "s_tr", "s_tev", "s_pv", "s_oev"))
        s_tanh, s_lora, s_loev = (sem(x) for x in ("s_tanh", "s_lora", "s_loev"))
        s_ls, s_d, s_lprev, s_dprev, s_kksq, s_n2, s_n2m, s_rn, s_kkrt, s_prep = (
            sem(x) for x in ("s_ls", "s_d", "s_lprev", "s_dprev", "s_kksq", "s_n2", "s_n2m", "s_rn", "s_kkrt", "s_prep"))
        s_fill, s_fill_act, s_fill_dve = (sem(x) for x in ("s_fill", "s_fill_act", "s_fill_dve"))
        s_nat, s_natev, s_A, s_Aev, s_tt, s_tn, s_tnev, s_nm, s_lx, s_xs, s_ly, s_up = (
            sem(x) for x in ("s_nat", "s_natev", "s_A", "s_Aev", "s_tt", "s_tn", "s_tnev", "s_nm", "s_lx", "s_xs",
                             "s_ly", "s_up"))
        s_akv, s_akvev, s_w1, s_w1ev, s_y1, s_y1ev, s_z, s_zev, s_ya, s_yaev, s_ms, s_stt, s_y, s_yev = (
            sem(x) for x in ("s_akv", "s_akvev", "s_w1", "s_w1ev", "s_y1", "s_y1ev", "s_z", "s_zev", "s_ya", "s_yaev",
                             "s_ms", "s_stt", "s_y", "s_yev"))
        s_gc, s_gsq, s_gy = (sem(x) for x in ("s_gc", "s_gsq", "s_gy"))
        s_osq, s_fn = sem("s_osq"), sem("s_fn")
        s_mxh, s_mxl, s_wo = sem("s_mxh"), sem("s_mxl"), sem("s_wo")
        s_h1h, s_h1l, s_qev, s_scp, s_scev = (sem(x) for x in ("s_h1h", "s_h1l", "s_qev", "s_scp", "s_scev"))
        s_rconst = sem("s_rconst")
        s_hraw = [sem(f"s_hraw{i}") for i in range(4)]
        s_hhi2, s_hlo2, s_up_mm, s_gelu = sem("s_hhi2"), sem("s_hlo2"), sem("s_up_mm"), sem("s_gelu")
        s_routed, s_gexp, s_gate, s_pt, s_pairs = (
            sem(x) for x in ("s_routed", "s_gexp", "s_gate", "s_pt", "s_pairs"))
        s_oh, s_ohb_act, s_ohb_pool, s_grid, s_gev, s_w_pool, s_w_dve = (
            sem(x) for x in ("s_oh", "s_ohb_act", "s_ohb_pool", "s_grid", "s_gev", "s_w_pool", "s_w_dve"))
        s_vraw = [sem(f"s_vraw{i}") for i in range(4)]
        s_vhi, s_vlo, s_wh, s_wl, s_down = (sem(x) for x in ("s_vhi", "s_vlo", "s_wh", "s_wl", "s_down"))
        s_sum, s_yf, s_h1s_dve = sem("s_sum"), sem("s_yf"), sem("s_h1s_dve")
        s_h1s, s_xf, s_wfh, s_wfl, s_nr = (sem(x) for x in ("s_h1s", "s_xf", "s_wfh", "s_wfl", "s_nr"))

        def col(name, k=0, n=1, rows=P):
            c = COLS[name] + k
            return colv[0:rows, c:c + n]

        def over(ap2, n):
            return ap2.unsqueeze(1).to_broadcast([ap2.shape[0], n, ap2.shape[1]])

        def along(ap2, n):
            return ap2.unsqueeze(2).to_broadcast([ap2.shape[0], ap2.shape[1], n])

        def flat(t3, a, n):
            return t3[:].rearrange("p x y -> p (x y)")[:, a:a + n]

        def head(h):
            return h // 2, HD * (h % 2)

        def scaled(k, n, c):
            return c if isinstance(k, int) else k * n + c

        def weighed(eng):
            eng.wait_ge(s_w_pool, NGR // 3 * 2)
            eng.wait_ge(s_w_dve, NGR // 3)

        block = ctx.enter_context(nc.Block())

        @block.sync
        def _(sp):
            sp.dma_start(colv[:], cols).then_inc(s_cols, 16)
            for q in range(XQ):
                ks = slice(KT // XQ * q, KT // XQ * (q + 1))
                sp.dma_start(xin[:, ks, :], xT[:, ks, :]).then_inc(s_x[q], 16)
            sp.dma_start(wfs[:], wf).then_inc(s_small, 16)
            sp.dma_start(w2s[:], w2a2).then_inc(s_small, 16)
            sp.dma_start(g2s[:], g2).then_inc(s_small, 16)
            sp.dma_start(kst[:], keysT).then_inc(s_small, 16)
            sp.dma_start(states[:, 6, :, :], s0T).then_inc(s_small, 16)

            def load(i):
                if i >= RAWS:
                    sp.wait_ge(s_item, i - RAWS + 1)
                sp.dma_start(raw[i % RAWS][:], wbig[i]).then_inc(s_raw[i % RAWS], 16)

            for i in range(I_RW):
                load(i)
                if i == RAWS - 1:
                    sp.wait_ge(s_ln, KT)
                    sp.dma_start(lfs[:, 0, 0:PAST], clf).then_inc(s_clf, 16)
            sp.wait_ge(s_vev, 4)
            for b in range(NQB):
                n = min(QB, TP - QB * b)
                sp.dma_start(vpo[QB * b:QB * b + n, :], vp[0:n, b, :]).then_inc(s_out, 16)
            sp.dma_start(vso, vs[HD:P, 4, :]).then_inc(s_out, 16)
            sp.wait_ge(s_pev, K_ITEMS)
            sp.dma_start(ko, kx[0:HD, :, :]).then_inc(s_out, 16)
            sp.wait_ge(s_logf, 1)
            sp.dma_start(lfo, lf[:, 2, :]).then_inc(s_out, 16)
            for i in range(I_RW, I_WO):
                load(i)
                if i == I_RW + 3:
                    sp.dma_start(ckx[0:HD, :, :], ckT).then_inc(s_cache, 16)
                    sp.dma_start(vs[0:HD, 0, :], cv[0:HD, :]).then_inc(s_cache, 16)
                    sp.dma_start(vs[:, 1:4, :], cv[HD:PAST - HD, :].rearrange("(i p) c -> p i c", p=P)).then_inc(s_cache, 16)
                    sp.dma_start(vs[0:HD, 4, :], cv[PAST - HD:PAST, :]).then_inc(s_cache, 16)
            sp.wait_ge(s_shift, RW_TILES)
            sp.dma_start(sho, shs[:]).then_inc(s_out, 16)
            for i in range(I_WO, N_ITEMS):
                load(i)
                if i == I_WO + RAWS - 1:
                    sp.wait_ge(s_stt, 6)
                    sp.dma_start(wkvo[:, 0], states[:, 5, :, :]).then_inc(s_out, 16)
                    sp.dma_start(wkvo[:, 1], states[:, 7, :, :]).then_inc(s_out, 16)

            sp.wait_ge(s_gy, 3)
            sp.wait_ge(s_mxl, NJ + NG)
            for q in range(4):
                sp.dma_start(hraw[q][:], uT[q]).then_inc(s_hraw[q], 16)
            with sp.Fori(1, 2 * NI // 4) as k:
                for q in range(4):
                    sp.wait_ge(s_up_mm, k * 8 + (2 * q - 6))
                    sp.dma_start(hraw[q][:], uT[bass.ds(k * 4 + q, 1)].rearrange("a p c -> (a p) c")).then_inc(s_hraw[q], 16)
            sp.wait_ge(s_grid, NGR)
            for q in range(4):
                sp.dma_start(hraw[q][:], vE[q]).then_inc(s_vraw[q], 16)
            with sp.Fori(1, 2 * NI // 4) as k:
                for q in range(4):
                    sp.wait_ge(s_down, k * 4 + (q - 3))
                    sp.dma_start(hraw[q][:], vE[bass.ds(k * 4 + q, 1)].rearrange("a p c -> (a p) c")).then_inc(s_vraw[q], 16)
            for q in range(4):
                sp.wait_ge(s_yf, 2 * q + 2)
                sp.dma_start(yT[:, 2 * q:2 * q + 2, :], XF[:, 2 * q:2 * q + 2, :]).then_inc(s_out, 16)
            sp.wait_ge(s_out, 16 * (NQB + 1 + 1 + 1 + 1 + 2 + 4))

        @block.gpsimd
        def _(pool):
            n = [0]

            def own(ins):
                n[0] += 1
                ins.then_inc(s_pool, 1)
                pool.wait_ge(s_pool, n[0])

            def select(t, pattern, op, base, cm, fill):
                own(nc.gpsimd.affine_select(out=t, in_=t, pattern=pattern, compare_op=op, fill=fill, base=base,
                                            channel_multiplier=cm))

            nc.gpsimd.memset(ones[:], 1.0 / D).then_inc(s_onesg, 1)
            own(nc.gpsimd.memset(ident[:], 0.0))
            select(ident[:], [[-1, P]], ALU.not_equal, 0, 1, 1.0)
            own(nc.gpsimd.memset(blk[:], 0.0))
            for e in range(2):
                own(nc.gpsimd.memset(blk[HD * e:HD * e + HD, HD * e:HD * e + HD], 1.0 / HD))
            own(nc.gpsimd.memset(causal[:], 1.0))
            for e, base in ((0, -1), (1, 0)):
                c = causal[:, P * e:P * e + P]
                select(c, [[1, P]], ALU.is_ge, base, -1, 0.0)
                own(nc.gpsimd.memset(c[0:CH, CH:P], 0.0))
            own(nc.gpsimd.memset(lev[:], 0.0))
            for l in range(6):
                b = 1 << l
                v = lev[:, l, :].rearrange("p (g x b) -> p g x b", x=2, b=b)[:, :, 1, :]
                own(nc.gpsimd.memset(v, 1.0))
                pat = [[2 * b, P // (2 * b)], [0, b]]
                select(v, [[-2 * b, P // (2 * b)], [0, b]], ALU.is_ge, 0, 1, 0.0)
                select(v, pat, ALU.is_ge, b - 1, -1, 0.0)
            own(nc.gpsimd.memset(eye2[:], 0.0))
            select(eye2[:], [[-1, HD]], ALU.not_equal, 0, 1, 1.0)
            select(eye2[:], [[-1, HD]], ALU.not_equal, -HD, 1, 1.0)
            own(nc.gpsimd.memset(amask[:], 0.0))
            select(amask[:], [[-1, P]], ALU.is_ge, 0, 1, NEG)
            own(nc.gpsimd.memset(keep[:], 1.0))
            own(nc.gpsimd.memset(keep[:, 0:TC:CH], 0.0))
            own(nc.gpsimd.memset(ones8[:], 1.0))
            own(nc.gpsimd.memset(qx[HD:KX, :, :], 0.0))
            select(qx[HD:KX, :, :], [[-1, H], [0, T]], ALU.not_equal, 0, 1, 1.0)
            own(nc.gpsimd.memset(pb[:, :, 0:1], 0.0))
            own(nc.gpsimd.memset(pb[:, :, TP + 1:PADP], 0.0))
            own(nc.gpsimd.memset(states[:, 0, :, :], 0.0))
            nc.gpsimd.sem_inc(s_const, 1)

            pool.wait_ge(s_logf, 2)
            pool.wait_ge(s_ln, KT)
            for dst, src in ((kx[HD:KX, :, 0:TP], lf[:, 3, 0:TP]), (kx[HD:KX, :, TP:T], lfs[:, 1, PAST:KEYS]),
                             (ckx[HD:KX, :, :], lfs[:, 1, 0:PAST])):
                nc.gpsimd.tensor_scalar(dst, over(src, H), -1.0, 0.0, ALU.mult, ALU.add).then_inc(s_negc, 1)
            pool.wait_ge(s_negc, 3)

            def wlo_of(i):
                pool.wait_ge(s_whi, i + 1)
                nc.gpsimd.tensor_tensor(wlo[i % RAWS][:], raw[i % RAWS][:], whi[i % HIS][:].bitcast(F32),
                                        ALU.subtract).then_inc(s_wlo_pool, 1)

            for r in range(RW_TILES):
                if r >= 3:
                    pool.wait_ge(s_xm, r - 2)
                    pool.wait_ge(s_shift, r - 2)
                nc.gpsimd.tensor_copy(pb[:, r % 3, PADP:PADP + 1], col("shift", RW_ORDER[r])).then_inc(s_state, 1)
                if r + 1 < RW_TILES:
                    wlo_of(I_RW + r + 1)
                pool.wait_ge(s_pev, I_RW + r - I_K + 1)
                nc.gpsimd.tensor_copy(shs[:, RW_ORDER[r], :], pb[:, r % 3, TP:TC + 1:TC - TP]).then_inc(s_shift, 1)

            n_nm = 0
            for gi in range(NG):
                for l in range(1, 6):
                    for hf in range(2):
                        if l == 1:
                            pool.wait_ge(s_Aev, 4 * gi + 2 * hf + 1)
                        if n_nm >= 2:
                            pool.wait_ge(s_lx, n_nm - 1)
                        nc.gpsimd.tensor_tensor(Nm[:, hf, :, :], NR[:, 4 * hf:4 * hf + 4, 0:P], over(lev[:, l, :], 4),
                                                ALU.mult).then_inc(s_nm, 1)
                        n_nm += 1
            wlo_of(I_WO)
            wlo_of(I_WO + 1)

            def lo(c, q):
                pool.wait_ge(s_hhi2, c + 1)
                cols_ = slice(256 * (q % 2), 256 * (q % 2) + 256)
                nc.gpsimd.tensor_tensor(hlo[q // 2 % 4][:, cols_], hraw[q // 2 % 4][:, cols_], hhiq[q % 4][:].bitcast(F32),
                                        ALU.subtract).then_inc(s_hlo2, 1)

            for q in range(4):
                lo(q, q)
            pool.wait_ge(s_scp, 12)
            own(nc.gpsimd.memset(identb[:], 0.0))
            select(identb[:], [[-1, P]], ALU.not_equal, 0, 1, 1.0)
            own(nc.gpsimd.iota(iotak[:], pattern=[[1, NK]], base=0, channel_multiplier=0,
                               allow_small_or_imprecise_dtypes=True))
            own(nc.gpsimd.iota(iota16[:], pattern=[[0, 16], [1, 16]], base=0, channel_multiplier=0,
                               allow_small_or_imprecise_dtypes=True))
            nc.gpsimd.sem_inc(s_rconst, 1)

            for q in range(4, 4 * RIT):
                lo(q, q)
            with pool.Fori(1, NI // RIT) as k:
                for q in range(4 * RIT):
                    lo(k * (4 * RIT) + q, q)

            pool.wait_ge(s_up_mm, 4 * NI)
            k = slice(0, KT // 2)
            nc.gpsimd.tensor_tensor(H1s[:, k, :], H1h[:, k, :].bitcast(F32), H1l[:, k, :].bitcast(F32),
                                    ALU.add).then_inc(s_h1s, 1)

            def grids(k, q):
                g_ = q if by_dve(q) else q - 3
                if by_dve(q):
                    pool.wait_ge(s_oh, scaled(k, GIT, q + 1))
                    tok = bass.ds(scaled(k, 4 * GIT, 4 * q), 4)
                    nc.gpsimd.tensor_tensor(oh[q % OH_SLOTS][:, 1, :, :], oh[q % OH_SLOTS][:, 1, :, :], along(pairg[:, tok], NK),
                                            ALU.mult).then_inc(s_ohb_pool, 1)
                elif g_ >= 0 or not isinstance(k, int):
                    weigh(scaled(k, per(g_), before(g_) + 1), before(g_) % 2, scaled(k, 4 * GIT, 4 * g_))

            def weigh(n, slot, t0):
                pool.wait_ge(s_gev, n)
                w = W[:, :, bass.ds(t0, 4)].rearrange("p e t -> p t e")
                nc.gpsimd.tensor_tensor(w, gridv[:, slot, :].rearrange("p (t e) -> p t e", e=NI), w,
                                        ALU.mult).then_inc(s_w_pool, 1)

            pool.wait_ge(s_pairs, 6)
            pool.wait_ge(s_gelu, NI)
            for q in range(GIT):
                grids(0, q)
            with pool.Fori(1, NGR // GIT) as k:
                for q in range(GIT):
                    grids(k, q)
            for g_ in (NGR - 3, NGR - 2):
                weigh(before(g_) + 1, before(g_) % 2, 4 * g_)
            pool.wait_ge(s_down, 2)
            nc.gpsimd.memset(ones2[:], 1.0 / D).then_inc(s_onesg, 1)

        @block.scalar
        def _(act):
            n = [0]

            def own(ins):
                n[0] += 1
                ins.then_inc(s_act, 1)
                act.wait_ge(s_act, n[0])

            def A(out, in_, f, **kw):
                return nc.scalar.activation(out, in_, f, **kw)

            def norm_squares(n, X, S):
                for j, k in enumerate(NORM_ORDER[n]):
                    act.wait_ge(s_xc, KT * n + j + 1)
                    A(S[:, k, :], X[:, k, :], ACT.Square).then_inc(s_sq, 1)

            def norm_root(n, sd):
                act.wait_ge(s_var, n + 1)
                A(sd[:], PS[:, VAR_BANK, 0:T], ACT.Sqrt, bias=LN_EPS).then_inc(s_sd, 1)

            def whi_of(i):
                act.wait_ge(s_raw[i % RAWS], 16 * (i // RAWS + 1))
                if i >= HIS:
                    act.wait_ge(s_item, i - HIS + 1)
                A(whi[i % HIS][:], raw[i % RAWS][:], ACT.Copy).then_inc(s_whi, 1)

            def evacuate(i):
                if i < V_ITEMS:
                    if i == V_ITEMS - 1:
                        act.wait_ge(s_item, V_ITEMS)
                        for b in range(NQB):
                            A(vp[0:QB, b, :], PS[0:QB, 4 + b, :], ACT.Copy).then_inc(s_vev, 1)
                        A(vs[HD:P, 4, :], PS[HD:P, 3 + NQB, :], ACT.Copy).then_inc(s_vev, 1)
                    return
                act.wait_ge(s_item, i + 1)
                b = PS[:, i % 2, :]
                if i < I_RW:
                    dst, j, scale = (kx, i - I_K, 1.0) if i < I_Q else (qx, i - I_Q, HD ** -0.5)
                    A(dst[0:HD, 2 * j, :], b[0:HD, 0:T], ACT.Copy, scale=scale)
                    A(dst[0:HD, 2 * j + 1, :], b[HD:P, 0:T], ACT.Copy, scale=scale).then_inc(s_pev, 1)
                    return
                r = i - I_RW
                t = RW_ORDER[r]
                if r >= 3:
                    act.wait_ge(s_xm, r - 2)
                    act.wait_ge(s_shift, r - 2)
                s = pb[:, r % 3, :]
                A(s[:, 1:TP + 1], b[:, 0:TP], ACT.Copy)
                A(s[:, PADP + 1:TC + 1], b[:, TP:T], ACT.Copy).then_inc(s_pev, 1)

            def attention(s):
                if s < NU:
                    rows, keys, _ = unit_shape(UNITS[s])
                    act.wait_ge(s_max, s + 1)
                    if s >= 2:
                        act.wait_ge(s_tr, s - 1)
                    b = 2 if UNITS[s][0] == "s" else 2 + s % 2
                    A(pr[0:rows, s % 2, 0:keys], flat(PS, 512 * b, keys)[0:rows], ACT.Exp,
                      bias=st[0:rows, s % 2, 1:2], accum_out=st[0:rows, s % 2, 2:3]).then_inc(s_exp, 1)
                if 1 <= s <= NU:
                    u = s - 1
                    rows, _, tiles = unit_shape(UNITS[u])
                    act.wait_ge(s_tr, u + 1)
                    if u >= 2:
                        act.wait_ge(s_pv, u - 1)
                    b = 4 if UNITS[u][0] == "s" else 4 + u % 2
                    full = sum(w == QB for _, w in tiles)
                    parts = [(0, 1, 64), (1, 5, P)] if UNITS[u][0] == "s" else [(0, full, QB)] * (full > 0)
                    if UNITS[u][0] == "p" and full < len(tiles):
                        parts.append((full, full + 1, tiles[-1][1]))
                    for a, z, w in parts:
                        ins = A(pt[0:w, u % 2, P * a:P * z].rearrange("p (x r) -> p x r", r=P)[:, :, 0:rows],
                                flat(PS, 512 * b + P * a, P * (z - a))[0:w].rearrange("p (x r) -> p x r", r=P)[:, :, 0:rows],
                                ACT.Copy)
                    ins.then_inc(s_tev, 1)
                if s >= 2:
                    u = s - 2
                    kind, a, qb = UNITS[u]
                    act.wait_ge(s_pv, u + 1)
                    if kind == "s":
                        A(oT[:, a, TP:T], PS[:, 6 + u % 2, 0:DEC], ACT.Copy).then_inc(s_oev, 1)
                    else:
                        rows = unit_shape(UNITS[u])[0]
                        j, o_ = head(a)
                        A(oT[o_:o_ + HD, j, QB * qb:QB * qb + rows], PS[o_:o_ + HD, 6 + u % 2, 0:rows],
                          ACT.Copy).then_inc(s_oev, 1)

            norm_squares(0, xin, SQ0)
            whi_of(0)
            norm_root(0, SD)
            act.wait_ge(s_small, 80)
            A(wfh[:], wfs[:], ACT.Copy).then_inc(s_wfh, 1)
            for j in range(KT):
                act.wait_ge(s_ln, j + 1)
                A(hTh[:, j, :], hT[:, j, :], ACT.Copy).then_inc(s_hhi, 1)
                if j == 0:
                    whi_of(1)

            act.wait_ge(s_const, 1)
            whi_of(2)
            act.wait_ge(s_fz, 1)
            own(A(lf[:, 1, :], lf[:, 1, :], ACT.Exp, scale=-1.0))
            A(lf[:, 1, :], lf[:, 1, :], ACT.Ln, bias=1.0).then_inc(s_fe, 1)
            def channels(r):
                if r == 1:
                    act.wait_ge(s_xm, 1)
                    A(xm[0:HD, 12, :], xm[0:HD, 12, :], ACT.Tanh).then_inc(s_tanh, 1)
                if r == 2:
                    act.wait_ge(s_xm, 2)
                    A(xm[:, 13, :], xm[:, 13, :], ACT.Sigmoid).then_inc(s_tanh, 1)
                    for j in range(NJ):
                        act.wait_ge(s_lora, 2 * j + 1)
                        A(AR[:, 0, j, :], PS[:, 6, 0:TC], ACT.Sigmoid, bias=col("w0", j)).then_inc(s_loev, 1)
                        act.wait_ge(s_lora, 2 * j + 2)
                        A(AA[:, j, :], PS[:, 7, 0:TC], ACT.Sigmoid, bias=col("a0", j)).then_inc(s_loev, 1)
                if 3 <= r < 3 + NJ:
                    j = r - 3
                    act.wait_ge(s_xm, 2 + j + 1)
                    if j == 3:
                        act.wait_ge(s_logf, 2)
                    A(BH[j][:], xm[:, NJ + j, :], ACT.Square, scale=col("k_k", j)).then_inc(s_kksq, 1)
                if r == 4:
                    act.wait_ge(s_ls, 1)
                    A(AR[:, 1, :, :], LS[:], ACT.Exp, scale=CDEC).then_inc(s_d, 1)
                if r == 5:
                    act.wait_ge(s_lprev, 1)
                    A(AR[:, 0, :, :], AR[:, 0, :, :], ACT.Exp, scale=CDEC).then_inc(s_dprev, 1)
                if r == 6:
                    A(LS[:], LS[:], ACT.Exp, scale=-CDEC).then_inc(s_dprev, 1)
                if r == 8:
                    act.wait_ge(s_rn, NJ)
                    for j in range(NJ):
                        A(BH[j][:], BH[j][:], ACT.Sqrt).then_inc(s_kkrt, 1)

            for i in range(I_WO):
                if 2 <= i < I_WO - 1:
                    whi_of(i + 1)
                if i >= I_RW:
                    attention(2 * (i - I_RW))
                evacuate(i)
                if i >= I_RW:
                    attention(2 * (i - I_RW) + 1)
                    channels(i - I_RW)
            for s in range(2 * RW_TILES, NU + 2):
                attention(s)

            def fill(f):
                kind, x = kind_of(f - 1)
                if kind == "M":
                    act.wait_ge(s_fill_dve, taken(f - 1)[1])
                    A(GSQ[:], AR[:, 0, :, P * x:P * x + P], ACT.Square).then_inc(s_gsq, 1)
                if kind == "F":
                    act.wait_ge(s_fn, x + 1)
                    A(MXh[:, x, :], oT[:, x, :], ACT.Copy).then_inc(s_mxh, 1)
                kind, x = kind_of(f - 2)
                if kind == "V":
                    act.wait_ge(s_gy, x + 1)
                    A(MXh[:, NJ:KT, P * x:P * x + P], AR[:, 0, :, P * x:P * x + P], ACT.Copy).then_inc(s_mxh, 1)
                kind, x = kind_of(f)
                if kind and kind in "GVF":
                    act.wait_ge(s_fill, f + 1)
                    b = PS[:, 6 + f % 2, :]
                if kind == "G":
                    A(xm[:, NJ + x, :], b[:, 0:TC], ACT.Copy).then_inc(s_fill_act, 1)
                if kind == "V":
                    A(GSD[:].rearrange("p j t -> p (j t)"), b, ACT.Sqrt, bias=LNX_EPS).then_inc(s_fill_act, 1)
                if kind == "F":
                    A(FSQ[:, x, :], b[:, 0:T], ACT.Sqrt, bias=1e-6).then_inc(s_fill_act, 1)

            act.wait_ge(s_oev, NU)
            act.wait_ge(s_out, 16 * (NQB + 4))
            for gi in range(NG):
                for k, dst in enumerate((vN, bN, kN, AX)):
                    act.wait_ge(s_nat, 4 * gi + k + 1)
                    if k == 0 and gi:
                        act.wait_ge(s_ya, gi)
                    src = PS[:, 6 + k % 2, :].rearrange("p (h c) -> p h c", c=HD)
                    A(dst[:, :, 0:HD], src, ACT.Copy).then_inc(s_natev, 1)
                for hf in range(2):
                    act.wait_ge(s_tn, 2 * gi + hf + 1)
                    A(Tn[:, 4 * hf:4 * hf + 4, :], PS[:, 4 + hf, :].rearrange("p (h c) -> p h c", c=P),
                      ACT.Copy).then_inc(s_tnev, 1)
                    if hf == 0:
                        act.wait_ge(s_akv, gi + 1)
                        A(AX[:, :, HD:P], PS[:, 6, :].rearrange("p (h c) -> p h c", c=HD), ACT.Copy).then_inc(s_akvev, 1)
                if gi == 0:
                    A(FSQ[:], oT[:], ACT.Square).then_inc(s_osq, 1)
                for l in range(1, 6):
                    for hf in range(2):
                        act.wait_ge(s_lx, 10 * gi + 2 * (l - 1) + hf + 1)
                        if l > 1 or gi:
                            act.wait_ge(s_ly, 10 * gi + 2 * (l - 1) + hf - 1)
                        A(Xs[:, 4 * hf:4 * hf + 4, :], PS[:, hf, :].rearrange("p (h c) -> p h c", c=P),
                          ACT.Copy).then_inc(s_xs, 1)
                    fill(5 * gi + l - 1)
                for hf in range(2):
                    act.wait_ge(s_w1, 2 * gi + hf + 1)
                    A(X12[:, 4 * hf:4 * hf + 4, :], PS[:, hf, :].rearrange("p (h c) -> p h c", c=P),
                      ACT.Copy).then_inc(s_w1ev, 1)
                act.wait_ge(s_ya, gi + 1)
                A(AR[:, 0, :, P * gi:P * gi + P], PS[:, 7, :].rearrange("p (j t) -> p j t", j=NJ), ACT.Copy).then_inc(s_yaev, 1)

            fill(len(FILL))
            whi_of(I_WO)
            whi_of(I_WO + 1)
            act.wait_ge(s_gc, 1)
            A(GSQ[:], AR[:, 0, :, P * (NG - 1):TC], ACT.Square).then_inc(s_gsq, 1)
            act.wait_ge(s_fill, len(FILL) + 2)
            A(GSD[:].rearrange("p j t -> p (j t)"), PS[:, 7, :], ACT.Sqrt, bias=LNX_EPS).then_inc(s_fill_act, 1)
            act.wait_ge(s_gy, NG)
            for a, z, w in chunk_tokens(NG - 1):
                ins = A(MXh[:, NJ:KT, z:z + w], AR[:, 0, :, a:a + w], ACT.Copy)
            ins.then_inc(s_mxh, 1)
            for i in range(I_WO + 2, I_WQ):
                whi_of(i)
            norm_squares(1, X1, SQ1)
            whi_of(I_WQ)
            norm_root(1, SD)
            for j in range(KT):
                act.wait_ge(s_ln, KT + j + 1)
                A(H1h[:, j, :], X1[:, j, :], ACT.Copy).then_inc(s_h1h, 1)

            def quarter(c, q, load):
                if q % 2 == 0:
                    act.wait_ge(s_hraw[q // 2 % 4], load)
                if not isinstance(c, int) or c >= 4:
                    act.wait_ge(s_up_mm, c - 3)
                A(hhiq[q % 4][:], hraw[q // 2 % 4][:, 256 * (q % 2):256 * (q % 2) + 256], ACT.Copy).then_inc(s_hhi2, 1)

            for i in range(I_WQ, N_ITEMS):
                if i > I_WQ:
                    whi_of(i)
                    q = i - 1 - I_WQ
                    act.wait_ge(s_item, i)
                    A(QT[:, q, :], PS[:, (i - 1) % 2, 0:T], ACT.Copy).then_inc(s_qev, 1)
            act.wait_ge(s_item, N_ITEMS)
            A(QT[:, 2 * PH - 1, :], PS[:, (N_ITEMS - 1) % 2, 0:T], ACT.Copy).then_inc(s_qev, 1)
            for c in range(4):
                quarter(c, c, 16)
            for k in range(12):
                act.wait_ge(s_scp, k + 1)
                A(scores[:, 512 * k:512 * k + 512], PS[:, 2 + k % 2, :], ACT.Copy).then_inc(s_scev, 1)

            def gelu(e, slot):
                act.wait_ge(s_up_mm, e * 4 + 4)
                A(W[:, bass.ds(e, 1), :].rearrange("p a t -> p (a t)"), PS[:, slot % 4, 0:T], ACT.Gelu).then_inc(s_gelu, 1)

            act.wait_ge(s_out, 16 * (NQB + 6))
            for e in range(RIT):
                for x in range(4 if e else 0):
                    quarter(4 * e + x, 4 * e + x, 16 * (e // 2 + 1))
                if e:
                    gelu(e - 1, e - 1)

            def up_rest(k, first_in_room=False):
                for e in range(RIT):
                    for x in range(4):
                        quarter(k * 16 + (4 * e + x), 4 * e + x, k * 32 + 16 * (e // 2 + 1))
                    if first_in_room and e == 1:
                        act.wait_ge(s_pairs, 6)
                    gelu(k * 4 + (e - 1), e - 1)

            with act.Fori(1, ROUTED) as k:
                up_rest(k)
            act.wait_ge(s_gexp, 1)
            A(best[:], best[:], ACT.Exp).then_inc(s_gate, 1)
            with act.Fori(ROUTED, 3 * PH) as k:
                up_rest(k)
            up_rest(3 * PH, True)
            with act.Fori(3 * PH + 1, NI // RIT) as k:
                up_rest(k)
            gelu(NI - 1, NI - 1)

            def gates(k, q):
                act.wait_ge(s_oh, scaled(k, GIT, q + 1))
                for x in range(4):
                    o_ = oh[q % OH_SLOTS][:, 1, x, :]
                    ins = A(o_, o_, ACT.Copy,
                            scale=pairg[:, bass.ds(scaled(k, 4 * GIT, 4 * q + x), 1)])
                ins.then_inc(s_ohb_act, 1)

            def fetch(k, g_):
                act.wait_ge(s_grid, scaled(k, GIT, g_ + 1))
                if not (isinstance(k, int) and before(g_) < 2):
                    act.wait_ge(s_w_pool, scaled(k, per(g_), before(g_) - 1))
                A(gridv[:, before(g_) % 2, :], PS[:, 2 + g_ % GRID_BANKS, :], ACT.Copy).then_inc(s_gev, 1)

            def grids(k, q):
                if not by_dve(q):
                    gates(k, q)
                if not by_dve(q - 2) and (q >= 2 or not isinstance(k, int)):
                    fetch(k, q - 2)

            for q in range(GIT):
                if q == 2:
                    act.wait_ge(s_h1s, 1)
                grids(0, q)
            with act.Fori(1, NGR // GIT) as k:
                for q in range(GIT):
                    grids(k, q)
            fetch(0, NGR - 2)

            def down(e, s, load):
                if not isinstance(e, int) or e >= 2:
                    act.wait_ge(s_down, e * 2 - 2)
                A(Wh[s][:], W[:, bass.ds(e, 1), :].rearrange("p a t -> p (a t)"), ACT.Copy).then_inc(s_wh, 1)
                for b in range(2):
                    act.wait_ge(s_vraw[2 * s + b], load)
                    if not isinstance(e, int):
                        act.wait_ge(s_down, e * 2 + (b - 3))
                    A(hhv[2 * s + b][:], hraw[2 * s + b][:], ACT.Copy).then_inc(s_vhi, 1)

            weighed(act)
            for e in range(2):
                down(e, e, 16)
            with act.Fori(1, NI // 2) as k:
                for e in range(2):
                    down(k * 2 + e, e, k * 16 + 16)
            norm_squares(2, XF, SQF)
            norm_root(2, SDF)
            for j in range(KT):
                act.wait_ge(s_nr, 2 * KT + j + 1)
                A(XF[:, j, :], XF[:, j, :], ACT.Identity, bias=col("ln2_b", j), scale=col("ln2_g", j)).then_inc(s_yf, 1)

        @block.tensor
        def _(pe):
            mm = nc.tensor.matmul

            def mean_part(n, j, X, c1):
                ins = mm(PS[:, MEAN_BANK, 0:T], c1[:], X[:, NORM_ORDER[n][j], :], start=(j == 0), stop=(j == KT - 1))
                if j == KT - 1:
                    ins.then_inc(s_mean, 1)

            def variance(n, S, c1):
                for j, k in enumerate(NORM_ORDER[n]):
                    pe.wait_ge(s_sq, KT * n + j + 1)
                    ins = mm(PS[:, VAR_BANK, 0:T], c1[:], S[:, k, :], start=(j == 0), stop=(j == KT - 1))
                ins.then_inc(s_var, 1)

            def three(out, whi_, wlo_, xhi, xlo, start, stop):
                mm(out, whi_, xhi, start=start, stop=False)
                mm(out, whi_, xlo, start=False, stop=False)
                return mm(out, wlo_, xhi, start=False, stop=stop)

            pe.wait_ge(s_onesg, 1)
            for j in range(KT):
                pe.wait_ge(s_x[j // (KT // XQ)], 16)
                mean_part(0, j, xin, ones)
            variance(0, SQ0, ones)

            def forget_logits():
                pe.wait_ge(s_wfl, 1)
                pe.wait_ge(s_hlo, KT)
                for k in range(KT):
                    w = slice(H * k, H * k + H)
                    ins = three(PS[0:H, 2, 0:T], wfh[:, w], wfl[:, w], hTh[:, k, :], hTl[:, k, :], k == 0, k == KT - 1)
                ins.then_inc(s_f, 1)

            def split(i):
                pool_did = min(max(i + 1 - POOL_ITEMS.start, 0), len(POOL_ITEMS))
                if i in POOL_ITEMS:
                    pe.wait_ge(s_wlo_pool, pool_did)
                else:
                    pe.wait_ge(s_wlo, i + 1 - pool_did)

            def item(i, xh, xl, ready=None, between=None, ks=range(KT)):
                if ks[0] == 0:
                    split(i)
                w, v = whi[i % HIS], wlo[i % RAWS]
                for k in ks:
                    if ready is not None:
                        pe.wait_ge(ready, k + 1)
                    if k == KT // 2 and between is not None:
                        between()
                    ins = three(PS[:, i % 2, 0:T], w[:, P * k:P * k + P], v[:, P * k:P * k + P], xh[:, k, :], xl[:, k, :],
                                k == 0, k == KT - 1)
                if ks[-1] == KT - 1:
                    ins.then_inc(s_item, 1)

            def scores_of(s):
                kind, a, qb = UNITS[s]
                rows, keys, tiles = unit_shape(UNITS[s])
                solo = s == 0 or "s" in (kind, UNITS[s - 1][0])
                if s:
                    pe.wait_ge(s_exp, s if solo else s - 1) if (solo or s >= 2) else None
                if kind == "p":
                    out = PS[0:rows, 2 + s % 2, :]
                    mm(out[:, 0:keys], qx[:, a, QB * qb:QB * qb + rows], kx[:, a, 0:keys], start=True, stop=False)
                    mm(out[:, QB * qb:keys], ident[0:rows, 0:rows], amask[0:rows, 0:rows], start=False,
                       stop=True).then_inc(s_sc, 1)
                    return
                pe.wait_ge(s_cache, 64)
                for e in range(2):
                    h, o_ = 2 * a + e, HD * e
                    mm(PS[o_:o_ + HD, 2, :], qx[:, h, TP:T], ckx[:, h, :], start=True, stop=True)
                    mm(PS[o_:o_ + HD, 3, 0:DEC], qx[:, h, TP:T], kx[:, h, TP:T], start=True, stop=False)
                    ins = mm(PS[o_:o_ + HD, 3, 0:DEC], ident[0:HD, 0:HD], amask[0:HD, 0:HD], start=False, stop=True)
                ins.then_inc(s_sc, 1)

            def transposes_of(u):
                kind = UNITS[u][0]
                rows, _, tiles = unit_shape(UNITS[u])
                pe.wait_ge(s_norm, u + 1)
                if u:
                    solo = "s" in (kind, UNITS[u - 1][0])
                    if solo or u >= 2:
                        pe.wait_ge(s_tev, u if solo else u - 1)
                b = 4 if kind == "s" else 4 + u % 2
                for i, (k0, w) in enumerate(tiles):
                    ins = nc.tensor.transpose(flat(PS, 512 * b + P * i, rows)[0:w], pr[0:rows, u % 2, k0:k0 + w],
                                              ident[0:rows, 0:rows])
                ins.then_inc(s_tr, 1)

            def values_of(u):
                kind, a, qb = UNITS[u]
                rows, _, tiles = unit_shape(UNITS[u])
                pe.wait_ge(s_tev, u + 1)
                if u >= 2:
                    pe.wait_ge(s_oev, u - 1)
                if u == 4:
                    pe.wait_ge(s_loev, 8)
                if u >= 7 and u % 2 and (u - 7) // 2 < NJ:
                    pe.wait_ge(s_n2m, (u - 7) // 2 + 1)
                for e in range(2 if kind == "s" else 1):
                    h = 2 * a + e if kind == "s" else a
                    o_ = head(h)[1]
                    q0, qn = (HD * e, DEC) if kind == "s" else (0, rows)
                    for i, (k0, w) in enumerate(tiles):
                        v = (vs if kind == "s" else vp)[0:w, i, HD * h:HD * h + HD]
                        ins = mm(PS[o_:o_ + HD, 6 + u % 2, 0:qn], v, pt[0:w, u % 2, P * i + q0:P * i + q0 + qn],
                                 start=(i == 0), stop=(i == len(tiles) - 1))
                ins.then_inc(s_pv, 1)

            def attention(s):
                if s < NU:
                    scores_of(s)
                if 1 <= s <= NU:
                    transposes_of(s - 1)
                if s >= 2:
                    values_of(s - 2)

            V0 = [QB * b for b in range(NQB)]
            assert V0[-1] == T - P
            for i in range(V_ITEMS):
                split(i)
                for kk in range(2):
                    k = 2 * i + kk
                    pe.wait_ge(s_hlo, k + 1)
                    for b, t0 in enumerate(V0):
                        w, v = whi[i % HIS][:, 512 * kk:512 * kk + 512], wlo[i % RAWS][:, 512 * kk:512 * kk + 512]
                        ins = three(PS[:, 4 + b, :], hTh[:, k, t0:t0 + P], hTl[:, k, t0:t0 + P], w, v,
                                    k == 0, k == KT - 1)
                ins.then_inc(s_item, 1)
                if i == 0:
                    forget_logits()

            def channels(r):
                if r == 2:
                    pe.wait_ge(s_tanh, 1)
                    pe.wait_ge(s_oev, 2 * r)
                    for j in range(NJ):
                        if j:
                            pe.wait_ge(s_loev, 2 * j - 1)
                        mm(PS[:, 6, 0:TC], w2s[0:HD, P * j:P * j + P], xm[0:HD, 12, :], start=True,
                           stop=True).then_inc(s_lora, 1)
                        if j:
                            pe.wait_ge(s_loev, 2 * j)
                        mm(PS[:, 7, 0:TC], w2s[HD:P, P * j:P * j + P], xm[HD:P, 12, :], start=True,
                           stop=True).then_inc(s_lora, 1)

            def within(r):
                if 4 <= r < 4 + NJ:
                    j = r - 4
                    pe.wait_ge(s_kksq, j + 1)
                    pe.wait_ge(s_oev, 2 * r - 2)
                    mm(PS[:, 7, 0:TC], blk[:], BH[j][:], start=True, stop=True).then_inc(s_n2, 1)
                attention(2 * r)

            for i in range(I_K, I_WO):
                if i - I_K >= 2:
                    pe.wait_ge(s_pev, i - I_K - 1)
                r = i - I_RW
                if r < 0:
                    item(i, hTh, hTl)
                    continue
                if r == 0:
                    item(i, hTh, hTl)
                    pe.wait_ge(s_negc, 3)
                    pe.wait_ge(s_vev, 4)
                    pe.wait_ge(s_pev, K_ITEMS + Q_ITEMS)
                    attention(0)
                else:
                    item(i, hTh, hTl, between=lambda: within(r))
                attention(2 * r + 1)
                channels(r)
            for s in range(2 * RW_TILES, NU + 2):
                attention(s)

            def fill(f):
                if f >= 2:
                    by_act, n = taken(f - 2)
                    pe.wait_ge(s_fill_act if by_act else s_fill_dve, n)
                kind, x = kind_of(f)
                b = PS[:, 6 + f % 2, :]
                if kind == "G":
                    pe.wait_ge(s_tanh, 2)
                    ins = mm(b[:, 0:TC], g2s[:, P * x:P * x + P], xm[:, 13, :], start=True, stop=True)
                if kind == "B":
                    ins = mm(b, blk[:], xm[:, 0:NJ, :].rearrange("p j t -> p (j t)")[:, 512 * x:512 * x + 512], start=True,
                             stop=True)
                if kind == "M":
                    pe.wait_ge(s_yev, 2 * x + 2)
                    ins = mm(b.rearrange("p (j t) -> p j t", j=NJ), blk[:], AR[:, 0, :, P * x:P * x + P], start=True, stop=True)
                if kind == "V":
                    pe.wait_ge(s_gsq, x + 1)
                    ins = mm(b, blk[:], GSQ[:].rearrange("p j t -> p (j t)"), start=True, stop=True)
                if kind == "F":
                    pe.wait_ge(s_osq, 1)
                    ins = mm(b[:, 0:T], blk[:], FSQ[:, x, :], start=True, stop=True)
                ins.then_inc(s_fill, 1)

            pe.wait_ge(s_oev, NU)
            for gi in range(NG):
                tok = slice(P * gi, P * gi + P)
                for k, src in enumerate(("v", "b", "k", "a")):
                    if k == 0:
                        pe.wait_ge(s_prep, 1)
                        if gi:
                            pe.wait_ge(s_zev, gi)
                    if k >= 2:
                        pe.wait_ge(s_natev, 4 * gi + k - 1)
                    if k == 1 and gi:
                        pe.wait_ge(s_yaev, gi)
                    for j in range(NJ):
                        t = {"v": xm[:, 8 + j, tok], "b": BH[j][:, tok], "k": LS[:, j, tok], "a": AR[:, 0, j, tok]}[src]
                        ins = nc.tensor.transpose(PS[:, 6 + k % 2, P * j:P * j + P], t, ident[:])
                    ins.then_inc(s_nat, 1)
                for hf in range(2):
                    if gi and not hf:
                        pe.wait_ge(s_stt, 2 * gi)
                        pe.wait_ge(s_yev, 2 * gi)
                    for x in range(2):
                        if hf and x:
                            pe.wait_ge(s_Aev, 4 * gi + 1)
                        for hh in range(4):
                            h = 4 * hf + hh
                            j, o_ = head(h)
                            src = LS[o_:o_ + HD, j, tok] if x else BH[j][o_:o_ + HD, tok]
                            out = PS[:, A_BANKS[hf][x] + hh % 2, 256 * (hh // 2):256 * (hh // 2) + 256]
                            ins = mm(out.rearrange("p (x t) -> p x t", x=2), src, AR[o_:o_ + HD, :, j, tok],
                                     start=True, stop=True)
                        ins.then_inc(s_A, 1)
                def transpose_start(hf):
                    pe.wait_ge(s_tt, 2 * gi + hf + 1)
                    for hh in range(4):
                        ins = nc.tensor.transpose(PS[:, 4 + hf, P * hh:P * hh + P], TT[:, 4 * hf + hh, :], ident[:])
                    ins.then_inc(s_tn, 1)

                pe.wait_ge(s_Aev, 4 * gi + 3)
                transpose_start(0)
                pe.wait_ge(s_Aev, 4 * gi + 4)
                pe.wait_ge(s_natev, 4 * gi + 4)
                for h in range(H):
                    ins = mm(PS[:, 6, HD * h:HD * h + HD], AK[:, h, 0:P], vN[:, h, :], start=True, stop=True)
                ins.then_inc(s_akv, 1)
                transpose_start(1)
                for l in range(1, 6):
                    for hf in range(2):
                        n = 10 * gi + 2 * (l - 1) + hf
                        pe.wait_ge(s_nm, n + 1)
                        if l == 1:
                            pe.wait_ge(s_tnev, 2 * gi + hf + 1)
                        else:
                            pe.wait_ge(s_up, n - 1)
                        for hh in range(4):
                            ins = mm(PS[:, hf, P * hh:P * hh + P], Nm[:, hf, hh, :], Tn[:, 4 * hf + hh, :], start=True, stop=True)
                        ins.then_inc(s_lx, 1)
                    for hf in range(2):
                        n = 10 * gi + 2 * (l - 1) + hf
                        pe.wait_ge(s_xs, n + 1)
                        for hh in range(4):
                            h = 4 * hf + hh
                            if l < 5:
                                mm(PS[:, 2 + hf, P * hh:P * hh + P], TT[:, h, :], Xs[:, h, :], start=True, stop=True)
                            ins = mm(PS[:, 4 + hf, P * hh:P * hh + P], Xs[:, h, :], TT[:, h, :], start=True, stop=True)
                        ins.then_inc(s_ly, 1)
                    if l == 1:
                        pe.wait_ge(s_akvev, gi + 1)
                    fill(5 * gi + l - 1)
                for hf in range(2):
                    pe.wait_ge(s_up, 10 * gi + 9 + hf)
                    for hh in range(4):
                        h = 4 * hf + hh
                        ins = mm(PS[:, hf, P * hh:P * hh + P], TT[:, h, :], AX[:, h, :], start=True, stop=True)
                    ins.then_inc(s_w1, 1)
                pe.wait_ge(s_w1ev, 2 * gi + 2)
                for h in range(H):
                    j, o_ = head(h)
                    ins = mm(PS[o_:o_ + HD, 2, P * j:P * j + P], X12[:, h, 0:HD], NR[:, h, P:2 * P], start=True, stop=True)
                ins.then_inc(s_y1, 1)
                for c in range(2):
                    r = slice(CH * c, CH * c + CH)
                    for h in range(H):
                        j, o_ = head(h)
                        ins = mm(PS[o_:o_ + HD, 3 + c, HD * j:HD * j + HD], X12[r, h, 0:HD], bN[r, h, :], start=True, stop=True)
                ins.then_inc(s_y1, 1)
                for f in (5 * gi + 3, 5 * gi + 4):
                    by_act, n = taken(f)
                    pe.wait_ge(s_fill_act if by_act else s_fill_dve, n)
                for c in range(2):
                    r = slice(CH * c, CH * c + CH)
                    for h in range(H):
                        j, o_ = head(h)
                        out = PS[o_:o_ + HD, 5 + c, HD * j:HD * j + HD]
                        mm(out, bN[r, h, :], X12[r, h, HD:P], start=True, stop=False)
                        ins = mm(out, kN[r, h, :], vN[r, h, :], start=False, stop=True)
                ins.then_inc(s_z, 1)
                for h in range(H):
                    j, o_ = head(h)
                    out = PS[o_:o_ + HD, 7, P * j:P * j + P]
                    mm(out, X12[:, h, HD:P], NR[:, h, P:2 * P], start=True, stop=False)
                    ins = mm(out, vN[:, h, :], AK[:, h, P:2 * P], start=False, stop=True)
                ins.then_inc(s_ya, 1)
                pe.wait_ge(s_y1ev, 2 * gi + 2)
                for c in range(2):
                    cc = 2 * gi + c
                    s_in = cc if cc < 5 else 6
                    if c:
                        pe.wait_ge(s_stt, cc)
                    for h in range(H):
                        j, o_ = head(h)
                        ins = mm(PS[o_:o_ + HD, c, HD * j:HD * j + HD], MT[o_:o_ + HD, c, j, :], states[o_:o_ + HD, s_in, j, :],
                                 start=True, stop=True)
                    ins.then_inc(s_ms, 1)
                    for h in range(H):
                        j, o_ = head(h)
                        ins = mm(PS[o_:o_ + HD, 2 + c, CH * j:CH * j + CH], states[o_:o_ + HD, s_in, j, :],
                                 Y1[o_:o_ + HD, j, CH * c:CH * c + CH], start=True, stop=True)
                    ins.then_inc(s_y, 1)

            FOX, RWKV = range(0, NJ), range(NJ, KT)
            pe.wait_ge(s_stt, 2 * NG)
            pe.wait_ge(s_yev, 2 * NG)
            mm(PS[:, 6, :].rearrange("p (j t) -> p j t", j=NJ), blk[:], AR[:, 0, :, P * (NG - 1):TC], start=True,
               stop=True).then_inc(s_fill, 1)
            pe.wait_ge(s_mxl, NJ + NG - 1)
            item(I_WO, MXh, MXl, ks=FOX)
            pe.wait_ge(s_gsq, NG)
            mm(PS[:, 7, :], blk[:], GSQ[:].rearrange("p j t -> p (j t)"), start=True, stop=True).then_inc(s_fill, 1)
            item(I_WO + 1, MXh, MXl, ks=FOX)

            pe.wait_ge(s_mxl, NJ + NG)
            for i in range(I_WO, I_WQ):
                if i - I_WO >= 2:
                    pe.wait_ge(s_wo, i - I_WO - 1)
                    item(i, MXh, MXl)
                else:
                    item(i, MXh, MXl, ks=RWKV)
            pe.wait_ge(s_sum, KT - 1)
            mm(PS[:, MEAN_BANK, 0:T], ones[:], SD[:], start=True, stop=True).then_inc(s_mean, 1)
            variance(1, SQ1, ones)

            for i in range(I_WQ, N_ITEMS):
                if i - I_WQ >= 2:
                    pe.wait_ge(s_qev, i - I_WQ - 1)
                item(i, H1h, H1l, ready=s_h1l if i == I_WQ else None)
            pe.wait_ge(s_qev, 2 * PH)
            for tt, t0 in enumerate((0, P, T - P)):
                for k4 in range(4):
                    k = 4 * tt + k4
                    if k >= 2:
                        pe.wait_ge(s_scev, k - 1)
                    for x in range(4):
                        q = 4 * k4 + x
                        ins = mm(PS[:, 2 + k % 2, P * x:P * x + P], QT[:, q, t0:t0 + P], kst[:, q % 2, :], start=True, stop=True)
                    ins.then_inc(s_scp, 1)

            def up(e, slot):
                for x in range(4):
                    pe.wait_ge(s_hlo2, e * 4 + (x + 1))
                    if x == 0 and not (isinstance(e, int) and e < 4):
                        pe.wait_ge(s_gelu, e - 3)
                    lo_ = hlo[(2 * slot + x // 2) % 4]
                    for kk in range(2):
                        k = 2 * x + kk
                        ins = three(PS[:, slot % 4, 0:T], hhiq[x][:, P * kk:P * kk + P], lo_[:, P * (k % 4):P * (k % 4) + P],
                                    H1h[:, k, :], H1l[:, k, :], k == 0, k == KT - 1)
                    ins.then_inc(s_up_mm, 1)

            pe.wait_ge(s_scev, 12)
            for e in range(RIT):
                up(e, e)
            with pe.Fori(1, ROUTED + 1) as k:
                for e in range(RIT):
                    up(k * 4 + e, e)
            pe.wait_ge(s_routed, 1)
            pe.wait_ge(s_rconst, 1)
            for x, src in enumerate((sel1, sel2, best)):
                if x == 2:
                    pe.wait_ge(s_routed, 2)
                for tt in range(3):
                    ins = nc.tensor.transpose(PS[:, 4 + x, P * tt:P * tt + P],
                                              src[:, PH * tt:PH * tt + PH, :].rearrange("p h k -> p (h k)"), identb[:])
                ins.then_inc(s_pt, 1)
            with pe.Fori(ROUTED + 1, NI // RIT) as k:
                for e in range(RIT):
                    up(k * 4 + e, e)

            def grid(k, q):
                pe.wait_ge(s_ohb_pool if by_dve(q) else s_ohb_act, scaled(k, per(q), before(q) + 1))
                if q >= GRID_BANKS or not isinstance(k, int):
                    pe.wait_ge(s_w_dve if by_dve(q) else s_gev, scaled(k, per(q), before(q - GRID_BANKS) + 1))
                for x in range(4):
                    ins = mm(PS[:, 2 + q % GRID_BANKS, P * x:P * x + P], oh[q % OH_SLOTS][:, 0, x, :],
                             oh[q % OH_SLOTS][:, 1, x, :], start=True, stop=True)
                ins.then_inc(s_grid, 1)

            pe.wait_ge(s_gelu, NI)
            for q in range(GIT):
                grid(0, q)
            with pe.Fori(1, NGR // GIT) as k:
                for q in range(GIT):
                    grid(k, q)

            def down(e, s, start, stop):
                pe.wait_ge(s_wl, e + 1)
                for b in range(2):
                    pe.wait_ge(s_vlo, e * 2 + (b + 1))
                    for kk in range(4):
                        ins = three(PS[:, 4 * b + kk, 0:T], hhv[2 * s + b][:, P * kk:P * kk + P], hlo[2 * s + b][:, P * kk:P * kk + P],
                                    Wh[s][:], Wl[s][:], start, stop)
                    ins.then_inc(s_down, 1)

            weighed(pe)
            for e in range(2):
                down(e, e, e == 0, False)
            with pe.Fori(1, NI // 2 - 1) as k:
                for e in range(2):
                    down(k * 2 + e, e, False, False)
            for e in range(NI - 2, NI):
                down(e, e % 2, False, e == NI - 1)
            pe.wait_ge(s_onesg, 2)
            pe.wait_ge(s_xf, 2)
            for j in range(KT):
                pe.wait_ge(s_xf, j + 1)
                mean_part(2, j, XF, ones2)
            variance(2, SQF, ones2)

        @block.vector
        def _(dve):
            v = nc.vector
            n = [0]

            def own(ins):
                n[0] += 1
                ins.then_inc(s_dve, 1)
                dve.wait_ge(s_dve, n[0])

            def tt(out, a, b, op):
                return v.tensor_tensor(out, a, b, op)

            def norm_center(n, X):
                dve.wait_ge(s_mean, n + 1)
                for k in NORM_ORDER[n]:
                    tt(X[:, k, :], X[:, k, :], PS[:, MEAN_BANK, 0:T], ALU.subtract).then_inc(s_xc, 1)

            def norm_apply(n, X, out, sd, g_, b_, lo=None):
                dve.wait_ge(s_sd, n + 1)
                own(v.reciprocal(sd[:], sd[:]))
                dve.wait_ge(s_xc, KT * n + KT)
                for j in range(KT + 3 if lo else KT + 1):
                    if j < KT:
                        tt(X[:, j, :], X[:, j, :], sd[:], ALU.mult).then_inc(s_nr, 1)
                    if out is not None and 1 <= j <= KT:
                        dve.wait_ge(s_nr, KT * n + j)
                        v.tensor_scalar(out[:, j - 1, :], X[:, j - 1, :], col(g_, j - 1), col(b_, j - 1), ALU.mult,
                                        ALU.add).then_inc(s_ln, 1)
                    if lo and j >= 3:
                        dst, hi, hi_done, done = lo
                        dve.wait_ge(s_ln, KT * n + j - 2)
                        dve.wait_ge(hi_done, j - 2)
                        tt(dst[:, j - 3, :], out[:, j - 3, :], hi[:, j - 3, :].bitcast(F32), ALU.subtract).then_inc(done, 1)

            def wlo_of(i):
                dve.wait_ge(s_whi, i + 1)
                tt(wlo[i % RAWS][:], raw[i % RAWS][:], whi[i % HIS][:].bitcast(F32), ALU.subtract).then_inc(s_wlo, 1)

            dve.wait_ge(s_cols, 16)
            norm_center(0, xin)
            wlo_of(0)
            norm_apply(0, xin, hT, SD, "ln_in_g", "ln_in_b", (hTl, hTh, s_hhi, s_hlo))
            dve.wait_ge(s_wfh, 1)
            tt(wfl[:], wfs[:], wfh[:].bitcast(F32), ALU.subtract).then_inc(s_wfl, 1)
            wlo_of(1)
            dve.wait_ge(s_f, 1)
            own(v.tensor_scalar(lf[:, 0, :], PS[0:H, 2, 0:T], col("b_f", rows=H), None, ALU.add))
            v.scalar_tensor_tensor(lf[:, 1, :], lf[:, 0, :], -1.0, lf[:, 0, :], ALU.mult, ALU.max).then_inc(s_fz, 1)
            wlo_of(2)
            dve.wait_ge(s_fe, 1)
            v.scalar_tensor_tensor(lf[:, 2, :], lf[:, 0, :], 0.0, lf[:, 1, :], ALU.min, ALU.subtract).then_inc(s_logf, 1)

            def maxima(u):
                rows, keys, _ = unit_shape(UNITS[u])
                dve.wait_ge(s_sc, u + 1)
                b = 2 if UNITS[u][0] == "s" else 2 + u % 2
                v.reduce_max(st[0:rows, u % 2, 1:2], flat(PS, 512 * b, keys)[0:rows], AX_X, negate=True).then_inc(s_max, 1)

            def probabilities(u):
                rows, keys, _ = unit_shape(UNITS[u])
                dve.wait_ge(s_exp, u + 1)
                own(v.reciprocal(st[0:rows, u % 2, 3:4], st[0:rows, u % 2, 2:3]))
                v.tensor_scalar(pr[0:rows, u % 2, 0:keys], pr[0:rows, u % 2, 0:keys], st[0:rows, u % 2, 3:4], None,
                                ALU.mult).then_inc(s_norm, 1)

            r_, k_, v_ = (xm[:, NJ * x:NJ * x + NJ, :] for x in range(3))

            def channels(h):
                if h == 6:
                    dve.wait_ge(s_loev, 8)
                    own(v.memset(AR[:, 0, :, TP:PADP], 0.0))
                    for j in range(NJ):
                        ins = v.tensor_tensor_scan(LS[:, j, :], keep[:], AR[:, 0, j, :], 0.0, ALU.mult, ALU.add)
                    ins.then_inc(s_ls, 1)
                if h == 7:
                    dve.wait_ge(s_ls, 1)
                    tt(AR[:, 0, :, :], LS[:], AR[:, 0, :, :], ALU.subtract).then_inc(s_lprev, 1)
                if h in range(7, 15, 2):
                    j = (h - 7) // 2
                    dve.wait_ge(s_n2, j + 1)
                    v.tensor_scalar(BH[j][:], PS[:, 7, 0:TC], float(HD), 1e-24, ALU.mult, ALU.max).then_inc(s_n2m, 1)
                if h in range(8, 16, 2):
                    j = (h - 8) // 2
                    dve.wait_ge(s_n2m, j + 1)
                    v.reciprocal(BH[j][:], BH[j][:]).then_inc(s_rn, 1)
                if h == 16:
                    for j in range(NJ):
                        ins = v.tensor_scalar(v_[:, j, :], AA[:, j, :], 1.0, col("k_a", j), ALU.subtract, ALU.mult)
                    own(ins)
                if h == 17:
                    dve.wait_ge(s_kkrt, NJ)
                    for j in range(NJ):
                        ins = v.scalar_tensor_tensor(BH[j][:], k_[:, j, :], col("k_k", j), BH[j][:], ALU.mult, ALU.mult)
                    own(ins)
                if h == 18:
                    own(v.scalar_tensor_tensor(k_, v_, 1.0, k_, ALU.add, ALU.mult))
                if h == 19:
                    dve.wait_ge(s_dprev, 2)
                    for j in range(NJ):
                        ins = v.scalar_tensor_tensor(AR[:, 0, j, :], BH[j][:], -1.0, AR[:, 0, j, :], ALU.mult, ALU.mult)
                    own(ins)
                if h == 20:
                    dve.wait_ge(s_d, 1)
                    own(v.tensor_copy(DL[:], AR[:, 1, :, CH - 1:TC:CH]))
                    own(tt(AR[:, 1, :, :], AR[:, 1, :, :], r_, ALU.mult))
                if h == 21:
                    for j in range(NJ):
                        ins = tt(BH[j][:], BH[j][:], AA[:, j, :], ALU.mult)
                    own(ins)
                if h == 22:
                    for j in range(NJ):
                        ins = tt(BH[j][:], BH[j][:], LS[:, j, :], ALU.mult)
                    own(ins)
                if h == 23:
                    for j in range(NJ):
                        ins = v.scalar_tensor_tensor(r_[:, j, :], r_[:, j, :], col("r_k", j), k_[:, j, :], ALU.mult, ALU.mult)
                    own(ins)
                if h == 24:
                    tt(LS[:], k_, LS[:], ALU.mult).then_inc(s_prep, 1)

            for i in range(I_WO):
                if 2 <= i < I_RW:
                    wlo_of(i + 1)
                if i == V_ITEMS - 1:
                    dve.wait_ge(s_logf, 1)
                    dve.wait_ge(s_const, 1)
                    dve.wait_ge(s_clf, 16)
                    own(v.tensor_copy(lfs[:, 0, PAST:KEYS], lf[:, 2, TP:T]))
                    v.tensor_tensor_scan(lf[:, 3, 0:TP], ones8[:, 0:TP], lf[:, 2, 0:TP], 0.0, ALU.mult, ALU.add)
                    v.tensor_tensor_scan(lfs[:, 1, :], ones8[:], lfs[:, 0, :], 0.0, ALU.mult, ALU.add).then_inc(s_logf, 1)
                if i >= I_RW:
                    r = i - I_RW
                    t = RW_ORDER[r]
                    maxima(2 * r)
                    probabilities(2 * r)
                    channels(2 * r - 1)
                    maxima(2 * r + 1)
                    dve.wait_ge(s_pev, i - I_K + 1)
                    dve.wait_ge(s_state, r + 1)
                    s = pb[:, r % 3, :]
                    own(tt(xm[:, t, :], s[:, 0:TC], s[:, 1:TC + 1], ALU.subtract))
                    own(v.scalar_tensor_tensor(xm[:, t, :], xm[:, t, :], col("mix", t), s[:, 1:TC + 1], ALU.mult, ALU.add))
                    v.memset(xm[:, t, TP:PADP], 0.0).then_inc(s_xm, 1)
                    probabilities(2 * r + 1)
                    dve.wait_ge(s_xm, r + 1)
                    channels(2 * r)
            dve.wait_ge(s_prep, 1)
            dve.wait_ge(s_pv, NU)
            dve.wait_ge(s_oev, NU)
            dve.wait_ge(s_out, 16 * (NQB + 4))

            def head_norm(x, finish):
                for a, _, w in chunk_tokens(x):
                    t = slice(a, a + w)
                    y = AR[:, 0, :, t]
                    if not finish:
                        ins = v.reciprocal(GSD[:, :, a - P * x:a - P * x + w], GSD[:, :, a - P * x:a - P * x + w])
                        continue
                    own(tt(y, y, GSD[:, :, a - P * x:a - P * x + w], ALU.mult))
                    for j in range(NJ):
                        ins = v.tensor_scalar(AR[:, 0, j, t], AR[:, 0, j, t], col("lnx_g", j), col("lnx_b", j), ALU.mult,
                                              ALU.add)
                    own(ins)
                    own(tt(y, y, AA[:, :, t], ALU.add))
                    ins = tt(y, y, xm[:, NJ:2 * NJ, t], ALU.mult)
                return ins

            def trailing(x):
                for a, z, w in chunk_tokens(x):
                    ins = tt(MXl[:, NJ:KT, z:z + w], AR[:, 0, :, a:a + w], MXh[:, NJ:KT, z:z + w].bitcast(F32), ALU.subtract)
                ins.then_inc(s_mxl, 1)

            def fill(f):
                kind, x = kind_of(f)
                if kind:
                    dve.wait_ge(s_fill, f + 1)
                b = PS[:, 6 + f % 2, :]
                if kind == "B":
                    c = slice(512 * x, 512 * x + 512)
                    v.scalar_tensor_tensor(AA[:].rearrange("p j t -> p (j t)")[:, c], b, float(HD),
                                           v_.rearrange("p j t -> p (j t)")[:, c], ALU.mult, ALU.mult).then_inc(s_fill_dve, 1)
                if kind == "M":
                    y = AR[:, 0, :, P * x:P * x + P]
                    tt(y, y, b.rearrange("p (j t) -> p j t", j=NJ), ALU.subtract).then_inc(s_fill_dve, 1)
                if kind == "V":
                    dve.wait_ge(s_fill_act, taken(f)[1])
                    own(head_norm(x, False))
                if kind == "F":
                    dve.wait_ge(s_fill_act, taken(f)[1])
                    own(v.reciprocal(FSQ[:, x, :], FSQ[:, x, :]))
                    own(tt(oT[:, x, :], oT[:, x, :], FSQ[:, x, :], ALU.mult))
                    v.tensor_scalar(oT[:, x, :], oT[:, x, :], col("fnorm", x), None, ALU.mult).then_inc(s_fn, 1)
                kind, x = kind_of(f - 1)
                if kind == "V":
                    dve.wait_ge(s_fill_dve, taken(FILL.index("B2"))[1])
                    head_norm(x, True).then_inc(s_gy, 1)
                if kind == "F":
                    dve.wait_ge(s_fn, x + 1)
                    dve.wait_ge(s_mxh, hi_count(f - 1))
                    tt(MXl[:, x, :], oT[:, x, :], MXh[:, x, :].bitcast(F32), ALU.subtract).then_inc(s_mxl, 1)
                kind, x = kind_of(f - 2)
                if kind == "V":
                    dve.wait_ge(s_gy, x + 1)
                    dve.wait_ge(s_mxh, hi_count(f - 2))
                    trailing(x)

            for gi in range(NG):
                for hf in range(2):
                    for x, dst in enumerate((NR, AK)):
                        dve.wait_ge(s_A, 4 * gi + 2 * hf + x + 1)
                        if gi and hf == 0 and x == 0:
                            dve.wait_ge(s_ya, gi)
                        for b in range(2):
                            h0 = 4 * hf + b
                            ins = tt(dst[:, h0:h0 + 3:2, :], PS[:, A_BANKS[hf][x] + b, :].rearrange("p (h c) -> p h c", c=2 * P),
                                     over(causal[:], 2), ALU.mult)
                        ins.then_inc(s_Aev, 1)
                    dve.wait_ge(s_Aev, 4 * gi + 2 * hf + 1)
                    hs = slice(4 * hf, 4 * hf + 4)
                    own(tt(TT[:, hs, :], NR[:, hs, 0:P], over(lev[:, 0, :], 4), ALU.mult))
                    tt(TT[:, hs, :], TT[:, hs, :], over(ident[:], 4), ALU.add).then_inc(s_tt, 1)
                for l in range(1, 6):
                    for hf in range(2):
                        hs = slice(4 * hf, 4 * hf + 4)
                        dve.wait_ge(s_ly, 10 * gi + 2 * (l - 1) + hf + 1)
                        if l == 1:
                            dve.wait_ge(s_tt, 2 * gi + hf + 1)
                            dve.wait_ge(s_tnev, 2 * gi + hf + 1)
                        if l < 5:
                            tt(Tn[:, hs, :], Tn[:, hs, :], PS[:, 2 + hf, :].rearrange("p (h c) -> p h c", c=P), ALU.add)
                        tt(TT[:, hs, :], TT[:, hs, :], PS[:, 4 + hf, :].rearrange("p (h c) -> p h c", c=P),
                           ALU.add).then_inc(s_up, 1)
                    if l < 5:
                        dve.wait_ge(s_up, 10 * gi + 2 * l)
                    fill(5 * gi + l - 1)

                dve.wait_ge(s_y1, 2 * gi + 1)
                tt(Y1[:], PS[:, 2, :].rearrange("p (j t) -> p j t", j=NJ), AR[:, 1, :, P * gi:P * gi + P],
                   ALU.add).then_inc(s_y1ev, 1)
                dve.wait_ge(s_y1, 2 * gi + 2)
                for c in range(2):
                    ins = tt(MT[:, c, :, :], PS[:, 3 + c, 0:NJ * HD].rearrange("p (j k) -> p j k", k=HD), over(eye2[:], NJ),
                             ALU.add)
                ins.then_inc(s_y1ev, 1)
                dve.wait_ge(s_z, gi + 1)
                for c in range(2):
                    ins = tt(Zs[:, c, :, :], PS[:, 5 + c, 0:NJ * HD].rearrange("p (j v) -> p j v", j=NJ),
                             along(DL[:, :, 2 * gi + c], HD), ALU.mult)
                ins.then_inc(s_zev, 1)
                dve.wait_ge(s_zev, gi + 1)
                dve.wait_ge(s_yaev, gi + 1)
                for c in range(2):
                    cc = 2 * gi + c
                    s_to = cc + 1 if cc < 5 else 7
                    dve.wait_ge(s_ms, cc + 1)
                    own(tt(states[:, s_to, :, :], PS[:, c, 0:NJ * HD].rearrange("p (j v) -> p j v", j=NJ),
                           along(DL[:, :, cc], HD), ALU.mult))
                    tt(states[:, s_to, :, :], states[:, s_to, :, :], Zs[:, c, :, :], ALU.add).then_inc(s_stt, 1)
                    dve.wait_ge(s_y, cc + 1)
                    y = AR[:, 0, :, CH * cc:CH * cc + CH]
                    tt(y, y, PS[:, 2 + c, 0:NJ * CH].rearrange("p (j t) -> p j t", j=NJ), ALU.add).then_inc(s_yev, 1)

            dve.wait_ge(s_yev, 2 * NG)
            fill(len(FILL))
            dve.wait_ge(s_fill, len(FILL) + 1)
            y = AR[:, 0, :, P * (NG - 1):TC]
            tt(y, y, PS[:, 6, :].rearrange("p (j t) -> p j t", j=NJ), ALU.subtract).then_inc(s_gc, 1)
            dve.wait_ge(s_gc, 1)
            dve.wait_ge(s_fill_act, taken(len(FILL) - 1)[1] + 1)
            own(head_norm(NG - 1, False))
            head_norm(NG - 1, True).then_inc(s_gy, 1)
            dve.wait_ge(s_gy, NG)
            dve.wait_ge(s_mxh, NJ + NG)
            trailing(NG - 1)

            for i in range(I_WO, I_WQ):
                if I_WO + 2 <= i + 1 < I_WQ:
                    wlo_of(i + 1)
                dve.wait_ge(s_item, i + 1)
                v.scalar_tensor_tensor(X1[:, i - I_WO, :], hT[:, i - I_WO, :], ALPHA, PS[:, i % 2, 0:T], ALU.mult,
                                       ALU.add).then_inc(s_wo, 1)
                k = i - I_WO
                if k:
                    dve.wait_ge(s_wo, k + 1)
                    if k > 1:
                        dve.wait_ge(s_sum, k - 1)
                    tt(SD[:], X1[:, 0, :] if k == 1 else SD[:], X1[:, k, :], ALU.add).then_inc(s_sum, 1)
            norm_center(1, X1)
            wlo_of(I_WQ)
            norm_apply(1, X1, X1, SD, "ln1_g", "ln1_b", (H1l, H1h, s_h1h, s_h1l))
            for i in range(I_WQ + 1, N_ITEMS):
                wlo_of(i)

            def route(k, part):
                if part == 0 or part == 1:
                    tk, ix, knock = ((top1, ix1, knock1), (top2, ix2, knock2))[part]
                    s = unit_s[:, part * NK:part * NK + NK]
                    if part == 0:
                        step(v.tensor_copy(unit_s[:], scores[:, bass.ds(k * (2 * NK), 2 * NK)]))
                    step(v.max(tk[:, 0:8], s))
                    step(v.max_index(ix[:, 0:8], tk[:, 0:8], s))
                    step(v.match_replace(knock[:], tk[:, 0:8], s, LOW))
                elif part == 2 or part == 3:
                    tk, ix, knock, ixf = ((top1, ix1, knock1, ix1f), (top2, ix2, knock2, ix2f))[part - 2]
                    step(v.max(tk[:, 8:16], knock[:]))
                    step(v.max_index(ix[:, 8:16], tk[:, 8:16], knock[:]))
                    step(v.tensor_copy(ixf[:], ix[:]))
                elif part == 4:
                    step(tt(cand[:], along(top1[:], 16), over(top2[:], 16), ALU.add))
                    c = cand[:].rearrange("p a b -> p (a b)")
                    step(v.max(top[:, 0:8], c))
                    step(v.max_index(pos[:, 0:8], top[:, 0:8], c))
                elif part == 5:
                    c, ck = (t[:].rearrange("p a b -> p (a b)") for t in (cand, candk))
                    step(v.match_replace(ck, top[:, 0:8], c, LOW))
                    step(v.max(top[:, 8:16], ck))
                    step(v.max_index(pos[:, 8:16], top[:, 8:16], ck))
                    step(v.tensor_copy(bestk(best, k), top[:]))
                elif part == 6:
                    step(v.tensor_scalar(posh[:], pos[:], 4, None, ALU.logical_shift_right))
                    step(v.tensor_scalar(posl[:], pos[:], 15, None, ALU.bitwise_and))
                    step(v.tensor_copy(poshf[:], posh[:]))
                    step(v.tensor_copy(poslf[:], posl[:]))
                    step(tt(hit1[:], iota16[:], along(poshf[:], 16), ALU.is_equal))
                    step(tt(hit2[:], iota16[:], along(poslf[:], 16), ALU.is_equal))
                else:
                    step(tt(hit1[:], hit1[:], over(ix1f[:], 16), ALU.mult))
                    step(tt(hit2[:], hit2[:], over(ix2f[:], 16), ALU.mult))
                    step(v.tensor_reduce(bestk(sel1, k), hit1[:], AX_X, ALU.add))
                    step(v.tensor_reduce(bestk(sel2, k), hit2[:], AX_X, ALU.add))

            def bestk(t, k):
                return t[:].rearrange("p u k -> p (u k)")[:, bass.ds(k * 16, 16)]

            def step(ins):
                dve.drain()

            dve.wait_ge(s_scev, 12)
            dve.wait_ge(s_rconst, 1)
            with dve.Fori(0, 3 * PH) as k:
                for part in range(8):
                    route(k, part)
            v.tensor_copy(gsum[:], best[:, :, 0]).then_inc(s_routed, 1)
            dve.wait_ge(s_routed, 1)
            tt(best[:], best[:], along(gsum[:], 16), ALU.subtract).then_inc(s_gexp, 1)
            dve.wait_ge(s_gate, 1)
            own(v.tensor_reduce(gsum[:], best[:], AX_X, ALU.add))
            own(v.reciprocal(gsum[:], gsum[:]))
            tt(best[:], best[:], along(gsum[:], 16), ALU.mult).then_inc(s_routed, 1)
            for x, dst in enumerate((pair1, pair2, pairg)):
                dve.wait_ge(s_pt, x + 1)
                v.tensor_copy(dst[:, 0:2 * P], PS[:, 4 + x, 0:2 * P]).then_inc(s_pairs, 1)
                v.tensor_copy(dst[:, 2 * P:T], PS[:, 4 + x, 2 * P + 3 * P - T:3 * P]).then_inc(s_pairs, 1)

            def one_hots(k, q):
                if q >= OH_SLOTS or not isinstance(k, int):
                    dve.wait_ge(s_grid, scaled(k, GIT, q - (OH_SLOTS - 1)))
                tok = bass.ds(scaled(k, 4 * GIT, 4 * q), 4)
                tt(oh[q % OH_SLOTS][:], iotak[:].unsqueeze(1).unsqueeze(1).to_broadcast([P, 2, 4, NK]),
                   pair12[:, :, tok].unsqueeze(3).to_broadcast([P, 2, 4, NK]), ALU.is_equal).then_inc(s_oh, 1)

            def weigh(k, g_):
                dve.wait_ge(s_grid, scaled(k, GIT, g_ + 1))
                w = W[:, :, bass.ds(scaled(k, 4 * GIT, 4 * g_), 4)].rearrange("p e t -> p t e")
                tt(w, PS[:, 2 + g_ % GRID_BANKS, :].rearrange("p (t e) -> p t e", e=NI), w, ALU.mult).then_inc(s_w_dve, 1)

            def grids(k, q):
                one_hots(k, q)
                if by_dve(q) and (q >= 3 or not isinstance(k, int)):
                    weigh(k, q - 3)

            dve.wait_ge(s_up_mm, 4 * NI)
            dve.wait_ge(s_pairs, 6)
            dve.wait_ge(s_gelu, NI)
            for q in range(GIT):
                if q == OH_SLOTS - 1:
                    k = slice(KT // 2, KT)
                    tt(H1s[:, k, :], H1h[:, k, :].bitcast(F32), H1l[:, k, :].bitcast(F32), ALU.add).then_inc(s_h1s_dve, 1)
                    dve.wait_ge(s_h1s_dve, 1)
                grids(0, q)
            with dve.Fori(1, NGR // GIT) as k:
                for q in range(GIT):
                    grids(k, q)
            weigh(0, NGR - 1)

            def down(e, s):
                dve.wait_ge(s_wh, e + 1)
                tt(Wl[s][:], W[:, bass.ds(e, 1), :].rearrange("p a t -> p (a t)"), Wh[s][:].bitcast(F32),
                   ALU.subtract).then_inc(s_wl, 1)
                for b in range(2):
                    dve.wait_ge(s_vhi, e * 2 + (b + 1))
                    tt(hlo[2 * s + b][:], hraw[2 * s + b][:], hhv[2 * s + b][:].bitcast(F32), ALU.subtract).then_inc(s_vlo, 1)

            weighed(dve)
            for e in range(2):
                down(e, e)
            with dve.Fori(1, NI // 2) as k:
                for e in range(2):
                    down(k * 2 + e, e)

            dve.wait_ge(s_h1s, 1)
            for j, k in enumerate(NORM_ORDER[2]):
                if j % NJ == 0:
                    dve.wait_ge(s_down, 2 * NI - 1 + j // NJ)
                v.scalar_tensor_tensor(XF[:, k, :], H1s[:, k, :], ALPHA, PS[:, k, 0:T], ALU.mult, ALU.add).then_inc(s_xf, 1)
            dve.wait_ge(s_xf, KT)
            norm_center(2, XF)
            norm_apply(2, XF, None, SDF, "ln2_g", "ln2_b")


def kernel(**inputs):
    from concourse import bacc as _bacc
    from concourse.bass_utils import run_bass_kernel_spmd as _run

    a = {n: np.asarray(x) for n, x in inputs.items()}
    DR = H * HD
    RW = RW_TILES * P

    def tile(w, c):
        return w[:, c:c + P].reshape(KT, P, P).transpose(1, 0, 2).reshape(P, D)

    x = np.concatenate([a["meta_tokens"], a["x_prompt"][0], a["x_sample"][0]])
    w_in, w_out, w_q = a["w_in"][0], a["w_out"][0], a["peer_w_q"][0]
    wv = w_in[:, RW + 2 * DR:RW + 3 * DR]
    items = [wv[2 * P * i:2 * P * i + 2 * P].reshape(2, P, DR).transpose(1, 0, 2).reshape(P, D) for i in range(V_ITEMS)]
    items += [tile(w_in, RW + DR + P * j) for j in range(NJ)]
    items += [tile(w_in, RW + P * j) for j in range(NJ)]
    items += [tile(w_in, P * t) for t in RW_ORDER]
    w_out = np.concatenate([w_out[DR:], w_out[:DR]])
    items += [tile(w_out, P * t) for t in range(KT)]
    items += [tile(w_q, P * t) for t in range(2 * PH)]
    vectors = {"ln_in_g": a["ln_in_g"], "ln_in_b": a["ln_in_b"], "ln1_g": a["ln1_g"], "ln1_b": a["ln1_b"],
               "ln2_g": a["ln2_g"], "ln2_b": a["ln2_b"], "mix": a["rwkv_mix"], "w0": a["rwkv_w0"], "a0": a["rwkv_a0"],
               "k_k": a["rwkv_k_k"], "k_a": a["rwkv_k_a"], "r_k": a["rwkv_r_k"], "lnx_g": a["rwkv_lnx_g"],
               "lnx_b": a["rwkv_lnx_b"], "fnorm": a["fox_norm_g"], "shift": a["state_rwkv_shift"],
               "b_f": np.pad(a["fox_b_f"].reshape(-1), (0, P - H))}
    cols = np.concatenate([vectors[n].reshape(-1, P).T for n in COLS], axis=1)
    ins = {
        "xT": x.reshape(T, KT, P).transpose(2, 1, 0),
        "cols": cols,
        "wbig": np.stack(items),
        "wf": w_in[:, RW + 3 * DR:].reshape(KT, P, H).transpose(1, 0, 2).reshape(P, KT * H),
        "w2a2": np.concatenate([a["rwkv_w2"][0], a["rwkv_a2"][0]]),
        "g2": a["rwkv_g2"][0],
        "keysT": np.stack([a["peer_keys1"][0].T, a["peer_keys2"][0].T], axis=1),
        "ckT": a["cache_fox_k"][0, 0].transpose(2, 1, 0),
        "cv": a["cache_fox_v"][0, 0].reshape(PAST, DR),
        "clf": a["cache_fox_logf"][0, 0].T,
        "s0T": a["state_rwkv_wkv"][0, 0].reshape(NJ, 2, HD, HD).transpose(1, 3, 0, 2).reshape(P, NJ, HD),
        "uT": a["peer_u"][0].reshape(NK, NK, 2, 4, P).transpose(1, 2, 4, 3, 0).reshape(2 * NK, P, 512),
        "vE": a["peer_v"][0].reshape(NK, NK, 2, 512).transpose(1, 2, 0, 3).reshape(2 * NK, P, 512),
    }
    outs = {"yT": (P, KT, T), "wkvo": (P, 2, NJ, HD), "ko": (HD, H, T), "vpo": (TP, DR), "vso": (DEC, DR),
            "lfo": (H, T), "sho": (P, RW_TILES, 2)}
    nc = _bacc.Bacc("TRN2", target_bir_lowering=False, num_devices=1)
    arrays, args = {}, []
    for name, arr in ins.items():
        arrays[f"in_{name}"] = np.ascontiguousarray(arr)
        args.append(nc.dram_tensor(f"in_{name}", arr.shape, mybir.dt.from_np(arr.dtype), kind="ExternalInput").ap())
    for name, shape in outs.items():
        args.append(nc.dram_tensor(f"out_{name}", shape, F32, kind="ExternalOutput").ap())
    build(nc, *args)
    r = _run(nc, [arrays], core_ids=[0]).results[0]
    o = {n: np.asarray(r[f"out_{n}"]) for n in outs}

    y = o["yT"].transpose(2, 1, 0).reshape(T, D)
    sh = o["sho"].transpose(2, 1, 0).reshape(2, RW)
    wkv = o["wkvo"].reshape(2, HD, 2, NJ, HD).transpose(2, 3, 0, 4, 1).reshape(2, H, HD, HD)
    k = o["ko"].transpose(2, 1, 0)
    lf = o["lfo"].T
    one = (1, 1)
    return (y[N_META:TP].reshape(1, SEQ, D), y[TP:].reshape(1, DEC, D),
            sh[0].reshape(*one, 1, RW), wkv[0].reshape(*one, H, HD, HD), k[:TP].reshape(*one, TP, H, HD),
            o["vpo"].reshape(*one, TP, H, HD), lf[:TP].reshape(*one, TP, H),
            sh[1].reshape(*one, 1, RW), wkv[1].reshape(*one, H, HD, HD), k[TP:].reshape(*one, DEC, H, HD),
            o["vso"].reshape(*one, DEC, H, HD), lf[TP:].reshape(*one, DEC, H))
```
